# Optimizing a Trainium2 kernel written in Bass

```python
import math
import jax, jax.numpy as jnp
from jax import lax
import numpy as np

D_MODEL = 1024
BATCH = 1
SEQ = 2048
DEPTH = 1

CHUNK = 64
D_MIX = D_MODEL
C_CONV = 512
CONV_WIDTH = 31
HEAD_DIM = 64
N_Q_HEADS = 8
N_KV_HEADS = 2
GQ = N_Q_HEADS // N_KV_HEADS
WINDOW = 128
WINDOW_CHUNKS = WINDOW // CHUNK
D_IN_TOTAL = 2 * C_CONV + N_Q_HEADS * HEAD_DIM + 2 * N_KV_HEADS * HEAD_DIM
N_GROUPS = 4
EXPERTS_PER_GROUP = 8
N_EXPERTS = N_GROUPS * EXPERTS_PER_GROUP
TOP_K = 2
D_EXPERT = 512
ROW_BLOCK = 256
LN_EPS = 1e-5
ALPHA = (2.0 * DEPTH) ** 0.25
BETA = (8.0 * DEPTH) ** -0.25

kernel_name = "hymba_conformer_swa_sink_hiermoe_deepnorm"

def layer_norm(x, g, b):
    xf = x.astype(jnp.float32)
    mu = jnp.mean(xf, axis=-1, keepdims=True)
    var = jnp.mean(jnp.square(xf - mu), axis=-1, keepdims=True)
    y = (xf - mu) * lax.rsqrt(var + LN_EPS) * g.astype(jnp.float32) + b.astype(jnp.float32)
    return y.astype(x.dtype)

def conformer_conv(a, gate, w_dw, ln_g, ln_b):
    u = a * jax.nn.sigmoid(gate)
    u = lax.conv_general_dilated(
        u, w_dw[:, None, :].astype(u.dtype),
        window_strides=(1,), padding=[(CONV_WIDTH - 1, 0)],
        dimension_numbers=("NWC", "WIO", "NWC"),
        feature_group_count=C_CONV)
    u = layer_norm(u, ln_g, ln_b)
    return jax.nn.silu(u)

def _shift_chunks(t, j):
    if j == 0:
        return t
    nc = t.shape[1]
    pad = [(0, 0)] * t.ndim
    pad[1] = (j, 0)
    return jnp.pad(t, pad)[:, :nc]

def swa_gqa_sinks(q, k, v, sinks):
    B, S, _ = q.shape
    nc = S // CHUNK
    qc = q.reshape(B, nc, CHUNK, N_KV_HEADS, GQ, HEAD_DIM)
    kc = k.reshape(B, nc, CHUNK, N_KV_HEADS, HEAD_DIM)
    vc = v.reshape(B, nc, CHUNK, N_KV_HEADS, HEAD_DIM)
    shifts = list(range(WINDOW_CHUNKS - 1, -1, -1))
    kb = jnp.concatenate([_shift_chunks(kc, j) for j in shifts], axis=2)
    vb = jnp.concatenate([_shift_chunks(vc, j) for j in shifts], axis=2)
    key_offset = jnp.repeat(jnp.arange(WINDOW_CHUNKS - 1, -1, -1), CHUNK)
    valid = jnp.arange(nc)[:, None] >= key_offset[None, :]
    scale = 1.0 / math.sqrt(HEAD_DIM)
    s = jnp.einsum("bnqhgd,bnkhd->bnhgqk", qc, kb).astype(jnp.float32) * scale
    s = jnp.where(valid[None, :, None, None, None, :], s, jnp.finfo(jnp.float32).min)
    sink = sinks.astype(jnp.float32).reshape(N_KV_HEADS, GQ)[None, None, :, :, None, None]
    m = jnp.maximum(jnp.max(s, axis=-1, keepdims=True), sink)
    p = jnp.exp(s - m)
    denom = jnp.sum(p, axis=-1, keepdims=True) + jnp.exp(sink - m)
    p = (p / denom).astype(v.dtype)
    o = jnp.einsum("bnhgqk,bnkhd->bnqhgd", p, vb)
    return o.reshape(B, S, N_Q_HEADS * HEAD_DIM)

def hier_moe(x, w_rg, b_rg, w_re, b_re, w1, w3, w2):
    B, S, D = x.shape
    T = B * S
    xt = x.reshape(T, D)
    g_logits = (xt @ w_rg + b_rg).astype(jnp.float32)
    g_prob = jax.nn.softmax(g_logits, axis=-1)
    g_sel = jnp.argmax(g_logits, axis=-1).astype(jnp.int32)
    p_g = jnp.take_along_axis(g_prob, g_sel[:, None], axis=1)
    e_logits = (xt @ w_re + b_re).astype(jnp.float32).reshape(T, N_GROUPS, EXPERTS_PER_GROUP)
    e_sel = jnp.take_along_axis(e_logits, g_sel[:, None, None], axis=1)[:, 0]
    e_prob = jax.nn.softmax(e_sel, axis=-1)
    top_w, top_i = lax.top_k(e_prob, TOP_K)
    top_w = top_w / jnp.sum(top_w, axis=-1, keepdims=True)
    gates = (p_g * top_w).astype(x.dtype)
    expert_idx = (g_sel[:, None] * EXPERTS_PER_GROUP + top_i).astype(jnp.int32)

    n_slots = T * TOP_K
    n_buf = -(-n_slots // ROW_BLOCK) * ROW_BLOCK + N_EXPERTS * ROW_BLOCK
    n_blocks = n_buf // ROW_BLOCK
    flat_e = expert_idx.reshape(-1)
    order = jnp.argsort(flat_e)
    sorted_e = flat_e[order]
    counts = jnp.zeros((N_EXPERTS,), jnp.int32).at[flat_e].add(1)
    padded = ((counts + ROW_BLOCK - 1) // ROW_BLOCK) * ROW_BLOCK
    padded_end = jnp.cumsum(padded)
    pad_start = padded_end - padded
    start = jnp.cumsum(counts) - counts
    rank = jnp.arange(n_slots, dtype=jnp.int32) - start[sorted_e]
    dest = pad_start[sorted_e] + rank
    slot_token = jnp.full((n_buf,), T, jnp.int32).at[dest].set((order // TOP_K).astype(jnp.int32))
    slot_gate = jnp.zeros((n_buf,), x.dtype).at[dest].set(gates.reshape(-1)[order])
    block_start = jnp.arange(n_blocks, dtype=jnp.int32) * ROW_BLOCK
    block_expert = jnp.minimum(jnp.searchsorted(padded_end, block_start, side="right"),
                               N_EXPERTS - 1).astype(jnp.int32)
    x_pad = jnp.concatenate([xt, jnp.zeros((1, D), xt.dtype)], axis=0)

    def expert_block(args):
        tok, e = args
        xb = x_pad[tok]
        h = jax.nn.silu(xb @ w1[e]) * (xb @ w3[e])
        return h @ w2[e]

    y_slots = lax.map(expert_block, (slot_token.reshape(n_blocks, ROW_BLOCK), block_expert))
    y_slots = y_slots.reshape(n_buf, D) * slot_gate[:, None]
    y = jax.ops.segment_sum(y_slots, slot_token, num_segments=T + 1)[:T]
    return y.reshape(B, S, D)

def setup_inputs(seed: int = 0) -> dict:
    key = jax.random.key(seed)
    ks = jax.random.split(key, 24)
    f32 = jnp.float32
    n = lambda k, shape, s: jax.random.normal(k, shape, f32) * s
    L = DEPTH
    return {
        "x": jax.random.normal(ks[0], (BATCH, SEQ, D_MODEL), f32),
        "ln_in_g": 1.0 + n(ks[1], (D_MODEL,), 0.02),
        "ln_in_b": n(ks[2], (D_MODEL,), 0.02),
        "w_in": n(ks[3], (L, D_MODEL, D_IN_TOTAL), D_MODEL ** -0.5),
        "b_in": n(ks[4], (L, D_IN_TOTAL), 0.02),
        "w_dw": n(ks[5], (L, CONV_WIDTH, C_CONV), CONV_WIDTH ** -0.5),
        "ln_conv_g": 1.0 + n(ks[6], (L, C_CONV), 0.02),
        "ln_conv_b": n(ks[7], (L, C_CONV), 0.02),
        "sinks": n(ks[8], (L, N_Q_HEADS), 0.5),
        "w_out": n(ks[9], (L, D_MIX, D_MODEL), BETA * D_MIX ** -0.5),
        "b_out": n(ks[10], (L, D_MODEL), 0.02),
        "ln_mix_g": 1.0 + n(ks[11], (L, D_MODEL), 0.02),
        "ln_mix_b": n(ks[12], (L, D_MODEL), 0.02),
        "w_router_group": n(ks[13], (L, D_MODEL, N_GROUPS), D_MODEL ** -0.5),
        "b_router_group": n(ks[14], (L, N_GROUPS), 0.01),
        "w_router_expert": n(ks[15], (L, D_MODEL, N_EXPERTS), D_MODEL ** -0.5),
        "b_router_expert": n(ks[16], (L, N_EXPERTS), 0.01),
        "w1": n(ks[17], (L, N_EXPERTS, D_MODEL, D_EXPERT), D_MODEL ** -0.5),
        "w3": n(ks[18], (L, N_EXPERTS, D_MODEL, D_EXPERT), D_MODEL ** -0.5),
        "w2": n(ks[19], (L, N_EXPERTS, D_EXPERT, D_MODEL), BETA * D_EXPERT ** -0.5),
        "ln_ffn_g": 1.0 + n(ks[20], (L, D_MODEL), 0.02),
        "ln_ffn_b": n(ks[21], (L, D_MODEL), 0.02),
    }

def reference(x, ln_in_g, ln_in_b, w_in, b_in, w_dw, ln_conv_g, ln_conv_b, sinks,
              w_out, b_out, ln_mix_g, ln_mix_b, w_router_group, b_router_group,
              w_router_expert, b_router_expert, w1, w3, w2, ln_ffn_g, ln_ffn_b):
    B, S, D = x.shape
    x = layer_norm(x, ln_in_g, ln_in_b)
    c1 = C_CONV
    c2 = 2 * C_CONV
    c3 = c2 + N_Q_HEADS * HEAD_DIM
    c4 = c3 + N_KV_HEADS * HEAD_DIM
    for l in range(DEPTH):
        proj = x @ w_in[l] + b_in[l]
        a, gt = proj[..., :c1], proj[..., c1:c2]
        q, k, v = proj[..., c2:c3], proj[..., c3:c4], proj[..., c4:]
        conv_out = conformer_conv(a, gt, w_dw[l], ln_conv_g[l], ln_conv_b[l])
        attn_out = swa_gqa_sinks(q, k, v, sinks[l])
        mix = jnp.concatenate([conv_out, attn_out], axis=-1) @ w_out[l] + b_out[l]
        x = layer_norm(ALPHA * x + mix, ln_mix_g[l], ln_mix_b[l])
        ffn = hier_moe(x, w_router_group[l], b_router_group[l], w_router_expert[l],
                       b_router_expert[l], w1[l], w3[l], w2[l])
        x = layer_norm(ALPHA * x + ffn, ln_ffn_g[l], ln_ffn_b[l])
    return x


_drawn_inputs = setup_inputs


def setup_inputs(seed=0):
    import zlib

    import numpy as np

    out = dict(_drawn_inputs(seed))
    spreads = {}
    factors = {'b_in': 3.848,
     'ln_conv_g': 6.377,
     'ln_conv_b': 6.536,
     'sinks': 175.804,
     'b_out': 2.782,
     'b_router_group': 6.364,
     'b_router_expert': 7.106,
     'ln_ffn_g': 25.46,
     'ln_ffn_b': 23.863}
    for name, (base, spread) in spreads.items():
        noise = np.random.default_rng([zlib.crc32(name.encode()), seed]).standard_normal(out[name].shape)
        drawn = base * np.exp(spread * noise) if base else spread * noise
        out[name] = __import__('jax').numpy.asarray(drawn.astype(out[name].dtype))
    for name, factor in factors.items():
        out[name] = (out[name] * factor).astype(out[name].dtype)
    return out
```

```python
from contextlib import ExitStack

import concourse.bass as bass
from concourse import mybir

F32 = mybir.dt.float32
I32 = mybir.dt.int32
U32 = mybir.dt.uint32
ALU = mybir.AluOpType
ACT = mybir.ActivationFunctionType
AXX = mybir.AxisListType.X

P = 128
D = 1024
SEQ = 2048
KD = D // P
T = 512
NCH = SEQ // T
TT = T // P
NT = SEQ // P
CONV = 512
CT = CONV // P
CW = 31
HALO = CW - 1
HD = 64
NQ = 8
NKV = 2
GQ = NQ // NKV
AC = 64
AS = T // AC
DIN = 2 * CONV + NQ * HD + 2 * NKV * HD
Q0 = 2 * CONV
K0 = Q0 + NQ * HD
V0 = K0 + NKV * HD
NG = 4
EG = 8
NE = NG * EG
NR = NG + NE
DE = 512
KE = DE // P
EPS = 1e-5
ALPHA = 2.0 ** 0.25
SCALE = 1.0 / 8.0
NEG = -3.0e38
NS = 2 * SEQ
MAXB = NS // P + NE


def build(nc, x, ln_in_g, ln_in_b, w_in, b_in, w_dw, ln_conv_g, ln_conv_b, sinks, w_out, b_out,
          ln_mix_g, ln_mix_b, w_rg, b_rg, w_re, b_re, w1, w3, w2, ln_ffn_g, ln_ffn_b, out):
    ctx = ExitStack()
    with ctx:
        def sb(name, shape, dt=F32):
            return ctx.enter_context(nc.sbuf_tensor(name, shape, dt))

        def sem(name):
            return ctx.enter_context(nc.semaphore(name))

        x_d = x.rearrange("a (t p) d -> (a t) p d", p=P)
        out_d = out.rearrange("a (t p) d -> (a t) p d", p=P)
        res_d = nc.dram_tensor("res_d", (NT, P, D), F32).ap()
        x2_d = nc.dram_tensor("x2_d", (SEQ, D), F32).ap()
        x2_t = x2_d.rearrange("(t p) d -> t p d", p=P)
        slot_d = nc.dram_tensor("slot_d", (NS + P, 1), I32).ap()
        ys_d = nc.dram_tensor("ys_d", (NS + P, D), F32).ap()

        WN = KD * DE * 2 + KE * D
        arena = sb("arena", [P, 2 * WN])
        win = arena[:, 0:KD * DIN].rearrange("p (k n) -> p k n", k=KD)
        wout = arena[:, KD * DIN:KD * DIN + KD * D].rearrange("p (k n) -> p k n", k=KD)
        rt_at = KD * DIN + KD * D
        rt = arena[:, rt_at:rt_at + 2 * D].rearrange("p (s n) -> p s n", s=2)
        we = []
        for s in range(2):
            o = s * WN
            we.append((arena[:, o:o + KD * DE].rearrange("p (k n) -> p k n", k=KD),
                       arena[:, o + KD * DE:o + 2 * KD * DE].rearrange("p (k n) -> p k n", k=KD),
                       arena[:, o + 2 * KD * DE:o + WN].rearrange("p (k n) -> p k n", k=KE)))
        xt = sb("xt", [P, 2, D])
        xb = sb("xb", [P, D])
        xT = sb("xT", [P, KD, T])
        u = sb("u", [P, CT, HALO + T])
        acc = sb("acc", [P, CT, T])
        sg = sb("sg", [P, 2, T])
        mixc = sb("mixc", [P, CT, T])
        mixa = sb("mixa", [P, GQ, T])
        qT = sb("qT", [P, AS, GQ * AC])
        kT = sb("kT", [P, NKV, AC + T])
        vO = sb("vO", [P, TT, P])
        vE = sb("vE", [P, TT + 1, P])
        pr = sb("pr", [P, GQ, P])
        pT = sb("pT", [P, GQ, P])
        crs = sb("crs", [P, T])
        x2T = sg[:, :, :].rearrange("p a (b n) -> p (a b) n", n=P)
        ag_b = sb("ag_b", [P, D])
        ab_b = sb("ab_b", [P, D])
        gm_b = sb("gm_b", [P, D])
        bm_b = sb("bm_b", [P, D])
        bv_b = sb("bv_b", [P, P])
        ident = sb("ident", [P, P])
        ones = sb("ones", [P, P])
        cmean = sb("cmean", [P, P])
        tri = sb("tri", [P, P])
        wr = sb("wr", [P, KD, NR])
        logits = sb("logits", [P, NT, NR])
        br_b = sb("br_b", [P, NR])
        mhalf = sb("mhalf", [P, 1])
        NV = 2 * KD + 2 * CT + 1 + 2 * CT + GQ
        vrow, wrow = pr[0:NV, 0, :], crs[0:CW, :]
        cols = sb("cols", [P, NV + CT * CW])
        lg_in, lb_in, b_ag, b_k, lcg, lcb, b_q = [
            cols[:, sum(w[:i]):sum(w[:i]) + w[i]] for w in ((KD, KD, 2 * CT, 1, CT, CT, GQ),) for i in range(7)]
        wdw = cols[:, NV:NV + CT * CW].rearrange("p (t w) -> p t w", t=CT)
        sink_b = sb("sink_b", [P, GQ])
        bst = sb("bst", [P, 2, 2, 6])
        mv = sb("mv", [P, 2, 2])
        ve = sb("ve", [P, 2])
        rs = sb("rs", [P, 2])
        cve = sb("cve", [P, TT])
        cpw = sb("cpw", [P, TT])
        mx = sb("mx", [P, GQ])
        mm_ = sb("mm_", [P, GQ])
        negm = sb("negm", [P, GQ])
        sk = sb("sk", [P, GQ])
        es = sb("es", [P, GQ])
        psum_ = sb("psum_", [P, GQ])
        den = sb("den", [P, GQ])
        rden = sb("rden", [P, GQ])
        rev = sb("rev", [P, EG])
        thr = sb("thr", [P, NT - 1])
        gate = sb("gate", [P, 2, NT])
        pos_u = sb("pos_u", [P, 2, NT], I32)
        tok_u = sb("tok_u", [P, NT], I32)
        blk_i = sb("blk_i", [1, 3 * NE + 1], I32)
        idx = sb("idx", [P, 1], I32)
        idy = sb("idy", [P, 2, 2], I32)

        xflat = xT[:, :, :].rearrange("p k n -> p (k n)")
        xg = xflat[:, 0:D]
        xe = xflat[:, D:2 * D].rearrange("p (k n) -> p k n", k=KD)
        he = xflat[:, 2 * D:2 * D + DE].rearrange("p (f n) -> p f n", f=KE)
        sl = xflat[:, 2 * D + DE:3 * D].rearrange("p (h n) -> p h n", h=2)
        ye = xflat[:, 3 * D:4 * D]

        def two(t):
            return t[:, :, :].rearrange("p a n -> p (a n)")[:, 0:2 * D].rearrange("p (s n) -> p s n", s=2)
        ya, yb, x2r, lnf = two(acc), two(mixc), two(mixa), two(qT)

        uf = u[:, :, :].rearrange("p a n -> p (a n)")
        af = acc[:, :, :].rearrange("p a n -> p (a n)")
        mf = mixa[:, :, :].rearrange("p a n -> p (a n)")
        qf = qT[:, :, :].rearrange("p a n -> p (a n)")

        def flat4(t):
            return t.rearrange("p t g e -> p (t g e)")

        def carve(t, sizes):
            o, got = 0, []
            for shape in sizes:
                n = 1
                for m in shape:
                    n *= m
                v = t[:, o:o + n]
                if len(shape) == 2:
                    v = v.rearrange("p (a b) -> p a b", b=shape[1])
                elif len(shape) == 3:
                    v = v.rearrange("p (a b c) -> p a b c", b=shape[1], c=shape[2])
                got.append(v)
                o += n
            return got

        r_G = logits[:, :, 0:NG]
        r_E = logits[:, :, NG:NR].rearrange("p t (g e) -> p t g e", g=NG)
        (r_gmax, r_gd, r_gk, r_hg, r_eg, r_es, r_k8, r_kmax, r_h1, r_h2, r_e2, r_m1, r_m2, r_ed, r_ee,
         r_sum, r_one, r_nb, r_zero, r_end, r_beg, r_pos) = carve(uf, [
            [NT], [NT, NG], [NT, NG], [NT, NG], [NT, NG], [NT, EG], [NT, EG], [NT], [NT, EG], [NT, EG], [NT, EG],
            [NT], [NT], [NT], [NT], [NT], [NT], [NE], [NE], [NE], [NE], [NT]])
        r_sel, r_hot1, r_hot2 = carve(af, [[NT, NG, EG]] * 3)
        r_pre, r_rank, r_tmp = carve(mf, [[NT + 1, NE], [NT, NE], [NT, NE]])
        (r_cmp,) = carve(qf, [[NE, NT - 1]])
        RT_EXP_G, RT_EXP_E = 3, 21

        bank = [ctx.enter_context(nc.psum_tensor(f"bank{i}", [P, 512], F32)) for i in range(8)]
        TP, PR, SB, OB = bank[0:2], bank[2:6], bank[6], bank[7]

        S = {n: sem(n) for n in (
            "passed", "c_ident", "c_tri", "c_ones", "c_bc", "c_fold", "c_halo", "c_vhalo", "cols_tr", "cols_in", "ld_small", "ld_win", "ld_wout", "ld_slot0",
            "ln1_st", "ln1_var", "ln1_rs", "ln1_done", "xb_st", "xb_ready", "xb_out",
            "xtr_done", "xT_ready", "gate_done", "a_done", "sg_ready", "u_ready", "conv_st", "sm0",
            "halo_u", "mean_done", "uc_ready", "sq_ready", "var_done", "cv_sum", "cv_ready", "cpw_ready", "dg_ready", "bc_done", "crs_ready", "un_ready",
            "mixc_ready", "q_done", "qk_ready", "v_done", "v_ready", "s_done", "sm_st", "sm_neg",
            "p_ready", "es_ready", "pn_ready", "ptr_done", "pT_ready", "pv_done", "o_ready", "halo_kv",
            "o_done", "o_evac", "ln2_st", "ln2_var", "ln2_rs", "ln2_done", "x2tr_done", "x2T_ready",
            "lg_done", "lg_ready",
            "rt_st", "rk_exp", "r_hot", "rk_done", "r_idx", "r_blk", "slot_out",
            "e_idx", "e_xg", "etr_done", "exa_ready", "exb_ready", "up_done", "sl_ready", "h_ready",
            "dn_done", "ya_free", "yb_free", "ys_out",
            "y_idx", "f_st", "f_a", "f_var", "f_rs", "f_done", "ld_lnf")}
        x_in = [sem(f"x_in{i}") for i in range(2)]
        r_in = [sem(f"r_in{i}") for i in range(2)]
        x2_out = [sem(f"x2_out{i}") for i in range(2)]
        w13_in = [sem(f"w13_in{i}") for i in range(2)]
        w2_in = [sem(f"w2_in{i}") for i in range(2)]
        y_in = [sem(f"y_in{i}") for i in range(2)]
        x2r_in = [sem(f"x2r_in{i}") for i in range(2)]
        f_out = [sem(f"f_out{i}") for i in range(2)]

        def at(t, i):
            return t[i] if isinstance(i, int) else t[bass.ds(i, 1)].squeeze(0)

        def wait_apart(eng, semaphore, value):
            eng.wait_ge(semaphore, value)
            eng.sem_inc(S["passed"], 1)

        def expert(eng, e):
            return (eng.value_load(blk_i[0:1, bass.ds(e, 1)], min_val=1, max_val=NT),
                    eng.value_load(blk_i[0:1, bass.ds(e + NE, 1)], min_val=0, max_val=MAXB - 1),
                    eng.value_load(blk_i[0:1, bass.ds(e + 2 * NE, 1)], min_val=0, max_val=NS))

        def block_slot(s0, b):
            return nc.s_assert_within(s0 + b * P, 0, NS, skip_runtime_bounds_check_because=
                                      "a block starts at or before its expert's last slot, or at its empty first")

        def row(v):
            return v.rearrange("(a n) -> a n", a=1).broadcast_to([P, v.shape[0]])

        SMALL = []

        w_in0, b_in0, w_dw0 = w_in[0], b_in[0], w_dw[0]
        SMALL += [
            (ag_b[:, :], row(ln_in_g)), (ab_b[:, :], row(ln_in_b)), (xb[:, :], row(b_out[0])),
            (gm_b[:, :], row(ln_mix_g[0])), (bm_b[:, :], row(ln_mix_b[0])),
            (bv_b[:, :], row(b_in0[V0:DIN])), (br_b[:, 0:NG], row(b_rg[0])), (br_b[:, NG:NR], row(b_re[0])),
            (wr[:, :, 0:NG], w_rg[0].rearrange("(k p) n -> p k n", p=P)),
            (wr[:, :, NG:NR], w_re[0].rearrange("(k p) n -> p k n", p=P)),
        ]
        at_row = 0
        for vec in (ln_in_g, ln_in_b, b_in0[0:2 * CONV], b_in0[K0:V0], ln_conv_g[0], ln_conv_b[0]):
            n = vec.shape[0] // P
            SMALL.append((vrow[at_row:at_row + n, :], vec.rearrange("(k p) -> k p", p=P)))
            at_row += n
        SMALL.append((vrow[at_row:at_row + GQ, :].rearrange("g (a d) -> g a d", a=NKV),
                      b_in0[Q0:K0].rearrange("(a g d) -> g a d", a=NKV, g=GQ)))
        SMALL.append((wrow, w_dw0))
        for g in range(2):
            SMALL.append((sink_b[g * AC:(g + 1) * AC, :],
                          sinks[0].rearrange("(a c g) -> a g c", a=1, g=2)[:, g, :].broadcast_to([AC, GQ])))
        NSMALL = len(SMALL)

        block = ctx.enter_context(nc.Block())

        @block.sync
        def _(sp):
            def load_x(c, j):
                if not (isinstance(c, int) and c == 0 and j < 2):
                    sp.wait_ge(S["xtr_done"], (4 * c + j - 1) * 2)
                    sp.wait_ge(S["xb_ready"], 4 * c + j - 1)
                sp.dma_start(xt[:, j % 2, :], at(x_d, 4 * c + j)).then_inc(x_in[j % 2], 16)

            def store_res(c, j):
                sp.wait_ge(S["xb_ready"], 4 * c + j + 1)
                sp.dma_start(at(res_d, 4 * c + j), xb[:, :]).then_inc(S["xb_out"], 16)

            def load_res(c, j):
                sp.wait_ge(S["xb_out"], 16 * (4 * c + j + 1))
                if j >= 2:
                    wait_apart(sp, x2_out[j % 2], 16 * (2 * c + j // 2))
                    sp.wait_ge(S["x2tr_done"], 2 * (4 * c + j - 1))
                sp.dma_start(rt[:, j % 2, :], at(res_d, 4 * c + j)).then_inc(r_in[j % 2], 16)

            def store_x2(c, j):
                sp.wait_ge(S["ln2_done"], 4 * c + j + 1)
                sp.dma_start(at(x2_t, 4 * c + j), rt[:, j % 2, :]).then_inc(x2_out[j % 2], 16)

            load_x(0, 0)
            load_x(0, 1)
            for t, src in SMALL:
                sp.dma_start(t, src, allow_slow_non_contiguous=True).then_inc(S["ld_small"], 16)
            for lo, hi in ((CONV, 2 * CONV), (0, CONV), (K0, DIN)):
                sp.dma_start(win[:, :, lo:hi], w_in0[:, lo:hi].rearrange("(k p) n -> p k n", p=P))\
                  .then_inc(S["ld_win"], 16)
            for k in range(KD):
                for kv in range(NKV):
                    sp.dma_start(win[:, k, Q0:K0].rearrange("p (g a d) -> p g a d", g=GQ, a=NKV)[:, :, kv, :],
                                 w_in0[k * P:(k + 1) * P, Q0 + kv * GQ * HD:Q0 + (kv + 1) * GQ * HD]
                                 .rearrange("p (g d) -> p g d", g=GQ)).then_inc(S["ld_win"], 16)
            for k in range(CT):
                sp.dma_start(wout[:, k, :], w_out[0][k * P:(k + 1) * P, :]).then_inc(S["ld_wout"], 16)
            for kv in range(NKV):
                r0 = CONV + kv * GQ * HD
                sp.dma_start(wout[kv * HD:(kv + 1) * HD, CT:KD, :],
                             w_out[0][r0:r0 + GQ * HD, :].rearrange("(g d) n -> d g n", d=HD))\
                  .then_inc(S["ld_wout"], 16)
            store_res(0, 0)
            load_x(0, 2)
            store_res(0, 1)
            load_x(0, 3)
            store_res(0, 2)
            store_res(0, 3)

            def chunk(c, has_out, has_front):
                if has_front:
                    load_x(c + 1, 0)
                    load_x(c + 1, 1)
                if has_out:
                    load_res(c - 1, 0)
                    load_res(c - 1, 1)
                for j in range(TT):
                    if has_front:
                        store_res(c + 1, j)
                        if j < 2:
                            load_x(c + 1, j + 2)
                    if has_out:
                        store_x2(c - 1, j)
                        if j < 2:
                            load_res(c - 1, j + 2)
                if has_out:
                    wait_apart(sp, x2_out[0], 32 * c)
                    wait_apart(sp, x2_out[1], 32 * c)
                    wait_apart(sp, S["x2tr_done"], 8 * c)

            chunk(0, False, True)
            with sp.Fori(1, NCH - 1) as c:
                chunk(c, True, True)
            chunk(NCH - 1, True, False)
            def load_w13(e, s, i):
                sp.dma_start(we[s][0], at(w1[0], e).rearrange("(k p) n -> p k n", p=P)).then_inc(w13_in[s], 16)
                sp.dma_start(we[s][1], at(w3[0], e).rearrange("(k p) n -> p k n", p=P)).then_inc(w13_in[s], 16)

            def load_w2(e, s, i):
                sp.dma_start(we[s][2], at(w2[0], e).rearrange("(k p) n -> p k n", p=P)).then_inc(w2_in[s], 16)

            sp.wait_ge(S["v_done"], NCH)
            load_w13(0, 0, 0)
            load_w2(0, 0, 0)
            c = NCH - 1
            load_res(c, 0)
            load_res(c, 1)
            for j in range(TT):
                store_x2(c, j)
                if j < 2:
                    load_res(c, j + 2)
            sp.wait_ge(S["o_done"], 8 * NCH)
            for s in range(2):
                sp.wait_ge(x2_out[s], 16 * NT // 2)
            sp.wait_ge(S["x2tr_done"], 2 * NT)
            load_w13(1, 1, 0)
            load_w2(1, 1, 0)
            sp.wait_ge(S["r_blk"], 1)
            with sp.Fori(1, NE // 2) as i:
                for s in range(2):
                    nb = sp.value_load(blk_i[0:1, bass.ds(2 * i - 2 + s, 1)], min_val=1, max_val=NT)
                    g0 = sp.value_load(blk_i[0:1, bass.ds(NE + 2 * i - 2 + s, 1)], min_val=0, max_val=MAXB)
                    sp.wait_ge(S["up_done"], (g0 + nb) * 2)
                    load_w13(2 * i + s, s, i)
                    sp.wait_ge(S["dn_done"], g0 + nb)
                    load_w2(2 * i + s, s, i)
            sp.wait_ge(S["dn_done"], sp.value_load(blk_i[0:1, 3 * NE:3 * NE + 1], min_val=1, max_val=MAXB))
            sp.dma_start(lnf[:, 0, :], row(ln_ffn_g[0])).then_inc(S["ld_lnf"], 16)
            sp.dma_start(lnf[:, 1, :], row(ln_ffn_b[0])).then_inc(S["ld_lnf"], 16)
            for s in range(2):
                sp.dma_start(x2r[:, s, :], x2_t[s]).then_inc(x2r_in[s], 16)
            with sp.Fori(0, NT // 2 - 1) as i:
                for s in range(2):
                    sp.wait_ge(S["f_done"], 2 * i + s + 1)
                    sp.dma_start(at(out_d, 2 * i + s), x2r[:, s, :]).then_inc(f_out[s], 16)
                    sp.wait_ge(f_out[s], 16 * (i + 1))
                    sp.dma_start(x2r[:, s, :], at(x2_t, 2 * i + 2 + s)).then_inc(x2r_in[s], 16)
            for s in range(2):
                sp.wait_ge(S["f_done"], NT - 1 + s)
                sp.dma_start(out_d[NT - 2 + s], x2r[:, s, :]).then_inc(f_out[s], 16)
            for s in range(2):
                sp.wait_ge(f_out[s], 16 * NT // 2)

        @block.gpsimd
        def _(pool):
            pool.memset(ident[:, :], 0.0).then_inc(S["c_ident"], 1)
            pool.memset(tri[:, :], 1.0).then_inc(S["c_tri"], 1)
            pool.memset(ones[:, :], 1.0).then_inc(S["c_ones"], 1)
            pool.memset(cmean[:, :], 1.0 / CONV).then_inc(S["c_ones"], 1)
            pool.memset(mhalf[:, :], -0.5).then_inc(S["c_ones"], 1)
            pool.memset(u[:, :, 0:HALO], 0.0).then_inc(S["c_halo"], 1)
            pool.memset(kT[:, :, :], 0.0).then_inc(S["c_halo"], 1)
            pool.wait_ge(S["c_ident"], 1)
            pool.affine_select(out=ident[:, :], in_=ident[:, :], compare_op=ALU.not_equal, fill=1.0,
                               base=0, pattern=[[-1, P]], channel_multiplier=1).then_inc(S["c_ident"], 1)
            pool.wait_ge(S["c_tri"], 1)
            pool.affine_select(out=tri[:, :], in_=tri[:, :], compare_op=ALU.is_gt, fill=0.0,
                               base=0, pattern=[[1, P]], channel_multiplier=-1).then_inc(S["c_tri"], 1)
            pool.iota(tok_u[:, :], pattern=[[P, NT]], base=0, channel_multiplier=1).then_inc(S["c_tri"], 1)
            pool.iota(rev[:, :], pattern=[[-1, EG]], base=EG, channel_multiplier=0,
                      allow_small_or_imprecise_dtypes=True).then_inc(S["c_tri"], 1)
            pool.iota(thr[:, :], pattern=[[P, NT - 1]], base=P, channel_multiplier=0,
                      allow_small_or_imprecise_dtypes=True).then_inc(S["c_tri"], 1)
            pool.wait_ge(S["c_halo"], 2)
            pool.dma_start(slot_d[NS:NS + P, :], kT[:, 0, 0:1].bitcast(I32)).then_inc(S["ld_slot0"], 16)
            pool.wait_ge(S["ld_small"], 16 * NSMALL)
            pool.tensor_scalar(ag_b[:, :], ag_b[:, :], ALPHA, None, ALU.mult).then_inc(S["c_fold"], 1)
            pool.tensor_scalar(ab_b[:, :], ab_b[:, :], ALPHA, None, ALU.mult).then_inc(S["c_fold"], 1)
            pool.wait_ge(S["c_fold"], 2)
            pool.tensor_tensor(ab_b[:, :], ab_b[:, :], xb[:, :], ALU.add).then_inc(S["c_fold"], 1)
            pool.wait_ge(S["c_fold"], 3)

            def rstd(var_sem, rs_sem, n, k):
                pool.wait_ge(S[var_sem], n + 1)
                pool.tensor_tensor(rs[:, k:k + 1], ve[:, k:k + 1], mhalf[:, 0:1], ALU.pow).then_inc(S[rs_sem], 1)

            def residual(c, j):
                n = 4 * c + j
                pool.wait_ge(S["ln1_done"], n + 1)
                if not (isinstance(n, int) and n == 0):
                    pool.wait_ge(S["xb_out"], 16 * n)
                pool.tensor_tensor(xb[:, :], xt[:, j % 2, :], ag_b[:, :], ALU.mult).then_inc(S["xb_st"], 1)
                pool.wait_ge(S["xb_st"], n + 1)
                pool.tensor_tensor(xb[:, :], xb[:, :], ab_b[:, :], ALU.add).then_inc(S["xb_ready"], 1)

            def front(c, j):
                rstd("ln1_var", "ln1_rs", 4 * c + j, 0)
                residual(c, j)

            for j in range(TT):
                front(0, j)

            def chunk(c, has_out, has_front):
                if has_front:
                    front(c + 1, 0)
                for a in range(AS):
                    if a == 2:
                        pool.wait_ge(S["cv_ready"], c + 1)
                        pool.tensor_tensor(cpw[:, :], cve[:, :], mhalf[:, :].broadcast_to([P, TT]), ALU.pow)\
                            .then_inc(S["cpw_ready"], 1)
                    if a % 2 and a < 6 and has_front:
                        front(c + 1, (a + 1) // 2)
                    if a % 2 == 0 and a and has_out:
                        rstd("ln2_var", "ln2_rs", 4 * (c - 1) + a // 2 - 1, 1)
                if has_out:
                    rstd("ln2_var", "ln2_rs", 4 * (c - 1) + 3, 1)

            chunk(0, False, True)
            with pool.Fori(1, NCH - 1) as c:
                chunk(c, True, True)
            chunk(NCH - 1, True, False)
            for j in range(TT):
                rstd("ln2_var", "ln2_rs", 4 * (NCH - 1) + j, 1)

            pool.wait_ge(S["r_idx"], 2)
            pool.wait_ge(S["ld_slot0"], 16)
            pool.wait_ge(S["c_tri"], 3)
            for k in range(2):
                for t in range(NT):
                    pool.indirect_dma_start(slot_d[0:NS, :], bass.IndirectOffsetOnAxis(ap=pos_u[:, k, t:t + 1], axis=0),
                                            tok_u[:, t:t + 1], None).then_inc(S["slot_out"], 16)
            pool.wait_ge(S["slot_out"], 16 * 2 * NT)
            pool.wait_ge(S["r_blk"], 1)
            for s in range(2):
                pool.wait_ge(x2_out[s], 16 * NT // 2)

            def gather(g, slot):
                pool.dma_start(idx[:, :], slot_d[bass.ds(slot, P), :]).then_inc(S["e_idx"], 16)
                wait_apart(pool, S["etr_done"], g * 2 + 2)
                wait_apart(pool, S["e_idx"], g * 16 + 16)
                pool.indirect_dma_start(xg, None, x2_d, bass.IndirectOffsetOnAxis(ap=idx[:, :], axis=0))\
                    .then_inc(S["e_xg"], 16)
                wait_apart(pool, S["e_xg"], g * 16 + 16)

            with pool.Fori(0, NE) as e:
                nb, g0, s0 = expert(pool, e)
                with pool.Fori(0, nb) as b:
                    gather(g0 + b, block_slot(s0, b))
            nall = pool.value_load(blk_i[0:1, 3 * NE:3 * NE + 1], min_val=1, max_val=MAXB)
            gather(nall, 0)
            wait_apart(pool, S["ys_out"], nall * 16 + 16)

            def rows(t, s):
                pool.tensor_copy(idy[:, s, :], pos_u[:, :, bass.ds(t, 1)].rearrange("p k a -> p (k a)"))\
                    .then_inc(S["y_idx"], 1)
                wait_apart(pool, S["y_idx"], t + 1)
                for k, y in enumerate((ya, yb)):
                    pool.indirect_dma_start(y[:, s, :], None, ys_d[0:NS, :],
                                            bass.IndirectOffsetOnAxis(ap=idy[:, s, k:k + 1], axis=0))\
                        .then_inc(y_in[s], 16)

            rows(0, 0)
            rows(1, 1)
            with pool.Fori(1, NT // 2) as i:
                for s in range(2):
                    pool.wait_ge(S["f_var"], 2 * i - 1 + s)
                    pool.tensor_tensor(rs[:, s:s + 1], ve[:, s:s + 1], mhalf[:, 0:1], ALU.pow)\
                        .then_inc(S["f_rs"], 1)
                    rows(2 * i + s, s)
            for s in range(2):
                pool.wait_ge(S["f_var"], NT - 1 + s)
                pool.tensor_tensor(rs[:, s:s + 1], ve[:, s:s + 1], mhalf[:, 0:1], ALU.pow)\
                    .then_inc(S["f_rs"], 1)

        @block.tensor
        def _(pe):
            def x_transposes(c, j, tp_free):
                pe.wait_ge(S["ln1_done"], 4 * c + j + 1)
                tp_free()
                for h in range(2):
                    for k in range(4):
                        m = pe.transpose(TP[h][:, k * P:(k + 1) * P],
                                         xt[:, j % 2, (4 * h + k) * P:(4 * h + k + 1) * P], ident[:, :])
                    m.then_inc(S["xtr_done"], 1)

            def project(dst, c0):
                for k in range(KD):
                    m = pe.matmul(dst, win[:, k, c0:c0 + P], xT[:, k, :], start=(k == 0), stop=(k == KD - 1))
                return m

            def projections(c):
                pe.wait_ge(S["xT_ready"], 8 * (c + 1))
                for ct in range(CT):
                    if isinstance(c, int) and c == 0:
                        if ct == 0:
                            pe.wait_ge(S["ld_win"], 16 * (3 + KD * NKV))
                            pe.wait_ge(S["ld_wout"], 16 * (CT + NKV))
                    if ct >= 2:
                        pe.wait_ge(S["u_ready"], 4 * c + ct - 1)
                    project(PR[2 * (ct % 2) + 1][:, :], CONV + ct * P).then_inc(S["gate_done"], 1)
                    project(PR[2 * (ct % 2)][:, :], ct * P).then_inc(S["a_done"], 1)
                for g in range(GQ):
                    pe.wait_ge(S["u_ready"], 4 * c + 3 + g // 2)
                    project(PR[g][:, :], Q0 + g * P).then_inc(S["q_done"], 1)
                pe.wait_ge(S["qk_ready"], 5 * c + 1)
                project(PR[0][:, :], K0).then_inc(S["q_done"], 1)
                pe.wait_ge(S["qk_ready"], 5 * c + 2)
                for j in range(TT):
                    for k in range(KD):
                        m = pe.matmul(PR[1][:, j * P:(j + 1) * P], xT[:, k, j * P:(j + 1) * P],
                                      win[:, k, V0:DIN], start=(k == 0), stop=(k == KD - 1))
                m.then_inc(S["v_done"], 1)

            def scores(c, a):
                if a == 0:
                    pe.wait_ge(S["qk_ready"], 5 * (c + 1))
                cur = AC + a * AC
                first = isinstance(c, int) and c == 0 and a == 0
                for kv in range(NKV):
                    for gp in range(2):
                        q = qT[:, a, gp * P:(gp + 1) * P]
                        o = (kv * 2 + gp) * P
                        if a % 2:
                            m = pe.matmul(SB[:, o:o + P], q, kT[:, kv, cur - AC:cur + AC], start=True, stop=True)
                        else:
                            m = pe.matmul(SB[:, o:o + AC], q, kT[:, kv, cur:cur + AC], start=True, stop=True)
                            if not first:
                                m = pe.matmul(SB[:, o + AC:o + P], q, kT[:, kv, cur - AC:cur], start=True, stop=True)
                m.then_inc(S["s_done"], 1)

            def p_transposes(c, a):
                pe.wait_ge(S["pn_ready"], 8 * c + a + 1)
                if not (isinstance(c, int) and c == 0 and a == 0):
                    pe.wait_ge(S["o_ready"], 8 * c + a)
                for i in range(GQ):
                    m = pe.transpose(OB[:, i * P:(i + 1) * P], pr[:, i, :], ident[:, :])
                m.then_inc(S["ptr_done"], 1)

            def attend(c, a):
                if a == 0:
                    if isinstance(c, int) and c == 0:
                        pe.wait_ge(S["c_vhalo"], 1)
                    pe.wait_ge(S["v_ready"], c + 1)
                pe.wait_ge(S["pT_ready"], 8 * c + a + 1)
                v = vO[:, a // 2, :] if a % 2 else vE[:, a // 2, :]
                for kv in range(NKV):
                    m = pe.matmul(OB[kv * HD:(kv + 1) * HD, 0:2 * P], v[:, kv * HD:(kv + 1) * HD],
                                  pT[:, 2 * kv:2 * kv + 2, :], start=True, stop=True)
                m.then_inc(S["pv_done"], 1)

            def out_half(c, i):
                j, n = i // 2, i % 2
                for k in range(KD):
                    mt = mixc if k < CT else mixa
                    m = pe.matmul(PR[i % 4][:, :], mt[:, k % CT, j * P:(j + 1) * P],
                                  wout[:, k, n * 512:(n + 1) * 512], start=(k == 0), stop=(k == KD - 1))
                m.then_inc(S["o_done"], 1)

            def x2_transposes(c, j):
                pe.wait_ge(S["ln2_done"], 4 * c + j + 1)
                for h in range(2):
                    for k in range(4):
                        m = pe.transpose(TP[h][:, k * P:(k + 1) * P],
                                         rt[:, j % 2, (4 * h + k) * P:(4 * h + k + 1) * P], ident[:, :])
                    m.then_inc(S["x2tr_done"], 1)

            def router(c, j):
                pe.wait_ge(S["x2T_ready"], 2 * (4 * c + j) + 2)
                for k in range(KD):
                    m = pe.matmul(TP[0][:, 0:NR], x2T[:, k, :], wr[:, k, :], start=(k == 0), stop=(k == KD - 1))
                m.then_inc(S["lg_done"], 1)

            def chunk(c, has_out, has_front):
                projections(c)
                if has_out:
                    pe.wait_ge(S["mixc_ready"], 4 * c)
                    pe.wait_ge(S["o_ready"], 8 * c)
                    pe.wait_ge(S["qk_ready"], 5 * (c + 1))
                    out_half(c - 1, 0)
                for a in range(AS):
                    scores(c, a)
                    if a:
                        attend(c, a - 1)
                    if a == 2:
                        pe.wait_ge(S["uc_ready"], 4 * (c + 1))
                        for ct in range(CT):
                            pe.wait_ge(S["sq_ready"], 4 * c + ct + 1)
                            for j in range(TT):
                                o = ct * TT + j
                                m = pe.matmul(TP[0][:, o:o + 1], sg[:, ct % 2, j * P:(j + 1) * P], cmean[:, 0:1],
                                              start=True, stop=True)
                            m.then_inc(S["var_done"], 1)
                    if a == 3:
                        if has_front:
                            pe.wait_ge(S["xT_ready"], 8 * (c + 1) + 4)
                        pe.wait_ge(S["dg_ready"], c + 1)
                        pe.matmul(TP[1][:, :], ones[:, :], crs[:, :], start=True, stop=True).then_inc(S["bc_done"], 1)
                    if a > 3 and a % 2 and has_out:
                        if has_front:
                            pe.wait_ge(S["xT_ready"], 8 * (c + 1) + 2 * ((a - 1) // 2) + 2)
                        else:
                            pe.wait_ge(S["lg_ready"], 4 * (c - 1) + (a - 3) // 2)
                        x2_transposes(c - 1, (a - 3) // 2)
                    if has_out and a < AS - 1:
                        if a == 0:
                            pe.wait_ge(S["v_ready"], c + 1)
                        if a >= 3:
                            pe.wait_ge(S["o_evac"], 8 * (c - 1) + a - 2)
                        out_half(c - 1, a + 1)
                    if a == 1:
                        if has_front:
                            pe.wait_ge(S["xT_ready"], 8 * (c + 1) + 2)
                        pe.wait_ge(S["conv_st"], CW * CT * (c + 1))
                        for ct in range(CT):
                            m = pe.matmul(TP[0][:, :], cmean[:, :], acc[:, ct, :], start=(ct == 0),
                                          stop=(ct == CT - 1))
                        m.then_inc(S["mean_done"], 1)
                    if a == 3 and has_out:
                        pe.wait_ge(S["crs_ready"], c + 1)
                        x2_transposes(c - 1, 0)
                    if a >= 3 and a % 2 and has_out:
                        router(c - 1, (a - 3) // 2)
                    if a % 2 == 0 and has_front:
                        def tp_free():
                            if a == 0:
                                return
                            elif a == 2:
                                pe.wait_ge(S["cv_ready"], c + 1)
                                pe.wait_ge(S["xT_ready"], 8 * (c + 1) + 2)
                            elif has_out:
                                pe.wait_ge(S["lg_ready"], 4 * (c - 1) + a // 2 - 1)
                            else:
                                if a == 4:
                                    pe.wait_ge(S["crs_ready"], c + 1)
                                pe.wait_ge(S["xT_ready"], 8 * (c + 1) + a)
                        x_transposes(c + 1, a // 2, tp_free)
                    p_transposes(c, a)
                attend(c, AS - 1)
                if has_out:
                    if has_front:
                        pe.wait_ge(S["xT_ready"], 8 * (c + 2))
                    pe.wait_ge(S["lg_ready"], 4 * (c - 1) + 3)
                    x2_transposes(c - 1, 3)
                    router(c - 1, 3)
                    pe.wait_ge(S["lg_ready"], 4 * c)

            pe.wait_ge(S["c_ident"], 2)
            pe.wait_ge(S["c_ones"], 3)
            pe.wait_ge(S["ld_small"], 16 * NSMALL)
            pe.transpose(OB[:, 0:NV], vrow, ident[0:NV, 0:NV])
            for ct in range(CT):
                m = pe.transpose(OB[:, NV + ct * CW:NV + (ct + 1) * CW], wrow[:, ct * P:(ct + 1) * P],
                                 ident[0:CW, 0:CW])
            m.then_inc(S["cols_tr"], 1)
            for j in range(TT):
                x_transposes(0, j, (lambda: pe.wait_ge(S["xT_ready"], 2 * j)) if j else (lambda: None))
            chunk(0, False, True)
            with pe.Fori(1, NCH - 1) as c:
                chunk(c, True, True)
            c = NCH - 1
            chunk(c, True, False)
            pe.wait_ge(S["mixc_ready"], 4 * NCH)
            pe.wait_ge(S["o_ready"], 8 * NCH)
            for i in range(8):
                pe.wait_ge(S["o_evac"], 8 * c + i - 3 if i >= 4 else 8 * c)
                out_half(c, i)
                if i in (3, 5, 7):
                    j = (i - 3) // 2
                    if j:
                        pe.wait_ge(S["lg_ready"], 4 * c + j)
                    x2_transposes(c, j)
                    router(c, j)
            pe.wait_ge(S["lg_ready"], 4 * c + 3)
            x2_transposes(c, 3)
            router(c, 3)

            pe.wait_ge(S["c_tri"], 2)
            pe.wait_ge(S["r_hot"], 1)
            hot = mixc[:, 0, :]
            pe.matmul(PR[0][:, :], tri[:, :], hot, start=True, stop=True).then_inc(S["rk_done"], 1)
            pe.matmul(PR[1][:, :], ones[:, :], hot, start=True, stop=True).then_inc(S["rk_done"], 1)

            def e_transposes(g):
                pe.wait_ge(S["e_xg"], g * 16 + 16)
                for h in range(2):
                    for k in range(4):
                        m = pe.transpose(TP[h][:, k * P:(k + 1) * P], xg[:, (4 * h + k) * P:(4 * h + k + 1) * P],
                                         ident[:, :])
                    m.then_inc(S["etr_done"], 1)

            pe.wait_ge(S["r_blk"], 1)
            pe.wait_ge(S["lg_ready"], 4 * NCH)
            pe.sem_inc(S["etr_done"], 2)
            pe.wait_ge(S["lg_ready"], 4 * NCH)
            e_transposes(0)
            HB, YB = PR[0:2], PR[2:4]
            with pe.Fori(0, NE // 2) as i:
                for s in range(2):
                    nb = pe.value_load(blk_i[0:1, bass.ds(2 * i + s, 1)], min_val=1, max_val=NT)
                    g0 = pe.value_load(blk_i[0:1, bass.ds(NE + 2 * i + s, 1)], min_val=0, max_val=MAXB)
                    wait_apart(pe, w13_in[s], i * 32 + 32)
                    with pe.Fori(0, nb) as b:
                        g = g0 + b
                        pe.wait_ge(S["exa_ready"], g + 1)
                        pe.wait_ge(S["exb_ready"], g + 1)
                        for h in range(2):
                            for w in range(2):
                                for f in range(2):
                                    f0 = (2 * h + f) * P
                                    for k in range(KD):
                                        m = pe.matmul(HB[h][:, (2 * w + f) * P:(2 * w + f + 1) * P],
                                                      we[s][w][:, k, f0:f0 + P], xe[:, k, :],
                                                      start=(k == 0), stop=(k == KD - 1))
                            m.then_inc(S["up_done"], 1)
                        e_transposes(g + 1)
                        pe.wait_ge(w2_in[s], i * 16 + 16)
                        pe.wait_ge(S["ya_free"], g + 1)
                        pe.wait_ge(S["yb_free"], g + 1)
                        for f in range(KE):
                            if f % 2 == 0:
                                pe.wait_ge(S["h_ready"], g * 2 + 1 + f // 2)
                            for n in range(2):
                                m = pe.matmul(YB[n][:, :], he[:, f, :], we[s][2][:, f, n * 512:(n + 1) * 512],
                                              start=(f == 0), stop=(f == KE - 1))
                        m.then_inc(S["dn_done"], 1)

        @block.scalar
        def _(act):
            def xT_evac(c, j):
                if j == 0 and not (isinstance(c, int) and c == 0):
                    act.wait_ge(S["v_done"], c)
                for h in range(2):
                    act.wait_ge(S["xtr_done"], 2 * (4 * c + j) + h + 1)
                    for k in range(4):
                        kk = 4 * h + k
                        m = act.activation(xT[:, kk, j * P:(j + 1) * P], TP[h][:, k * P:(k + 1) * P], ACT.Identity,
                                           bias=lb_in[:, kk:kk + 1], scale=lg_in[:, kk:kk + 1])
                    m.then_inc(S["xT_ready"], 1)

            def x2T_evac(c, j):
                if not (isinstance(c, int) and c == 0) or j:
                    act.wait_ge(S["lg_done"], 4 * c + j)
                for h in range(2):
                    act.wait_ge(S["x2tr_done"], 2 * (4 * c + j) + h + 1)
                    act.copy(x2T[:, 4 * h:4 * h + 4, :], TP[h][:, :].rearrange("p (k n) -> p k n", k=4))\
                       .then_inc(S["x2T_ready"], 1)

            def logits_evac(c, j):
                act.wait_ge(S["lg_done"], 4 * c + j + 1)
                act.copy(logits[:, bass.ds(4 * c + j, 1), :].rearrange("p a n -> p (a n)"), TP[0][:, 0:NR])\
                   .then_inc(S["lg_ready"], 1)

            def chunk(c, has_out, has_front):
                for ct in range(CT):
                    act.wait_ge(S["gate_done"], 4 * c + ct + 1)
                    if ct >= 2:
                        act.wait_ge(S["u_ready"], 4 * c + ct - 1)
                    act.activation(sg[:, ct % 2, :], PR[2 * (ct % 2) + 1][:, :], ACT.Sigmoid,
                                   bias=b_ag[:, CT + ct:CT + ct + 1]).then_inc(S["sg_ready"], 1)
                for g in range(GQ + 1):
                    act.wait_ge(S["q_done"], 5 * c + g + 1)
                    if g < GQ:
                        act.activation(qT[:, :, g * AC:(g + 1) * AC],
                                       PR[g][:, :].rearrange("p (a n) -> p a n", a=AS), ACT.Identity,
                                       bias=b_q[:, g:g + 1])\
                           .then_inc(S["qk_ready"], 1)
                    else:
                        if not (isinstance(c, int) and c == 0):
                            act.wait_ge(S["halo_kv"], 2 * c)
                        for kv in range(NKV):
                            r = slice(kv * HD, (kv + 1) * HD)
                            m = act.activation(kT[r, kv, AC:AC + T], PR[0][r, :], ACT.Identity, bias=b_k[r, 0:1])
                        m.then_inc(S["qk_ready"], 1)
                for a in range(AS):
                    act.wait_ge(S["sm_neg"], 8 * c + a + 1)
                    act.wait_ge(S["s_done"], 8 * c + a + 1)
                    if not (isinstance(c, int) and c == 0 and a == 0):
                        act.wait_ge(S["ptr_done"], 8 * c + a)
                    for i in range(GQ):
                        m = act.activation(pr[:, i, :], SB[:, i * P:(i + 1) * P], ACT.Exp, bias=negm[:, i:i + 1],
                                           scale=SCALE, accum_out=psum_[:, i:i + 1])
                    m.then_inc(S["p_ready"], 1)
                    act.activation(es[:, :], sk[:, :], ACT.Exp).then_inc(S["es_ready"], 1)
                    if a:
                        o_evac(c, a - 1)
                    if a == 2:
                        for ct in range(2, CT):
                            act.wait_ge(S["uc_ready"], 4 * c + ct + 1)
                            act.wait_ge(S["var_done"], 4 * c + ct - 1)
                            act.activation(sg[:, ct % 2, :], acc[:, ct, :], ACT.Square).then_inc(S["sq_ready"], 1)
                    if a == 3:
                        act.wait_ge(S["bc_done"], c + 1)
                        act.copy(crs[:, :], TP[1][:, :]).then_inc(S["crs_ready"], 1)
                    if a >= 3 and a % 2 and has_out:
                        x2T_evac(c - 1, (a - 3) // 2)
                        logits_evac(c - 1, (a - 3) // 2)
                    if a % 2 == 0 and has_front:
                        xT_evac(c + 1, a // 2)
                    act.wait_ge(S["ptr_done"], 8 * c + a + 1)
                    act.copy(pT[:, :, :], OB[:, :].rearrange("p (i n) -> p i n", i=GQ)).then_inc(S["pT_ready"], 1)
                    if a == 1:
                        for ct in range(2):
                            act.wait_ge(S["uc_ready"], 4 * c + ct + 1)
                            act.activation(sg[:, ct, :], acc[:, ct, :], ACT.Square).then_inc(S["sq_ready"], 1)
                o_evac(c, AS - 1)
                act.copy(kT[:, :, 0:AC], kT[:, :, T:T + AC]).then_inc(S["halo_kv"], 1)
                act.copy(vE[HD:P, 0, :], vE[HD:P, TT, :]).then_inc(S["halo_kv"], 1)
                if has_out:
                    x2T_evac(c - 1, 3)
                    logits_evac(c - 1, 3)
                    act.wait_ge(S["o_done"], 8 * c)
                for ct in range(CT):
                    act.wait_ge(S["un_ready"], 4 * c + ct + 1)
                    act.activation(mixc[:, ct, :], acc[:, ct, :], ACT.Silu, bias=lcb[:, ct:ct + 1],
                                   scale=lcg[:, ct:ct + 1]).then_inc(S["mixc_ready"], 1)

            def o_evac(c, a):
                act.wait_ge(S["pv_done"], 8 * c + a + 1)
                act.copy(mixa[:, :, a * AC:(a + 1) * AC], OB[:, 0:2 * P].rearrange("p (g n) -> p g n", g=GQ))\
                   .then_inc(S["o_ready"], 1)

            act.wait_ge(S["ld_small"], 16 * NSMALL)
            act.wait_ge(S["c_halo"], 2)
            act.wait_ge(S["ld_slot0"], 16)
            act.wait_ge(S["cols_tr"], 1)
            act.copy(cols[:, :], OB[:, 0:NV + CT * CW]).then_inc(S["cols_in"], 1)
            act.wait_ge(S["cols_in"], 1)
            for j in range(TT):
                xT_evac(0, j)
            chunk(0, False, True)
            with act.Fori(1, NCH - 1) as c:
                chunk(c, True, True)
            c = NCH - 1
            chunk(c, True, False)
            for j in range(TT):
                x2T_evac(c, j)
                logits_evac(c, j)
            act.wait_ge(S["rt_st"], RT_EXP_G)
            act.activation(r_eg, r_gd, ACT.Exp).then_inc(S["rk_exp"], 1)
            act.wait_ge(S["rt_st"], RT_EXP_E)
            act.activation(r_ee, r_ed, ACT.Exp).then_inc(S["rk_exp"], 1)
            act.sem_inc(S["ya_free"], 1)
            act.sem_inc(S["ys_out"], 16)
            act.wait_ge(S["r_blk"], 1)

            def exa(g):
                act.wait_ge(S["etr_done"], g * 2 + 3)
                act.copy(xe[:, 0:4, :], TP[0][:, :].rearrange("p (k n) -> p k n", k=4)).then_inc(S["exa_ready"], 1)

            exa(0)
            with act.Fori(0, NE) as e:
                nb, g0, s0 = expert(act, e)
                with act.Fori(0, nb) as b:
                    g = g0 + b
                    for h in range(2):
                        act.wait_ge(S["up_done"], g * 2 + h + 1)
                        act.activation(sl[:, h, :], PR[h][:, 0:2 * P], ACT.Silu).then_inc(S["sl_ready"], 1)
                    exa(g + 1)
                    act.wait_ge(S["dn_done"], g + 1)
                    act.wait_ge(S["ys_out"], g * 16 + 16)
                    act.copy(ye[:, 0:512], PR[2][:, :]).then_inc(S["ya_free"], 1)
                    act.wait_ge(S["ya_free"], g + 2)
                    act.wait_ge(S["yb_free"], g + 2)
                    act.dma_start(ys_d[bass.ds(block_slot(s0, b), P), :], ye).then_inc(S["ys_out"], 16)
            with act.Fori(0, NT // 2) as i:
                for s in range(2):
                    t = 2 * i + s
                    act.wait_ge(y_in[s], i * 32 + 32)
                    act.activation(ya[:, s, :], ya[:, s, :], ACT.Copy, scale=gate[:, 0, bass.ds(t, 1)])\
                       .then_inc(S["f_a"], 1)

        @block.vector
        def _(dve):
            def statistics(src, st_sem, per, n, k):
                for h in range(2):
                    dve.bn_stats(bst[:, k, h, :], src[:, h * 512:(h + 1) * 512]).then_inc(S[st_sem], 1)
                wait_apart(dve, S[st_sem], per * n + 2)
                dve.bn_aggr(mv[:, k, :], bst[:, k, :, :].rearrange("p h s -> p (h s)")).then_inc(S[st_sem], 1)
                dve.wait_ge(S[st_sem], per * n + 3)

            def ln1(c, j):
                n = 4 * c + j
                t = xt[:, j % 2, :]
                dve.wait_ge(x_in[j % 2], 16 * (2 * c + j // 2 + 1))
                statistics(t, "ln1_st", 3, n, 0)
                dve.tensor_scalar(ve[:, 0:1], mv[:, 0, 1:2], EPS, None, ALU.add).then_inc(S["ln1_var"], 1)
                dve.wait_ge(S["ln1_rs"], n + 1)
                dve.tensor_scalar(t, t, mv[:, 0, 0:1], rs[:, 0:1], ALU.subtract, ALU.mult).then_inc(S["ln1_done"], 1)

            def ln2(c, j):
                n = 4 * c + j
                t = rt[:, j % 2, :]
                dve.wait_ge(S["o_evac"], 2 * (n + 1))
                statistics(t, "ln2_st", 4, n, 1)
                dve.tensor_scalar(ve[:, 1:2], mv[:, 1, 1:2], EPS, None, ALU.add).then_inc(S["ln2_var"], 1)
                dve.scalar_tensor_tensor(t, t, mv[:, 1, 0:1], gm_b[:, :], ALU.subtract, ALU.mult)\
                   .then_inc(S["ln2_st"], 1)
                dve.wait_ge(S["ln2_st"], 4 * n + 4)
                dve.wait_ge(S["ln2_rs"], n + 1)
                dve.scalar_tensor_tensor(t, t, rs[:, 1:2], bm_b[:, :], ALU.mult, ALU.add).then_inc(S["ln2_done"], 1)

            def glu(c, ct):
                dve.wait_ge(S["sg_ready"], 4 * c + ct + 1)
                dve.wait_ge(S["a_done"], 4 * c + ct + 1)
                if not (isinstance(c, int) and c == 0):
                    dve.wait_ge(S["halo_u"], c)
                dve.scalar_tensor_tensor(u[:, ct, HALO:HALO + T], PR[2 * (ct % 2)][:, :], b_ag[:, ct:ct + 1],
                                         sg[:, ct % 2, :], ALU.add, ALU.mult).then_inc(S["u_ready"], 1)

            def conv_taps(c, pair, k0, k1):
                if pair == 0 and k0 == 0 and not (isinstance(c, int) and c == 0):
                    dve.wait_ge(S["mixc_ready"], 4 * c)
                if k0 == 0:
                    dve.wait_ge(S["u_ready"], 4 * c + 2 * pair + 2)
                for k in range(k0, k1):
                    for q in range(2):
                        ct = 2 * pair + q
                        w = wdw[:, ct, k:k + 1]
                        if k == 0:
                            m = dve.tensor_scalar(acc[:, ct, :], u[:, ct, 0:T], w, None, ALU.mult)
                        else:
                            dve.wait_ge(S["conv_st"], CW * CT * c + 2 * CW * pair + 2 * k + q - 1)
                            m = dve.scalar_tensor_tensor(acc[:, ct, :], u[:, ct, k:k + T], w, acc[:, ct, :],
                                                         ALU.mult, ALU.add)
                        m.then_inc(S["conv_st"], 1)

            def v_evac(c):
                dve.wait_ge(S["v_done"], c + 1)
                if not (isinstance(c, int) and c == 0):
                    dve.wait_ge(S["halo_kv"], 2 * c)
                src = PR[1][:, :].rearrange("p (j n) -> p j n", j=TT)
                bias = bv_b[:, :].unsqueeze(1).broadcast_to([P, TT, P])
                dve.tensor_tensor(vO[:, :, :], src, bias, ALU.add)
                dve.tensor_tensor(vE[0:HD, 0:TT, :], src[0:HD], bias[0:HD], ALU.add)
                dve.tensor_tensor(vE[HD:P, 1:TT + 1, :], src[HD:P], bias[HD:P], ALU.add).then_inc(S["v_ready"], 1)

            def softmax_max(c, a):
                n = 8 * c + a
                dve.wait_ge(S["s_done"], n + 1)
                s3 = SB[:, :].rearrange("p (i n) -> p i n", i=GQ)
                if isinstance(c, int) and n == 0:
                    dve.memset(s3[:, :, AC:P], NEG).then_inc(S["sm0"], 1)
                    dve.wait_ge(S["sm0"], 1)
                dve.tensor_reduce(mx[:, :], s3, AXX, ALU.max).then_inc(S["sm_st"], 1)
                dve.wait_ge(S["sm_st"], 4 * n + 1)
                dve.scalar_tensor_tensor(mm_[:, :], mx[:, :], SCALE, sink_b[:, :], ALU.mult, ALU.max)\
                   .then_inc(S["sm_st"], 1)
                dve.wait_ge(S["sm_st"], 4 * n + 2)
                dve.tensor_tensor(sk[:, :], sink_b[:, :], mm_[:, :], ALU.subtract)
                dve.tensor_scalar(negm[:, :], mm_[:, :], -1.0, None, ALU.mult).then_inc(S["sm_neg"], 1)

            def softmax_norm(c, a):
                n = 8 * c + a
                dve.wait_ge(S["p_ready"], n + 1)
                dve.wait_ge(S["es_ready"], n + 1)
                dve.tensor_tensor(den[:, :], psum_[:, :], es[:, :], ALU.add).then_inc(S["sm_st"], 1)
                dve.wait_ge(S["sm_st"], 4 * n + 3)
                dve.reciprocal(rden[:, :], den[:, :]).then_inc(S["sm_st"], 1)
                dve.wait_ge(S["sm_st"], 4 * n + 4)
                dve.tensor_tensor(pr[:, :, :], pr[:, :, :], rden[:, :].unsqueeze(2).broadcast_to([P, GQ, P]),
                                  ALU.mult).then_inc(S["pn_ready"], 1)

            def out_evac(c, i):
                j, n = i // 2, i % 2
                dve.wait_ge(S["o_done"], 8 * c + i + 1)
                dve.wait_ge(r_in[j % 2], 16 * (2 * c + j // 2 + 1))
                t = rt[:, j % 2, n * 512:(n + 1) * 512]
                dve.tensor_tensor(t, PR[i % 4][:, :], t, ALU.add).then_inc(S["o_evac"], 1)

            def chunk(c, has_out, has_front):
                glu(c, 0)
                glu(c, 1)
                conv_taps(c, 0, 0, 13)
                glu(c, 2)
                conv_taps(c, 0, 13, 22)
                glu(c, 3)
                conv_taps(c, 0, 22, CW)
                conv_taps(c, 1, 0, 20)
                v_evac(c)
                if has_front:
                    ln1(c + 1, 0)
                for a in range(AS):
                    softmax_max(c, a)
                    if a == 0:
                        conv_taps(c, 1, 20, 24)
                    if has_out:
                        out_evac(c - 1, a)
                    softmax_norm(c, a)
                    if a == 0:
                        conv_taps(c, 1, 24, CW)
                        dve.wait_ge(S["conv_st"], CW * CT * (c + 1))
                        dve.tensor_copy(u[:, :, 0:HALO], u[:, :, T:T + HALO]).then_inc(S["halo_u"], 1)
                    if a == 1:
                        dve.wait_ge(S["mean_done"], c + 1)
                        for ct in range(CT):
                            dve.tensor_tensor(acc[:, ct, :], acc[:, ct, :], TP[0][:, :], ALU.subtract)\
                               .then_inc(S["uc_ready"], 1)
                    if a == 3:
                        dve.wait_ge(S["crs_ready"], c + 1)
                        for ct in range(CT):
                            dve.tensor_tensor(acc[:, ct, :], acc[:, ct, :], crs[:, :], ALU.mult)\
                               .then_inc(S["un_ready"], 1)
                    if a % 2 and a < 6 and has_front:
                        ln1(c + 1, (a + 1) // 2)
                    if a == 2:
                        dve.wait_ge(S["var_done"], 4 * (c + 1))
                        dve.tensor_reduce(cve[:, :], TP[0][:, 0:CT * TT].rearrange("p (a j) -> p j a", a=CT), AXX,
                                          ALU.add).then_inc(S["cv_sum"], 1)
                        dve.wait_ge(S["cv_sum"], c + 1)
                        dve.tensor_scalar(cve[:, :], cve[:, :], EPS, None, ALU.add).then_inc(S["cv_ready"], 1)
                    if a % 2 == 0 and a and has_out:
                        ln2(c - 1, a // 2 - 1)
                    if a == 2:
                        dve.wait_ge(S["cpw_ready"], c + 1)
                        dve.tensor_tensor(crs[:, :].rearrange("p (j n) -> p j n", j=TT),
                                          ident[:, :].unsqueeze(1).broadcast_to([P, TT, P]),
                                          cpw[:, :].unsqueeze(2).broadcast_to([P, TT, P]), ALU.mult)\
                           .then_inc(S["dg_ready"], 1)
                if has_out:
                    ln2(c - 1, 3)

            dve.memset(vE[HD:P, 0, :], 0.0).then_inc(S["c_vhalo"], 1)
            dve.wait_ge(S["ld_small"], 16 * NSMALL)
            dve.wait_ge(S["c_halo"], 2)
            for j in range(TT):
                ln1(0, j)
            dve.wait_ge(S["cols_in"], 1)
            chunk(0, False, True)
            with dve.Fori(1, NCH - 1) as c:
                chunk(c, True, True)
            c = NCH - 1
            chunk(c, True, False)
            for i in range(8):
                out_evac(c, i)
                if i % 2:
                    ln2(c, i // 2)

            count = [0]

            def step(m, also=None):
                count[0] += 1
                m.then_inc(S["rt_st"], 1)
                dve.wait_ge(S["rt_st"], count[0])

            def bc(t, axis, shape):
                return t.unsqueeze(axis).broadcast_to(shape)

            G, E = r_G, r_E
            dve.wait_ge(S["lg_ready"], NT)
            dve.wait_ge(S["c_tri"], 5)
            step(dve.tensor_tensor(logits[:, :, :], logits[:, :, :], bc(br_b[:, :], 1, [P, NT, NR]), ALU.add))
            step(dve.tensor_reduce(r_gmax, G, AXX, ALU.max))
            step(dve.tensor_tensor(r_gd, G, bc(r_gmax, 2, [P, NT, NG]), ALU.subtract))
            step(dve.tensor_scalar(r_gk, r_gd, 0.0, None, ALU.is_ge))
            step(dve.tensor_tensor(r_gk, r_gk, bc(rev[:, EG - NG:EG], 1, [P, NT, NG]), ALU.mult))
            step(dve.tensor_reduce(r_gmax, r_gk, AXX, ALU.max))
            step(dve.tensor_tensor(r_hg, r_gk, bc(r_gmax, 2, [P, NT, NG]), ALU.is_equal))
            step(dve.tensor_tensor(r_sel, E, bc(r_hg, 3, [P, NT, NG, EG]), ALU.mult))
            step(dve.tensor_reduce(r_es, r_sel.rearrange("p t g e -> p t e g"), AXX, ALU.add))
            step(dve.tensor_reduce(r_m1, r_es, AXX, ALU.max))

            def first_of(vals, top, hot):
                step(dve.tensor_tensor(r_k8, vals, bc(top, 2, [P, NT, EG]), ALU.is_ge))
                step(dve.tensor_tensor(r_k8, r_k8, bc(rev[:, :], 1, [P, NT, EG]), ALU.mult))
                step(dve.tensor_reduce(r_kmax, r_k8, AXX, ALU.max))
                step(dve.tensor_tensor(hot, r_k8, bc(r_kmax, 2, [P, NT, EG]), ALU.is_equal))

            first_of(r_es, r_m1, r_h1)
            step(dve.scalar_tensor_tensor(r_e2, r_h1, NEG, r_es, ALU.mult, ALU.add))
            step(dve.tensor_reduce(r_m2, r_e2, AXX, ALU.max))
            first_of(r_e2, r_m2, r_h2)
            step(dve.tensor_tensor(r_ed, r_m2, r_m1, ALU.subtract))
            assert count[0] == RT_EXP_E, count[0]
            for hot8, hot in ((r_h1, r_hot1), (r_h2, r_hot2)):
                step(dve.tensor_tensor(hot, bc(r_hg, 3, [P, NT, NG, EG]), bc(hot8, 2, [P, NT, NG, EG]), ALU.mult))
            hot_all = mixc[:, 0, :]
            dve.tensor_tensor(hot_all, flat4(r_hot1), flat4(r_hot2), ALU.add).then_inc(S["r_hot"], 1)
            dve.wait_ge(S["rk_exp"], 2)
            step(dve.tensor_reduce(r_sum, r_eg, AXX, ALU.add))
            step(dve.tensor_scalar(r_one, r_ee, 1.0, None, ALU.add))
            step(dve.tensor_tensor(r_sum, r_sum, r_one, ALU.mult))
            step(dve.reciprocal(gate[:, 0, :], r_sum))
            step(dve.tensor_tensor(gate[:, 1, :], gate[:, 0, :], r_ee, ALU.mult))
            dve.wait_ge(S["rk_done"], 2)
            tot = PR[1][:, :].rearrange("p (t e) -> p t e", e=NE)
            step(dve.memset(r_pre[:, 0, :], 0.0))
            for t in range(NT):
                step(dve.tensor_tensor(r_pre[:, t + 1, :], r_pre[:, t, :], tot[:, t, :], ALU.add))
            cnt = r_pre[:, NT, :]
            step(dve.tensor_tensor(r_cmp, bc(cnt, 2, [P, NE, NT - 1]), bc(thr[:, :], 1, [P, NE, NT - 1]), ALU.is_gt))
            step(dve.tensor_reduce(r_nb, r_cmp, AXX, ALU.add))
            step(dve.tensor_scalar(r_nb, r_nb, 1.0, None, ALU.add))
            step(dve.memset(r_zero, 0.0))
            step(dve.tensor_tensor_scan(r_end, r_nb, r_zero, 0.0, ALU.add, ALU.add))
            step(dve.tensor_tensor(r_beg, r_end, r_nb, ALU.subtract))
            step(dve.tensor_copy(blk_i[0:1, 0:NE], r_nb[0:1, :]))
            step(dve.tensor_copy(blk_i[0:1, NE:2 * NE], r_beg[0:1, :]))
            step(dve.tensor_copy(blk_i[0:1, 3 * NE:3 * NE + 1], r_end[0:1, NE - 1:NE]))
            step(dve.tensor_tensor_scan(r_end, cnt, r_zero, 0.0, ALU.add, ALU.add))
            step(dve.tensor_tensor(r_beg, r_end, cnt, ALU.subtract))
            dve.tensor_copy(blk_i[0:1, 2 * NE:3 * NE], r_beg[0:1, :]).then_inc(S["r_blk"], 1)
            rk = PR[0][:, :].rearrange("p (t e) -> p t e", e=NE)
            step(dve.tensor_tensor(r_rank, rk, r_pre[:, 0:NT, :], ALU.add))
            step(dve.tensor_tensor(r_rank, r_rank, bc(r_beg, 1, [P, NT, NE]), ALU.add))
            for k, hot in enumerate((r_hot1, r_hot2)):
                step(dve.tensor_tensor(r_tmp, hot.rearrange("p t g e -> p t (g e)"), r_rank, ALU.mult))
                step(dve.tensor_reduce(r_pos, r_tmp, AXX, ALU.add))
                dve.tensor_copy(pos_u[:, k, :], r_pos).then_inc(S["r_idx"], 1)
                dve.wait_ge(S["r_idx"], k + 1)

            dve.sem_inc(S["yb_free"], 1)

            def exb(g):
                dve.wait_ge(S["etr_done"], g * 2 + 4)
                dve.tensor_copy(xe[:, 4:8, :], TP[1][:, :].rearrange("p (k n) -> p k n", k=4))\
                   .then_inc(S["exb_ready"], 1)

            exb(0)
            nall = dve.value_load(blk_i[0:1, 3 * NE:3 * NE + 1], min_val=1, max_val=MAXB)
            with dve.Fori(0, nall) as g:
                for h in range(2):
                    dve.wait_ge(S["sl_ready"], g * 2 + h + 1)
                    dve.tensor_tensor(he[:, 2 * h:2 * h + 2, :],
                                      sl[:, h, :].rearrange("p (f n) -> p f n", f=2),
                                      PR[h][:, 2 * P:4 * P].rearrange("p (f n) -> p f n", f=2), ALU.mult)\
                       .then_inc(S["h_ready"], 1)
                exb(g + 1)
                dve.wait_ge(S["dn_done"], g + 1)
                dve.wait_ge(S["ys_out"], g * 16 + 16)
                dve.tensor_copy(ye[:, 512:1024], PR[3][:, :]).then_inc(S["yb_free"], 1)

            dve.wait_ge(S["ld_lnf"], 32)
            with dve.Fori(0, NT // 2) as i:
                for s in range(2):
                    t = 2 * i + s
                    dve.wait_ge(x2r_in[s], i * 16 + 16)
                    dve.wait_ge(S["f_a"], t + 1)
                    dve.scalar_tensor_tensor(x2r[:, s, :], x2r[:, s, :], ALPHA, ya[:, s, :], ALU.mult, ALU.add)\
                       .then_inc(S["f_st"], 1)
                    dve.wait_ge(S["f_st"], t * 6 + 1)
                    dve.scalar_tensor_tensor(x2r[:, s, :], yb[:, s, :], gate[:, 1, bass.ds(t, 1)], x2r[:, s, :],
                                             ALU.mult, ALU.add).then_inc(S["f_st"], 1)
                    dve.wait_ge(S["f_st"], t * 6 + 2)
                    for h in range(2):
                        dve.bn_stats(bst[:, s, h, :], x2r[:, s, h * 512:(h + 1) * 512]).then_inc(S["f_st"], 1)
                    wait_apart(dve, S["f_st"], t * 6 + 4)
                    dve.bn_aggr(mv[:, s, :], bst[:, s, :, :].rearrange("p h s -> p (h s)")).then_inc(S["f_st"], 1)
                    dve.wait_ge(S["f_st"], t * 6 + 5)
                    dve.tensor_scalar(ve[:, s:s + 1], mv[:, s, 1:2], EPS, None, ALU.add).then_inc(S["f_var"], 1)
                    dve.scalar_tensor_tensor(x2r[:, s, :], x2r[:, s, :], mv[:, s, 0:1], lnf[:, 0, :],
                                             ALU.subtract, ALU.mult).then_inc(S["f_st"], 1)
                    dve.wait_ge(S["f_st"], t * 6 + 6)
                    dve.wait_ge(S["f_rs"], t + 1)
                    dve.scalar_tensor_tensor(x2r[:, s, :], x2r[:, s, :], rs[:, s:s + 1], lnf[:, 1, :],
                                             ALU.mult, ALU.add).then_inc(S["f_done"], 1)

    return nc


_INS = ['x', 'ln_in_g', 'ln_in_b', 'w_in', 'b_in', 'w_dw', 'ln_conv_g', 'ln_conv_b', 'sinks', 'w_out', 'b_out',
        'ln_mix_g', 'ln_mix_b', 'w_router_group', 'b_router_group', 'w_router_expert', 'b_router_expert',
        'w1', 'w3', 'w2', 'ln_ffn_g', 'ln_ffn_b']
_OUTS = [((1, SEQ, D), 'float32')]


def kernel(**inputs):
    import numpy as _np
    import concourse.bacc as _bacc
    from concourse import mybir as _mybir
    from concourse.bass_utils import run_bass_kernel_spmd as _run

    nc = _bacc.Bacc("TRN2", target_bir_lowering=False, num_devices=1)
    arrays, args = {}, []
    for name in _INS:
        a = _np.ascontiguousarray(inputs[name])
        arrays[f"in_{name}_dram"] = a
        args.append(nc.dram_tensor(f"in_{name}_dram", a.shape, _mybir.dt.from_np(a.dtype), kind="ExternalInput").ap())
    for i, (shape, dtype) in enumerate(_OUTS):
        dt = _mybir.dt.from_np(_np.dtype(dtype))
        args.append(nc.dram_tensor(f"out_{i}_dram", shape, dt, kind="ExternalOutput").ap())
    build(nc, *args)
    r = _run(nc, [arrays], core_ids=[0])
    return r.results[0]["out_0_dram"]
```

```python
from contextlib import ExitStack

import concourse.bass as bass
from concourse import mybir

F32 = mybir.dt.float32
I32 = mybir.dt.int32
U32 = mybir.dt.uint32
ALU = mybir.AluOpType
ACT = mybir.ActivationFunctionType
AXX = mybir.AxisListType.X

P = 128
D = 1024
SEQ = 2048
KD = D // P
T = 512
NCH = SEQ // T
TT = T // P
NT = SEQ // P
CONV = 512
CT = CONV // P
CW = 31
HALO = CW - 1
HD = 64
NQ = 8
NKV = 2
GQ = NQ // NKV
AC = 64
AS = T // AC
DIN = 2 * CONV + NQ * HD + 2 * NKV * HD
Q0 = 2 * CONV
K0 = Q0 + NQ * HD
V0 = K0 + NKV * HD
NG = 4
EG = 8
NE = NG * EG
NR = NG + NE
DE = 512
KE = DE // P
EPS = 1e-5
ALPHA = 2.0 ** 0.25
SCALE = 1.0 / 8.0
NEG = -3.0e38
NS = 2 * SEQ
MAXB = NS // P + NE


def build(nc, x, ln_in_g, ln_in_b, w_in, b_in, w_dw, ln_conv_g, ln_conv_b, sinks, w_out, b_out,
          ln_mix_g, ln_mix_b, w_rg, b_rg, w_re, b_re, w1, w3, w2, ln_ffn_g, ln_ffn_b, out):
    ctx = ExitStack()
    with ctx:
        def sb(name, shape, dt=F32):
            return ctx.enter_context(nc.sbuf_tensor(name, shape, dt))

        def sem(name):
            return ctx.enter_context(nc.semaphore(name))

        x_d = x.rearrange("a (t p) d -> (a t) p d", p=P)
        out_d = out.rearrange("a (t p) d -> (a t) p d", p=P)
        res_d = nc.dram_tensor("res_d", (NT, P, D), F32).ap()
        x2_d = nc.dram_tensor("x2_d", (SEQ, D), F32).ap()
        x2_t = x2_d.rearrange("(t p) d -> t p d", p=P)
        ys_d = nc.dram_tensor("ys_d", (NS + P, D), F32).ap()

        WN = KD * DE * 2 + KE * D
        arena = sb("arena", [P, 2 * WN])
        win = arena[:, 0:KD * DIN].rearrange("p (k n) -> p k n", k=KD)
        wout = arena[:, KD * DIN:KD * DIN + KD * D].rearrange("p (k n) -> p k n", k=KD)
        rt_at = KD * DIN + KD * D
        rt = arena[:, rt_at:rt_at + 2 * D].rearrange("p (s n) -> p s n", s=2)
        we = []
        for s in range(2):
            o = s * WN
            we.append((arena[:, o:o + KD * DE].rearrange("p (k n) -> p k n", k=KD),
                       arena[:, o + KD * DE:o + 2 * KD * DE].rearrange("p (k n) -> p k n", k=KD),
                       arena[:, o + 2 * KD * DE:o + WN].rearrange("p (k n) -> p k n", k=KE)))
        xt = sb("xt", [P, 2, D])
        xb = sb("xb", [P, D])
        xT = sb("xT", [P, KD, T])
        u = sb("u", [P, CT, HALO + T])
        acc = sb("acc", [P, CT, T])
        sg = sb("sg", [P, 2, T])
        mixc = sb("mixc", [P, CT, T])
        mixa = sb("mixa", [P, GQ, T])
        qT = sb("qT", [P, AS, GQ * AC])
        kT = sb("kT", [P, NKV, AC + T])
        vO = sb("vO", [P, TT, P])
        vE = sb("vE", [P, TT + 1, P])
        pr = sb("pr", [P, GQ, P])
        pT = sb("pT", [P, GQ, P])
        crs = sb("crs", [P, T])
        x2T = sg[:, :, :].rearrange("p a (b n) -> p (a b) n", n=P)
        ag_b = sb("ag_b", [P, D])
        ab_b = sb("ab_b", [P, D])
        gm_b = sb("gm_b", [P, D])
        bm_b = sb("bm_b", [P, D])
        bv_b = sb("bv_b", [P, P])
        ident = sb("ident", [P, P])
        ones = sb("ones", [P, P])
        cmean = sb("cmean", [P, P])
        tri = sb("tri", [P, P])
        wr = sb("wr", [P, KD, NR])
        logits = sb("logits", [P, NT, NR])
        br_b = sb("br_b", [P, NR])
        mhalf = sb("mhalf", [P, 1])
        NV = 2 * KD + 2 * CT + 1 + 2 * CT + GQ
        vrow, wrow = pr[0:NV, 0, :], crs[0:CW, :]
        cols = sb("cols", [P, NV + CT * CW])
        lg_in, lb_in, b_ag, b_k, lcg, lcb, b_q = [
            cols[:, sum(w[:i]):sum(w[:i]) + w[i]] for w in ((KD, KD, 2 * CT, 1, CT, CT, GQ),) for i in range(7)]
        wdw = cols[:, NV:NV + CT * CW].rearrange("p (t w) -> p t w", t=CT)
        sink_b = sb("sink_b", [P, GQ])
        idy = sb("idy", [P, 4, 2], I32)
        nm = sb("nm", [P, 4])
        nr = sb("nr", [P, 4])
        rs4 = sb("rs4", [P, 4])
        ve4 = sb("ve4", [P, 4])
        bst = sb("bst", [P, 2, 2, 6])
        mv = sb("mv", [P, 2, 2])
        ve = sb("ve", [P, 2])
        rs = sb("rs", [P, 2])
        cve = sb("cve", [P, TT])
        cpw = sb("cpw", [P, TT])
        mx = sb("mx", [P, GQ])
        mm_ = sb("mm_", [P, GQ])
        negm = sb("negm", [P, GQ])
        sk = sb("sk", [P, GQ])
        es = sb("es", [P, GQ])
        psum_ = sb("psum_", [P, GQ])
        den = sb("den", [P, GQ])
        rden = sb("rden", [P, GQ])
        rev = sb("rev", [P, EG])
        thr = sb("thr", [P, NT - 1])
        gate = sb("gate", [P, 2, NT])
        pos_u = sb("pos_u", [P, 2, NT], I32)
        blk_i = sb("blk_i", [1, 3 * NE + 1], I32)
        idx = sb("idx", [P, 1], I32)

        xflat = xT[:, :, :].rearrange("p k n -> p (k n)")
        xg = xflat[:, 0:D]
        xe = xflat[:, D:2 * D].rearrange("p (k n) -> p k n", k=KD)
        he = xflat[:, 2 * D:2 * D + DE].rearrange("p (f n) -> p f n", f=KE)
        sl = xflat[:, 2 * D + DE:3 * D].rearrange("p (h n) -> p h n", h=2)
        ye = xflat[:, 3 * D:4 * D]

        def two(t):
            return t[:, :, :].rearrange("p a n -> p (a n)")[:, 0:2 * D].rearrange("p (s n) -> p s n", s=2)
        lnf = two(qT)
        NY = 4
        ya, yb, x2r = [arena[:, i * NY * D:(i + 1) * NY * D].rearrange("p (s n) -> p s n", s=NY) for i in range(3)]

        tab = pT[:, :, :].rearrange("p a n -> p (a n)")[:, 0:MAXB + 1].bitcast(I32)

        uf = u[:, :, :].rearrange("p a n -> p (a n)")
        af = acc[:, :, :].rearrange("p a n -> p (a n)")
        mf = mixa[:, :, :].rearrange("p a n -> p (a n)")
        qf = qT[:, :, :].rearrange("p a n -> p (a n)")

        def flat4(t):
            return t.rearrange("p t g e -> p (t g e)")

        def carve(t, sizes):
            o, got = 0, []
            for shape in sizes:
                n = 1
                for m in shape:
                    n *= m
                v = t[:, o:o + n]
                if len(shape) == 2:
                    v = v.rearrange("p (a b) -> p a b", b=shape[1])
                elif len(shape) == 3:
                    v = v.rearrange("p (a b c) -> p a b c", b=shape[1], c=shape[2])
                got.append(v)
                o += n
            return got

        r_G = logits[:, :, 0:NG]
        r_E = logits[:, :, NG:NR].rearrange("p t (g e) -> p t g e", g=NG)
        (r_gmax, r_gd, r_gk, r_hg, r_eg, r_es, r_k8, r_kmax, r_h1, r_h2, r_e2, r_m1, r_m2, r_ed, r_ee,
         r_sum, r_one, r_nb, r_zero, r_end, r_beg, r_pos) = carve(uf, [
            [NT], [NT, NG], [NT, NG], [NT, NG], [NT, NG], [NT, EG], [NT, EG], [NT], [NT, EG], [NT, EG], [NT, EG],
            [NT], [NT], [NT], [NT], [NT], [NT], [NE], [NE], [NE], [NE], [NT]])
        r_lo, r_hi, r_blk, r_shift, r_cnt = carve(uf[:, 1400:], [[2, NT], [2, NT], [2, NT], [NE], [NE]])
        r_sel, r_hot1, r_hot2 = carve(af, [[NT, NG, EG]] * 3)
        r_tmp, r_rank, r_blkrank = carve(mf, [[NT, NE]] * 3)
        r_cmp, r_tot, r_z = carve(qf, [[NE, NT - 1], [NE, NT], [NE, NT]])
        r_inc = mixc[:, 1, :].rearrange("p (e t) -> p e t", e=NE)
        r_pre = mixc[:, 2, :].rearrange("p (e t) -> p e t", e=NE)
        r_ohl = xT[:, :, :].rearrange("p k n -> p (k n)").rearrange("p (k t n) -> p k t n", k=2, n=P)
        r_ohb = xt[:, :, :].rearrange("p k n -> p (k n)").rearrange("p (k t n) -> p k t n", k=2, n=MAXB)
        r_iota, r_tok = xb[:, 0:P], xb[:, P:P + NT]
        RT_EXP_G, RT_EXP_E = 3, 21

        bank = [ctx.enter_context(nc.psum_tensor(f"bank{i}", [P, 512], F32)) for i in range(8)]
        TP, PR, SB, OB = bank[0:2], bank[2:6], bank[6], bank[7]

        S = {n: sem(n) for n in (
            "passed", "c_ident", "c_tri", "c_ones", "c_bc", "c_fold", "c_halo", "c_vhalo", "cols_tr", "cols_in", "ld_small", "ld_wglu", "ld_win", "ld_wout", 
            "ln1_st", "ln1_var", "ln1_rs", "ln1_done", "xb_st", "xb_ready", "xb_out",
            "xtr_done", "xT_ready", "gate_done", "a_done", "sg_ready", "u_ready", "conv_st", "sm0",
            "halo_u", "mean_done", "uc_ready", "sq_ready", "var_done", "cv_sum", "cv_ready", "cpw_ready", "dg_ready", "bc_done", "crs_ready", "un_ready",
            "mixc_ready", "q_done", "qk_ready", "v_done", "v_ready", "s_done", "sm_st", "sm_neg",
            "p_ready", "es_ready", "pn_ready", "ptr_done", "pT_ready", "pv_done", "o_ready", "halo_kv",
            "o_done", "o_evac", "ln2_st", "ln2_var", "ln2_rs", "ln2_done", "x2tr_done", "x2T_ready",
            "lg_done", "lg_ready",
            "rt_st", "rk_exp", "r_hot", "rk_done", "r_iota", "r_place", "r_ohd", "r_ohp", "r_tabd", "r_tab", "r_idx", "r_blk",
            "e_idx", "e_xg", "etr_done", "exa_ready", "exb_ready", "up_done", "sl_ready", "h_ready",
            "dn_done", "ya_free", "yb_free", "ys_out",
            "y_idx", "f_st", "f_a", "f_var", "f_pow", "f_rs", "f_n", "f_g", "f_done", "ld_lnf")}
        x_in = [sem(f"x_in{i}") for i in range(2)]
        r_in = [sem(f"r_in{i}") for i in range(2)]
        x2_out = [sem(f"x2_out{i}") for i in range(2)]
        w13_in = [sem(f"w13_in{i}") for i in range(2)]
        w2_in = [sem(f"w2_in{i}") for i in range(2)]
        y_in = [sem(f"y_in{i}") for i in range(NY)]
        x2r_in = [sem(f"x2r_in{i}") for i in range(NY)]
        f_out = [sem(f"f_out{i}") for i in range(NY)]

        def at(t, i):
            return t[i] if isinstance(i, int) else t[bass.ds(i, 1)].squeeze(0)

        def wait_apart(eng, semaphore, value):
            eng.wait_ge(semaphore, value)
            eng.sem_inc(S["passed"], 1)

        def expert(eng, e):
            return (eng.value_load(blk_i[0:1, bass.ds(e, 1)], min_val=1, max_val=NT),
                    eng.value_load(blk_i[0:1, bass.ds(e + NE, 1)], min_val=0, max_val=MAXB - 1),
                    eng.value_load(blk_i[0:1, bass.ds(e + 2 * NE, 1)], min_val=0, max_val=NS))

        def block_slot(s0, b):
            return nc.s_assert_within(s0 + b * P, 0, NS, skip_runtime_bounds_check_because=
                                      "a block starts at or before its expert's last slot, or at its empty first")

        def row(v):
            return v.rearrange("(a n) -> a n", a=1).broadcast_to([P, v.shape[0]])

        SMALL = []

        w_in0, b_in0, w_dw0 = w_in[0], b_in[0], w_dw[0]
        SMALL += [
            (ag_b[:, :], row(ln_in_g)), (ab_b[:, :], row(ln_in_b)), (xb[:, :], row(b_out[0])),
            (gm_b[:, :], row(ln_mix_g[0])), (bm_b[:, :], row(ln_mix_b[0])),
            (bv_b[:, :], row(b_in0[V0:DIN])), (br_b[:, 0:NG], row(b_rg[0])), (br_b[:, NG:NR], row(b_re[0])),
            (wr[:, :, 0:NG], w_rg[0].rearrange("(k p) n -> p k n", p=P)),
            (wr[:, :, NG:NR], w_re[0].rearrange("(k p) n -> p k n", p=P)),
        ]
        at_row = 0
        for vec in (ln_in_g, ln_in_b, b_in0[0:2 * CONV], b_in0[K0:V0], ln_conv_g[0], ln_conv_b[0]):
            n = vec.shape[0] // P
            SMALL.append((vrow[at_row:at_row + n, :], vec.rearrange("(k p) -> k p", p=P)))
            at_row += n
        SMALL.append((vrow[at_row:at_row + GQ, :].rearrange("g (a d) -> g a d", a=NKV),
                      b_in0[Q0:K0].rearrange("(a g d) -> g a d", a=NKV, g=GQ)))
        SMALL.append((wrow, w_dw0))
        for g in range(2):
            SMALL.append((sink_b[g * AC:(g + 1) * AC, :],
                          sinks[0].rearrange("(a c g) -> a g c", a=1, g=2)[:, g, :].broadcast_to([AC, GQ])))
        NSMALL = len(SMALL)

        block = ctx.enter_context(nc.Block())

        @block.sync
        def _(sp):
            def load_x(c, j):
                if not (isinstance(c, int) and c == 0 and j < 2):
                    sp.wait_ge(S["xtr_done"], (4 * c + j - 1) * 2)
                    sp.wait_ge(S["xb_ready"], 4 * c + j - 1)
                sp.dma_start(xt[:, j % 2, :], at(x_d, 4 * c + j)).then_inc(x_in[j % 2], 16)

            def store_res(c, j):
                sp.wait_ge(S["xb_ready"], 4 * c + j + 1)
                sp.dma_start(at(res_d, 4 * c + j), xb[:, :]).then_inc(S["xb_out"], 16)

            def load_res(c, j):
                sp.wait_ge(S["xb_out"], 16 * (4 * c + j + 1))
                if j >= 2:
                    wait_apart(sp, x2_out[j % 2], 16 * (2 * c + j // 2))
                    sp.wait_ge(S["x2tr_done"], 2 * (4 * c + j - 1))
                sp.dma_start(rt[:, j % 2, :], at(res_d, 4 * c + j)).then_inc(r_in[j % 2], 16)

            def store_x2(c, j):
                sp.wait_ge(S["ln2_done"], 4 * c + j + 1)
                sp.dma_start(at(x2_t, 4 * c + j), rt[:, j % 2, :]).then_inc(x2_out[j % 2], 16)

            load_x(0, 0)
            load_x(0, 1)
            for t, src in SMALL:
                sp.dma_start(t, src, allow_slow_non_contiguous=True).then_inc(S["ld_small"], 16)
            def load_win(lo, hi, done):
                sp.dma_start(win[:, :, lo:hi], w_in0[:, lo:hi].rearrange("(k p) n -> p k n", p=P))\
                  .then_inc(done, 16)

            load_win(CONV, 2 * CONV, S["ld_wglu"])
            load_x(0, 2)
            load_win(0, CONV, S["ld_wglu"])
            store_res(0, 0)
            store_res(0, 1)
            load_x(0, 3)
            load_win(K0, DIN, S["ld_win"])
            for k in range(KD):
                for kv in range(NKV):
                    sp.dma_start(win[:, k, Q0:K0].rearrange("p (g a d) -> p g a d", g=GQ, a=NKV)[:, :, kv, :],
                                 w_in0[k * P:(k + 1) * P, Q0 + kv * GQ * HD:Q0 + (kv + 1) * GQ * HD]
                                 .rearrange("p (g d) -> p g d", g=GQ)).then_inc(S["ld_win"], 16)
            store_res(0, 2)
            store_res(0, 3)
            for k in range(CT):
                sp.dma_start(wout[:, k, :], w_out[0][k * P:(k + 1) * P, :]).then_inc(S["ld_wout"], 16)
            for kv in range(NKV):
                r0 = CONV + kv * GQ * HD
                sp.dma_start(wout[kv * HD:(kv + 1) * HD, CT:KD, :],
                             w_out[0][r0:r0 + GQ * HD, :].rearrange("(g d) n -> d g n", d=HD))\
                  .then_inc(S["ld_wout"], 16)

            def chunk(c, has_out, has_front):
                if has_front:
                    load_x(c + 1, 0)
                    load_x(c + 1, 1)
                if has_out:
                    load_res(c - 1, 0)
                    load_res(c - 1, 1)
                for j in range(TT):
                    if has_front:
                        store_res(c + 1, j)
                        if j < 2:
                            load_x(c + 1, j + 2)
                    if has_out:
                        store_x2(c - 1, j)
                        if j < 2:
                            load_res(c - 1, j + 2)
                if has_out:
                    wait_apart(sp, x2_out[0], 32 * c)
                    wait_apart(sp, x2_out[1], 32 * c)
                    wait_apart(sp, S["x2tr_done"], 8 * c)

            chunk(0, False, True)
            with sp.Fori(1, NCH - 1) as c:
                chunk(c, True, True)
            chunk(NCH - 1, True, False)
            def load_w13(e, s, i):
                sp.dma_start(we[s][0], at(w1[0], e).rearrange("(k p) n -> p k n", p=P)).then_inc(w13_in[s], 16)
                sp.dma_start(we[s][1], at(w3[0], e).rearrange("(k p) n -> p k n", p=P)).then_inc(w13_in[s], 16)

            def load_w2(e, s, i):
                sp.dma_start(we[s][2], at(w2[0], e).rearrange("(k p) n -> p k n", p=P)).then_inc(w2_in[s], 16)

            sp.wait_ge(S["v_done"], NCH)
            load_w13(0, 0, 0)
            load_w2(0, 0, 0)
            c = NCH - 1
            load_res(c, 0)
            load_res(c, 1)
            for j in range(TT):
                store_x2(c, j)
                if j < 2:
                    load_res(c, j + 2)
            sp.wait_ge(S["o_done"], 8 * NCH)
            for s in range(2):
                sp.wait_ge(x2_out[s], 16 * NT // 2)
            sp.wait_ge(S["x2tr_done"], 2 * NT)
            load_w13(1, 1, 0)
            load_w2(1, 1, 0)
            sp.wait_ge(S["r_blk"], 1)
            with sp.Fori(1, NE // 2) as i:
                for s in range(2):
                    nb = sp.value_load(blk_i[0:1, bass.ds(2 * i - 2 + s, 1)], min_val=1, max_val=NT)
                    g0 = sp.value_load(blk_i[0:1, bass.ds(NE + 2 * i - 2 + s, 1)], min_val=0, max_val=MAXB)
                    sp.wait_ge(S["up_done"], (g0 + nb) * 2)
                    load_w13(2 * i + s, s, i)
                    sp.wait_ge(S["dn_done"], g0 + nb)
                    load_w2(2 * i + s, s, i)
            sp.wait_ge(S["dn_done"], sp.value_load(blk_i[0:1, 3 * NE:3 * NE + 1], min_val=1, max_val=MAXB))
            sp.dma_start(lnf[:, 0, :], row(ln_ffn_g[0])).then_inc(S["ld_lnf"], 16)
            sp.dma_start(lnf[:, 1, :], row(ln_ffn_b[0])).then_inc(S["ld_lnf"], 16)
            for s in range(NY):
                sp.dma_start(x2r[:, s, :], x2_t[s]).then_inc(x2r_in[s], 16)
            with sp.Fori(0, NT // NY - 1) as i:
                for s in range(NY):
                    sp.wait_ge(S["f_done"], NY * i + s + 1)
                    sp.dma_start(at(out_d, NY * i + s), x2r[:, s, :]).then_inc(f_out[s], 16)
                    if s:
                        sp.wait_ge(f_out[s - 1], 16 * (i + 1))
                        sp.dma_start(x2r[:, s - 1, :], at(x2_t, NY * i + NY + s - 1)).then_inc(x2r_in[s - 1], 16)
                sp.wait_ge(f_out[NY - 1], 16 * (i + 1))
                sp.dma_start(x2r[:, NY - 1, :], at(x2_t, NY * i + 2 * NY - 1)).then_inc(x2r_in[NY - 1], 16)
            for s in range(NY):
                sp.wait_ge(S["f_done"], NT - NY + s + 1)
                sp.dma_start(out_d[NT - NY + s], x2r[:, s, :]).then_inc(f_out[s], 16)
            for s in range(NY):
                sp.wait_ge(f_out[s], 16 * NT // NY)

        @block.gpsimd
        def _(pool):
            pool.memset(ident[:, :], 0.0).then_inc(S["c_ident"], 1)
            pool.memset(tri[:, :], 1.0).then_inc(S["c_tri"], 1)
            pool.memset(ones[:, :], 1.0).then_inc(S["c_ones"], 1)
            pool.memset(cmean[:, :], 1.0 / CONV).then_inc(S["c_ones"], 1)
            pool.memset(mhalf[:, :], -0.5).then_inc(S["c_ones"], 1)
            pool.memset(u[:, :, 0:HALO], 0.0).then_inc(S["c_halo"], 1)
            pool.memset(kT[:, :, :], 0.0).then_inc(S["c_halo"], 1)
            pool.wait_ge(S["c_ident"], 1)
            pool.affine_select(out=ident[:, :], in_=ident[:, :], compare_op=ALU.not_equal, fill=1.0,
                               base=0, pattern=[[-1, P]], channel_multiplier=1).then_inc(S["c_ident"], 1)
            pool.wait_ge(S["c_tri"], 1)
            pool.affine_select(out=tri[:, :], in_=tri[:, :], compare_op=ALU.is_gt, fill=0.0,
                               base=0, pattern=[[1, P]], channel_multiplier=-1).then_inc(S["c_tri"], 1)
            pool.iota(rev[:, :], pattern=[[-1, EG]], base=EG, channel_multiplier=0,
                      allow_small_or_imprecise_dtypes=True).then_inc(S["c_tri"], 1)
            pool.iota(thr[:, :], pattern=[[P, NT - 1]], base=P, channel_multiplier=0,
                      allow_small_or_imprecise_dtypes=True).then_inc(S["c_tri"], 1)
            pool.wait_ge(S["ld_small"], 16 * NSMALL)
            pool.wait_ge(S["c_fold"], 2)

            def rstd(var_sem, rs_sem, n, k):
                pool.wait_ge(S[var_sem], n + 1)
                pool.tensor_tensor(rs[:, k:k + 1], ve[:, k:k + 1], mhalf[:, 0:1], ALU.pow).then_inc(S[rs_sem], 1)

            def residual(c, j):
                n = 4 * c + j
                pool.wait_ge(S["ln1_done"], n + 1)
                if not (isinstance(n, int) and n == 0):
                    pool.wait_ge(S["xb_out"], 16 * n)
                pool.tensor_tensor(xb[:, :], xt[:, j % 2, :], ag_b[:, :], ALU.mult).then_inc(S["xb_st"], 1)
                pool.wait_ge(S["xb_st"], n + 1)
                pool.tensor_tensor(xb[:, :], xb[:, :], ab_b[:, :], ALU.add).then_inc(S["xb_ready"], 1)

            def front(c, j):
                rstd("ln1_var", "ln1_rs", 4 * c + j, 0)
                residual(c, j)

            for j in range(TT):
                front(0, j)

            def chunk(c, has_out, has_front):
                if has_front:
                    front(c + 1, 0)
                for a in range(AS):
                    if a == 2:
                        pool.wait_ge(S["cv_ready"], c + 1)
                        pool.tensor_tensor(cpw[:, :], cve[:, :], mhalf[:, :].broadcast_to([P, TT]), ALU.pow)\
                            .then_inc(S["cpw_ready"], 1)
                    if a % 2 and a < 6 and has_front:
                        front(c + 1, (a + 1) // 2)
                    if a % 2 == 0 and a and has_out:
                        rstd("ln2_var", "ln2_rs", 4 * (c - 1) + a // 2 - 1, 1)
                if has_out:
                    rstd("ln2_var", "ln2_rs", 4 * (c - 1) + 3, 1)

            chunk(0, False, True)
            with pool.Fori(1, NCH - 1) as c:
                chunk(c, True, True)
            chunk(NCH - 1, True, False)
            for j in range(TT):
                rstd("ln2_var", "ln2_rs", 4 * (NCH - 1) + j, 1)

            pool.wait_ge(S["xb_out"], 16 * NT)
            pool.iota(r_iota, pattern=[[1, P]], base=0, channel_multiplier=0,
                      allow_small_or_imprecise_dtypes=True).then_inc(S["r_iota"], 1)
            pool.iota(r_tok, pattern=[[P, NT]], base=0, channel_multiplier=1,
                      allow_small_or_imprecise_dtypes=True).then_inc(S["r_iota"], 1)
            pool.wait_ge(S["r_iota"], 2)
            pool.wait_ge(S["r_place"], 2)
            pool.tensor_tensor(r_ohb[:, 1], r_ohb[:, 1], r_tok.unsqueeze(2).broadcast_to([P, NT, MAXB]), ALU.mult)\
                .then_inc(S["r_ohp"], 1)
            pool.wait_ge(S["r_tab"], 1)
            for s in range(2):
                pool.wait_ge(x2_out[s], 16 * NT // 2)

            def gather(g):
                pool.tensor_copy(idx[:, :], tab[:, bass.ds(g, 1)]).then_inc(S["e_idx"], 1)
                wait_apart(pool, S["etr_done"], g * 2 + 2)
                wait_apart(pool, S["e_idx"], g + 1)
                pool.indirect_dma_start(xg, None, x2_d, bass.IndirectOffsetOnAxis(ap=idx[:, :], axis=0))\
                    .then_inc(S["e_xg"], 16)
                wait_apart(pool, S["e_xg"], g * 16 + 16)

            nall = pool.value_load(blk_i[0:1, 3 * NE:3 * NE + 1], min_val=1, max_val=MAXB)
            with pool.Fori(0, nall) as g:
                gather(g)
            gather(nall)
            wait_apart(pool, S["ys_out"], nall * 16 + 16)

            def rows(t, s):
                pool.tensor_copy(idy[:, s, :], pos_u[:, :, bass.ds(t, 1)].rearrange("p k a -> p (k a)"))\
                    .then_inc(S["y_idx"], 1)
                wait_apart(pool, S["y_idx"], t + 1)
                for k, y in enumerate((ya, yb)):
                    pool.indirect_dma_start(y[:, s, :], None, ys_d[0:NS, :],
                                            bass.IndirectOffsetOnAxis(ap=idy[:, s, k:k + 1], axis=0))\
                        .then_inc(y_in[s], 16)

            def rstd4(t, s):
                pool.wait_ge(S["f_var"], t + 1)
                pool.tensor_tensor(rs4[:, s:s + 1], ve4[:, s:s + 1], mhalf[:, 0:1], ALU.pow)\
                    .then_inc(S["f_pow"], 1)
                pool.wait_ge(S["f_pow"], t + 1)
                pool.tensor_tensor(nr[:, s:s + 1], nm[:, s:s + 1], rs4[:, s:s + 1], ALU.mult)\
                    .then_inc(S["f_rs"], 1)

            def shift4(t, s):
                pool.wait_ge(S["f_g"], t + 1)
                pool.tensor_tensor(x2r[:, s, :], x2r[:, s, :], lnf[:, 1, :], ALU.add).then_inc(S["f_done"], 1)

            pool.wait_ge(S["r_idx"], 1)
            wait_apart(pool, S["ld_lnf"], 32)
            for s in range(NY):
                rows(s, s)
            with pool.Fori(0, NT // NY - 1) as i:
                for s in range(NY):
                    rstd4(NY * i + s, s)
                    rows(NY * i + NY + s, s)
                    if s:
                        shift4(NY * i + s - 1, s - 1)
                shift4(NY * i + NY - 1, NY - 1)
            for s in range(NY):
                rstd4(NT - NY + s, s)
                if s:
                    shift4(NT - NY + s - 1, s - 1)
            shift4(NT - 1, NY - 1)

        @block.tensor
        def _(pe):
            def x_transposes(c, j, tp_free):
                pe.wait_ge(S["ln1_done"], 4 * c + j + 1)
                tp_free()
                for h in range(2):
                    for k in range(4):
                        m = pe.transpose(TP[h][:, k * P:(k + 1) * P],
                                         xt[:, j % 2, (4 * h + k) * P:(4 * h + k + 1) * P], ident[:, :])
                    m.then_inc(S["xtr_done"], 1)

            def project(dst, c0):
                for k in range(KD):
                    m = pe.matmul(dst, win[:, k, c0:c0 + P], xT[:, k, :], start=(k == 0), stop=(k == KD - 1))
                return m

            def projections(c):
                pe.wait_ge(S["xT_ready"], 8 * (c + 1))
                for ct in range(CT):
                    if isinstance(c, int) and c == 0:
                        if ct == 0:
                            pe.wait_ge(S["ld_wglu"], 32)
                    if ct >= 2:
                        pe.wait_ge(S["u_ready"], 4 * c + ct - 1)
                    project(PR[2 * (ct % 2) + 1][:, :], CONV + ct * P).then_inc(S["gate_done"], 1)
                    project(PR[2 * (ct % 2)][:, :], ct * P).then_inc(S["a_done"], 1)
                if isinstance(c, int) and c == 0:
                    pe.wait_ge(S["ld_win"], 16 * (1 + KD * NKV))
                    pe.wait_ge(S["ld_wout"], 16 * (CT + NKV))
                for g in range(GQ):
                    pe.wait_ge(S["u_ready"], 4 * c + 3 + g // 2)
                    project(PR[g][:, :], Q0 + g * P).then_inc(S["q_done"], 1)
                pe.wait_ge(S["qk_ready"], 5 * c + 1)
                project(PR[0][:, :], K0).then_inc(S["q_done"], 1)
                pe.wait_ge(S["qk_ready"], 5 * c + 2)
                for j in range(TT):
                    for k in range(KD):
                        m = pe.matmul(PR[1][:, j * P:(j + 1) * P], xT[:, k, j * P:(j + 1) * P],
                                      win[:, k, V0:DIN], start=(k == 0), stop=(k == KD - 1))
                m.then_inc(S["v_done"], 1)

            def scores(c, a):
                if a == 0:
                    pe.wait_ge(S["qk_ready"], 5 * (c + 1))
                cur = AC + a * AC
                first = isinstance(c, int) and c == 0 and a == 0
                for kv in range(NKV):
                    for gp in range(2):
                        q = qT[:, a, gp * P:(gp + 1) * P]
                        o = (kv * 2 + gp) * P
                        if a % 2:
                            m = pe.matmul(SB[:, o:o + P], q, kT[:, kv, cur - AC:cur + AC], start=True, stop=True)
                        else:
                            m = pe.matmul(SB[:, o:o + AC], q, kT[:, kv, cur:cur + AC], start=True, stop=True)
                            if not first:
                                m = pe.matmul(SB[:, o + AC:o + P], q, kT[:, kv, cur - AC:cur], start=True, stop=True)
                m.then_inc(S["s_done"], 1)

            def p_transposes(c, a):
                pe.wait_ge(S["pn_ready"], 8 * c + a + 1)
                if not (isinstance(c, int) and c == 0 and a == 0):
                    pe.wait_ge(S["o_ready"], 8 * c + a)
                for i in range(GQ):
                    m = pe.transpose(OB[:, i * P:(i + 1) * P], pr[:, i, :], ident[:, :])
                m.then_inc(S["ptr_done"], 1)

            def attend(c, a):
                if a == 0:
                    if isinstance(c, int) and c == 0:
                        pe.wait_ge(S["c_vhalo"], 1)
                    pe.wait_ge(S["v_ready"], c + 1)
                pe.wait_ge(S["pT_ready"], 8 * c + a + 1)
                v = vO[:, a // 2, :] if a % 2 else vE[:, a // 2, :]
                for kv in range(NKV):
                    m = pe.matmul(OB[kv * HD:(kv + 1) * HD, 0:2 * P], v[:, kv * HD:(kv + 1) * HD],
                                  pT[:, 2 * kv:2 * kv + 2, :], start=True, stop=True)
                m.then_inc(S["pv_done"], 1)

            def out_half(c, i):
                j, n = i // 2, i % 2
                for k in range(KD):
                    mt = mixc if k < CT else mixa
                    m = pe.matmul(PR[i % 4][:, :], mt[:, k % CT, j * P:(j + 1) * P],
                                  wout[:, k, n * 512:(n + 1) * 512], start=(k == 0), stop=(k == KD - 1))
                m.then_inc(S["o_done"], 1)

            def x2_transposes(c, j):
                pe.wait_ge(S["ln2_done"], 4 * c + j + 1)
                for h in range(2):
                    for k in range(4):
                        m = pe.transpose(TP[h][:, k * P:(k + 1) * P],
                                         rt[:, j % 2, (4 * h + k) * P:(4 * h + k + 1) * P], ident[:, :])
                    m.then_inc(S["x2tr_done"], 1)

            def router(c, j):
                pe.wait_ge(S["x2T_ready"], 2 * (4 * c + j) + 2)
                for k in range(KD):
                    m = pe.matmul(TP[0][:, 0:NR], x2T[:, k, :], wr[:, k, :], start=(k == 0), stop=(k == KD - 1))
                m.then_inc(S["lg_done"], 1)

            def chunk(c, has_out, has_front):
                projections(c)
                if has_out:
                    pe.wait_ge(S["mixc_ready"], 4 * c)
                    pe.wait_ge(S["o_ready"], 8 * c)
                    pe.wait_ge(S["qk_ready"], 5 * (c + 1))
                    out_half(c - 1, 0)
                for a in range(AS):
                    scores(c, a)
                    if a:
                        attend(c, a - 1)
                    if a == 2:
                        pe.wait_ge(S["uc_ready"], 4 * (c + 1))
                        for ct in range(CT):
                            pe.wait_ge(S["sq_ready"], 4 * c + ct + 1)
                            for j in range(TT):
                                o = ct * TT + j
                                m = pe.matmul(TP[0][:, o:o + 1], sg[:, ct % 2, j * P:(j + 1) * P], cmean[:, 0:1],
                                              start=True, stop=True)
                            m.then_inc(S["var_done"], 1)
                    if a == 3:
                        if has_front:
                            pe.wait_ge(S["xT_ready"], 8 * (c + 1) + 4)
                        pe.wait_ge(S["dg_ready"], c + 1)
                        pe.matmul(TP[1][:, :], ones[:, :], crs[:, :], start=True, stop=True).then_inc(S["bc_done"], 1)
                    if a > 3 and a % 2 and has_out:
                        if has_front:
                            pe.wait_ge(S["xT_ready"], 8 * (c + 1) + 2 * ((a - 1) // 2) + 2)
                        else:
                            pe.wait_ge(S["lg_ready"], 4 * (c - 1) + (a - 3) // 2)
                        x2_transposes(c - 1, (a - 3) // 2)
                    if has_out and a < AS - 1:
                        if a == 0:
                            pe.wait_ge(S["v_ready"], c + 1)
                        if a >= 3:
                            pe.wait_ge(S["o_evac"], 8 * (c - 1) + a - 2)
                        out_half(c - 1, a + 1)
                    if a == 1:
                        if has_front:
                            pe.wait_ge(S["xT_ready"], 8 * (c + 1) + 2)
                        pe.wait_ge(S["conv_st"], CW * CT * (c + 1))
                        for ct in range(CT):
                            m = pe.matmul(TP[0][:, :], cmean[:, :], acc[:, ct, :], start=(ct == 0),
                                          stop=(ct == CT - 1))
                        m.then_inc(S["mean_done"], 1)
                    if a == 3 and has_out:
                        pe.wait_ge(S["crs_ready"], c + 1)
                        x2_transposes(c - 1, 0)
                    if a >= 3 and a % 2 and has_out:
                        router(c - 1, (a - 3) // 2)
                    if a % 2 == 0 and has_front:
                        def tp_free():
                            if a == 0:
                                return
                            elif a == 2:
                                pe.wait_ge(S["cv_ready"], c + 1)
                                pe.wait_ge(S["xT_ready"], 8 * (c + 1) + 2)
                            elif has_out:
                                pe.wait_ge(S["lg_ready"], 4 * (c - 1) + a // 2 - 1)
                            else:
                                if a == 4:
                                    pe.wait_ge(S["crs_ready"], c + 1)
                                pe.wait_ge(S["xT_ready"], 8 * (c + 1) + a)
                        x_transposes(c + 1, a // 2, tp_free)
                    p_transposes(c, a)
                attend(c, AS - 1)
                if has_out:
                    if has_front:
                        pe.wait_ge(S["xT_ready"], 8 * (c + 2))
                    pe.wait_ge(S["lg_ready"], 4 * (c - 1) + 3)
                    x2_transposes(c - 1, 3)
                    router(c - 1, 3)
                    pe.wait_ge(S["lg_ready"], 4 * c)

            pe.wait_ge(S["c_ident"], 2)
            pe.wait_ge(S["c_ones"], 3)
            pe.wait_ge(S["ld_small"], 16 * NSMALL)
            pe.transpose(OB[:, 0:NV], vrow, ident[0:NV, 0:NV])
            for ct in range(CT):
                m = pe.transpose(OB[:, NV + ct * CW:NV + (ct + 1) * CW], wrow[:, ct * P:(ct + 1) * P],
                                 ident[0:CW, 0:CW])
            m.then_inc(S["cols_tr"], 1)
            for j in range(TT):
                x_transposes(0, j, (lambda: pe.wait_ge(S["xT_ready"], 2 * j)) if j else (lambda: None))
            chunk(0, False, True)
            with pe.Fori(1, NCH - 1) as c:
                chunk(c, True, True)
            c = NCH - 1
            chunk(c, True, False)
            pe.wait_ge(S["mixc_ready"], 4 * NCH)
            pe.wait_ge(S["o_ready"], 8 * NCH)
            for i in range(8):
                pe.wait_ge(S["o_evac"], 8 * c + i - 3 if i >= 4 else 8 * c)
                out_half(c, i)
                if i in (3, 5, 7):
                    j = (i - 3) // 2
                    if j:
                        pe.wait_ge(S["lg_ready"], 4 * c + j)
                    x2_transposes(c, j)
                    router(c, j)
            pe.wait_ge(S["lg_ready"], 4 * c + 3)
            x2_transposes(c, 3)
            router(c, 3)

            pe.wait_ge(S["c_tri"], 2)
            pe.wait_ge(S["r_hot"], 1)
            hot = mixc[:, 0, :]
            pe.matmul(PR[0][:, :], tri[:, :], hot, start=True, stop=True).then_inc(S["rk_done"], 1)
            pe.matmul(PR[1][:, :], ones[:, :], hot, start=True, stop=True).then_inc(S["rk_done"], 1)
            for k in range(2):
                pe.wait_ge(S["r_ohd"], k + 1)
                if k:
                    pe.wait_ge(S["r_ohp"], 1)
                for t in range(NT):
                    m = pe.matmul(PR[2][:, 0:MAXB], r_ohl[:, k, t, :], r_ohb[:, k, t, :],
                                  start=(k == 0 and t == 0), stop=(k == 1 and t == NT - 1))
            m.then_inc(S["r_tabd"], 1)

            def e_transposes(g):
                pe.wait_ge(S["e_xg"], g * 16 + 16)
                for h in range(2):
                    for k in range(4):
                        m = pe.transpose(TP[h][:, k * P:(k + 1) * P], xg[:, (4 * h + k) * P:(4 * h + k + 1) * P],
                                         ident[:, :])
                    m.then_inc(S["etr_done"], 1)

            pe.wait_ge(S["r_blk"], 1)
            pe.wait_ge(S["r_tab"], 1)
            pe.sem_inc(S["etr_done"], 2)
            pe.wait_ge(S["lg_ready"], 4 * NCH)
            e_transposes(0)
            HB, YB = PR[0:2], PR[2:4]
            with pe.Fori(0, NE // 2) as i:
                for s in range(2):
                    nb = pe.value_load(blk_i[0:1, bass.ds(2 * i + s, 1)], min_val=1, max_val=NT)
                    g0 = pe.value_load(blk_i[0:1, bass.ds(NE + 2 * i + s, 1)], min_val=0, max_val=MAXB)
                    wait_apart(pe, w13_in[s], i * 32 + 32)
                    with pe.Fori(0, nb) as b:
                        g = g0 + b
                        pe.wait_ge(S["exa_ready"], g + 1)
                        pe.wait_ge(S["exb_ready"], g + 1)
                        for h in range(2):
                            for w in range(2):
                                for f in range(2):
                                    f0 = (2 * h + f) * P
                                    for k in range(KD):
                                        m = pe.matmul(HB[h][:, (2 * w + f) * P:(2 * w + f + 1) * P],
                                                      we[s][w][:, k, f0:f0 + P], xe[:, k, :],
                                                      start=(k == 0), stop=(k == KD - 1))
                            m.then_inc(S["up_done"], 1)
                        e_transposes(g + 1)
                        pe.wait_ge(w2_in[s], i * 16 + 16)
                        pe.wait_ge(S["ya_free"], g + 1)
                        pe.wait_ge(S["yb_free"], g + 1)
                        for f in range(KE):
                            if f % 2 == 0:
                                pe.wait_ge(S["h_ready"], g * 2 + 1 + f // 2)
                            for n in range(2):
                                m = pe.matmul(YB[n][:, :], he[:, f, :], we[s][2][:, f, n * 512:(n + 1) * 512],
                                              start=(f == 0), stop=(f == KE - 1))
                        m.then_inc(S["dn_done"], 1)

        @block.scalar
        def _(act):
            def xT_evac(c, j):
                if j == 0 and not (isinstance(c, int) and c == 0):
                    act.wait_ge(S["v_done"], c)
                for h in range(2):
                    act.wait_ge(S["xtr_done"], 2 * (4 * c + j) + h + 1)
                    for k in range(4):
                        kk = 4 * h + k
                        m = act.activation(xT[:, kk, j * P:(j + 1) * P], TP[h][:, k * P:(k + 1) * P], ACT.Identity,
                                           bias=lb_in[:, kk:kk + 1], scale=lg_in[:, kk:kk + 1])
                    m.then_inc(S["xT_ready"], 1)

            def x2T_evac(c, j):
                if not (isinstance(c, int) and c == 0) or j:
                    act.wait_ge(S["lg_done"], 4 * c + j)
                for h in range(2):
                    act.wait_ge(S["x2tr_done"], 2 * (4 * c + j) + h + 1)
                    act.copy(x2T[:, 4 * h:4 * h + 4, :], TP[h][:, :].rearrange("p (k n) -> p k n", k=4))\
                       .then_inc(S["x2T_ready"], 1)

            def logits_evac(c, j):
                act.wait_ge(S["lg_done"], 4 * c + j + 1)
                act.copy(logits[:, bass.ds(4 * c + j, 1), :].rearrange("p a n -> p (a n)"), TP[0][:, 0:NR])\
                   .then_inc(S["lg_ready"], 1)

            def chunk(c, has_out, has_front):
                for ct in range(CT):
                    act.wait_ge(S["gate_done"], 4 * c + ct + 1)
                    if ct >= 2:
                        act.wait_ge(S["u_ready"], 4 * c + ct - 1)
                    act.activation(sg[:, ct % 2, :], PR[2 * (ct % 2) + 1][:, :], ACT.Sigmoid,
                                   bias=b_ag[:, CT + ct:CT + ct + 1]).then_inc(S["sg_ready"], 1)
                for g in range(GQ + 1):
                    act.wait_ge(S["q_done"], 5 * c + g + 1)
                    if g < GQ:
                        act.activation(qT[:, :, g * AC:(g + 1) * AC],
                                       PR[g][:, :].rearrange("p (a n) -> p a n", a=AS), ACT.Identity,
                                       bias=b_q[:, g:g + 1])\
                           .then_inc(S["qk_ready"], 1)
                    else:
                        if not (isinstance(c, int) and c == 0):
                            act.wait_ge(S["halo_kv"], 2 * c)
                        for kv in range(NKV):
                            r = slice(kv * HD, (kv + 1) * HD)
                            m = act.activation(kT[r, kv, AC:AC + T], PR[0][r, :], ACT.Identity, bias=b_k[r, 0:1])
                        m.then_inc(S["qk_ready"], 1)
                for a in range(AS):
                    act.wait_ge(S["sm_neg"], 8 * c + a + 1)
                    act.wait_ge(S["s_done"], 8 * c + a + 1)
                    if not (isinstance(c, int) and c == 0 and a == 0):
                        act.wait_ge(S["ptr_done"], 8 * c + a)
                    for i in range(GQ):
                        m = act.activation(pr[:, i, :], SB[:, i * P:(i + 1) * P], ACT.Exp, bias=negm[:, i:i + 1],
                                           scale=SCALE, accum_out=psum_[:, i:i + 1])
                    m.then_inc(S["p_ready"], 1)
                    act.activation(es[:, :], sk[:, :], ACT.Exp).then_inc(S["es_ready"], 1)
                    if a:
                        o_evac(c, a - 1)
                    if a == 2:
                        for ct in range(2, CT):
                            act.wait_ge(S["uc_ready"], 4 * c + ct + 1)
                            act.wait_ge(S["var_done"], 4 * c + ct - 1)
                            act.activation(sg[:, ct % 2, :], acc[:, ct, :], ACT.Square).then_inc(S["sq_ready"], 1)
                    if a == 3:
                        act.wait_ge(S["bc_done"], c + 1)
                        act.copy(crs[:, :], TP[1][:, :]).then_inc(S["crs_ready"], 1)
                    if a >= 3 and a % 2 and has_out:
                        x2T_evac(c - 1, (a - 3) // 2)
                        logits_evac(c - 1, (a - 3) // 2)
                    if a % 2 == 0 and has_front:
                        xT_evac(c + 1, a // 2)
                    act.wait_ge(S["ptr_done"], 8 * c + a + 1)
                    act.copy(pT[:, :, :], OB[:, :].rearrange("p (i n) -> p i n", i=GQ)).then_inc(S["pT_ready"], 1)
                    if a == 1:
                        for ct in range(2):
                            act.wait_ge(S["uc_ready"], 4 * c + ct + 1)
                            act.activation(sg[:, ct, :], acc[:, ct, :], ACT.Square).then_inc(S["sq_ready"], 1)
                o_evac(c, AS - 1)
                act.copy(kT[:, :, 0:AC], kT[:, :, T:T + AC]).then_inc(S["halo_kv"], 1)
                act.copy(vE[HD:P, 0, :], vE[HD:P, TT, :]).then_inc(S["halo_kv"], 1)
                if has_out:
                    x2T_evac(c - 1, 3)
                    logits_evac(c - 1, 3)
                    act.wait_ge(S["o_done"], 8 * c)
                for ct in range(CT):
                    act.wait_ge(S["un_ready"], 4 * c + ct + 1)
                    act.activation(mixc[:, ct, :], acc[:, ct, :], ACT.Silu, bias=lcb[:, ct:ct + 1],
                                   scale=lcg[:, ct:ct + 1]).then_inc(S["mixc_ready"], 1)

            def o_evac(c, a):
                act.wait_ge(S["pv_done"], 8 * c + a + 1)
                act.copy(mixa[:, :, a * AC:(a + 1) * AC], OB[:, 0:2 * P].rearrange("p (g n) -> p g n", g=GQ))\
                   .then_inc(S["o_ready"], 1)

            act.wait_ge(S["ld_small"], 16 * NSMALL)
            act.wait_ge(S["c_halo"], 2)
            act.wait_ge(S["cols_tr"], 1)
            act.copy(cols[:, :], OB[:, 0:NV + CT * CW]).then_inc(S["cols_in"], 1)
            act.wait_ge(S["cols_in"], 1)
            for j in range(TT):
                xT_evac(0, j)
            chunk(0, False, True)
            with act.Fori(1, NCH - 1) as c:
                chunk(c, True, True)
            c = NCH - 1
            chunk(c, True, False)
            for j in range(TT):
                x2T_evac(c, j)
                logits_evac(c, j)
            act.wait_ge(S["rt_st"], RT_EXP_G)
            act.activation(r_eg, r_gd, ACT.Exp).then_inc(S["rk_exp"], 1)
            act.wait_ge(S["rt_st"], RT_EXP_E)
            act.activation(r_ee, r_ed, ACT.Exp).then_inc(S["rk_exp"], 1)
            act.sem_inc(S["ya_free"], 1)
            act.sem_inc(S["ys_out"], 16)
            act.wait_ge(S["r_blk"], 1)

            def exa(g):
                act.wait_ge(S["etr_done"], g * 2 + 3)
                act.copy(xe[:, 0:4, :], TP[0][:, :].rearrange("p (k n) -> p k n", k=4)).then_inc(S["exa_ready"], 1)

            exa(0)
            with act.Fori(0, NE) as e:
                nb, g0, s0 = expert(act, e)
                with act.Fori(0, nb) as b:
                    g = g0 + b
                    for h in range(2):
                        act.wait_ge(S["up_done"], g * 2 + h + 1)
                        act.activation(sl[:, h, :], PR[h][:, 0:2 * P], ACT.Silu).then_inc(S["sl_ready"], 1)
                    exa(g + 1)
                    act.wait_ge(S["dn_done"], g + 1)
                    act.wait_ge(S["ys_out"], g * 16 + 16)
                    act.copy(ye[:, 0:512], PR[2][:, :]).then_inc(S["ya_free"], 1)
                    act.wait_ge(S["ya_free"], g + 2)
                    act.wait_ge(S["yb_free"], g + 2)
                    act.dma_start(ys_d[bass.ds(block_slot(s0, b), P), :], ye).then_inc(S["ys_out"], 16)
            def norm4(t, s):
                act.wait_ge(S["f_rs"], t + 1)
                act.activation(x2r[:, s, :], x2r[:, s, :], ACT.Identity, bias=nr[:, s:s + 1], scale=rs4[:, s:s + 1])\
                   .then_inc(S["f_n"], 1)

            with act.Fori(0, NT // NY) as i:
                for s in range(NY):
                    t = NY * i + s
                    act.wait_ge(y_in[s], i * 32 + 32)
                    act.activation(ya[:, s, :], ya[:, s, :], ACT.Copy, scale=gate[:, 0, bass.ds(t, 1)])\
                       .then_inc(S["f_a"], 1)
                    if s:
                        norm4(t - 1, s - 1)
                norm4(NY * i + NY - 1, NY - 1)

        @block.vector
        def _(dve):
            def statistics(src, st_sem, per, n, k):
                for h in range(2):
                    dve.bn_stats(bst[:, k, h, :], src[:, h * 512:(h + 1) * 512]).then_inc(S[st_sem], 1)
                wait_apart(dve, S[st_sem], per * n + 2)
                dve.bn_aggr(mv[:, k, :], bst[:, k, :, :].rearrange("p h s -> p (h s)")).then_inc(S[st_sem], 1)
                dve.wait_ge(S[st_sem], per * n + 3)

            def ln1(c, j):
                n = 4 * c + j
                t = xt[:, j % 2, :]
                dve.wait_ge(x_in[j % 2], 16 * (2 * c + j // 2 + 1))
                statistics(t, "ln1_st", 3, n, 0)
                dve.tensor_scalar(ve[:, 0:1], mv[:, 0, 1:2], EPS, None, ALU.add).then_inc(S["ln1_var"], 1)
                dve.wait_ge(S["ln1_rs"], n + 1)
                dve.tensor_scalar(t, t, mv[:, 0, 0:1], rs[:, 0:1], ALU.subtract, ALU.mult).then_inc(S["ln1_done"], 1)

            def ln2(c, j):
                n = 4 * c + j
                t = rt[:, j % 2, :]
                dve.wait_ge(S["o_evac"], 2 * (n + 1))
                statistics(t, "ln2_st", 4, n, 1)
                dve.tensor_scalar(ve[:, 1:2], mv[:, 1, 1:2], EPS, None, ALU.add).then_inc(S["ln2_var"], 1)
                dve.scalar_tensor_tensor(t, t, mv[:, 1, 0:1], gm_b[:, :], ALU.subtract, ALU.mult)\
                   .then_inc(S["ln2_st"], 1)
                dve.wait_ge(S["ln2_st"], 4 * n + 4)
                dve.wait_ge(S["ln2_rs"], n + 1)
                dve.scalar_tensor_tensor(t, t, rs[:, 1:2], bm_b[:, :], ALU.mult, ALU.add).then_inc(S["ln2_done"], 1)

            def glu(c, ct):
                dve.wait_ge(S["sg_ready"], 4 * c + ct + 1)
                dve.wait_ge(S["a_done"], 4 * c + ct + 1)
                if not (isinstance(c, int) and c == 0):
                    dve.wait_ge(S["halo_u"], c)
                dve.scalar_tensor_tensor(u[:, ct, HALO:HALO + T], PR[2 * (ct % 2)][:, :], b_ag[:, ct:ct + 1],
                                         sg[:, ct % 2, :], ALU.add, ALU.mult).then_inc(S["u_ready"], 1)

            def conv_taps(c, pair, k0, k1):
                if pair == 0 and k0 == 0 and not (isinstance(c, int) and c == 0):
                    dve.wait_ge(S["mixc_ready"], 4 * c)
                if k0 == 0:
                    dve.wait_ge(S["u_ready"], 4 * c + 2 * pair + 2)
                for k in range(k0, k1):
                    for q in range(2):
                        ct = 2 * pair + q
                        w = wdw[:, ct, k:k + 1]
                        if k == 0:
                            m = dve.tensor_scalar(acc[:, ct, :], u[:, ct, 0:T], w, None, ALU.mult)
                        else:
                            dve.wait_ge(S["conv_st"], CW * CT * c + 2 * CW * pair + 2 * k + q - 1)
                            m = dve.scalar_tensor_tensor(acc[:, ct, :], u[:, ct, k:k + T], w, acc[:, ct, :],
                                                         ALU.mult, ALU.add)
                        m.then_inc(S["conv_st"], 1)

            def v_evac(c):
                dve.wait_ge(S["v_done"], c + 1)
                if not (isinstance(c, int) and c == 0):
                    dve.wait_ge(S["halo_kv"], 2 * c)
                src = PR[1][:, :].rearrange("p (j n) -> p j n", j=TT)
                bias = bv_b[:, :].unsqueeze(1).broadcast_to([P, TT, P])
                dve.tensor_tensor(vO[:, :, :], src, bias, ALU.add)
                dve.tensor_tensor(vE[0:HD, 0:TT, :], src[0:HD], bias[0:HD], ALU.add)
                dve.tensor_tensor(vE[HD:P, 1:TT + 1, :], src[HD:P], bias[HD:P], ALU.add).then_inc(S["v_ready"], 1)

            def softmax_max(c, a):
                n = 8 * c + a
                dve.wait_ge(S["s_done"], n + 1)
                s3 = SB[:, :].rearrange("p (i n) -> p i n", i=GQ)
                if isinstance(c, int) and n == 0:
                    dve.memset(s3[:, :, AC:P], NEG).then_inc(S["sm0"], 1)
                    dve.wait_ge(S["sm0"], 1)
                dve.tensor_reduce(mx[:, :], s3, AXX, ALU.max).then_inc(S["sm_st"], 1)
                dve.wait_ge(S["sm_st"], 4 * n + 1)
                dve.scalar_tensor_tensor(mm_[:, :], mx[:, :], SCALE, sink_b[:, :], ALU.mult, ALU.max)\
                   .then_inc(S["sm_st"], 1)
                dve.wait_ge(S["sm_st"], 4 * n + 2)
                dve.tensor_tensor(sk[:, :], sink_b[:, :], mm_[:, :], ALU.subtract)
                dve.tensor_scalar(negm[:, :], mm_[:, :], -1.0, None, ALU.mult).then_inc(S["sm_neg"], 1)

            def softmax_norm(c, a):
                n = 8 * c + a
                dve.wait_ge(S["p_ready"], n + 1)
                dve.wait_ge(S["es_ready"], n + 1)
                dve.tensor_tensor(den[:, :], psum_[:, :], es[:, :], ALU.add).then_inc(S["sm_st"], 1)
                dve.wait_ge(S["sm_st"], 4 * n + 3)
                dve.reciprocal(rden[:, :], den[:, :]).then_inc(S["sm_st"], 1)
                dve.wait_ge(S["sm_st"], 4 * n + 4)
                dve.tensor_tensor(pr[:, :, :], pr[:, :, :], rden[:, :].unsqueeze(2).broadcast_to([P, GQ, P]),
                                  ALU.mult).then_inc(S["pn_ready"], 1)

            def out_evac(c, i):
                j, n = i // 2, i % 2
                dve.wait_ge(S["o_done"], 8 * c + i + 1)
                dve.wait_ge(r_in[j % 2], 16 * (2 * c + j // 2 + 1))
                t = rt[:, j % 2, n * 512:(n + 1) * 512]
                dve.tensor_tensor(t, PR[i % 4][:, :], t, ALU.add).then_inc(S["o_evac"], 1)

            def chunk(c, has_out, has_front):
                glu(c, 0)
                glu(c, 1)
                conv_taps(c, 0, 0, 13)
                glu(c, 2)
                conv_taps(c, 0, 13, 22)
                glu(c, 3)
                conv_taps(c, 0, 22, CW)
                conv_taps(c, 1, 0, 20)
                v_evac(c)
                if has_front:
                    ln1(c + 1, 0)
                for a in range(AS):
                    softmax_max(c, a)
                    if a == 0:
                        conv_taps(c, 1, 20, 24)
                    if has_out:
                        out_evac(c - 1, a)
                    softmax_norm(c, a)
                    if a == 0:
                        conv_taps(c, 1, 24, CW)
                        dve.wait_ge(S["conv_st"], CW * CT * (c + 1))
                        dve.tensor_copy(u[:, :, 0:HALO], u[:, :, T:T + HALO]).then_inc(S["halo_u"], 1)
                    if a == 1:
                        dve.wait_ge(S["mean_done"], c + 1)
                        for ct in range(CT):
                            dve.tensor_tensor(acc[:, ct, :], acc[:, ct, :], TP[0][:, :], ALU.subtract)\
                               .then_inc(S["uc_ready"], 1)
                    if a == 3:
                        dve.wait_ge(S["crs_ready"], c + 1)
                        for ct in range(CT):
                            dve.tensor_tensor(acc[:, ct, :], acc[:, ct, :], crs[:, :], ALU.mult)\
                               .then_inc(S["un_ready"], 1)
                    if a % 2 and a < 6 and has_front:
                        ln1(c + 1, (a + 1) // 2)
                    if a == 2:
                        dve.wait_ge(S["var_done"], 4 * (c + 1))
                        dve.tensor_reduce(cve[:, :], TP[0][:, 0:CT * TT].rearrange("p (a j) -> p j a", a=CT), AXX,
                                          ALU.add).then_inc(S["cv_sum"], 1)
                        dve.wait_ge(S["cv_sum"], c + 1)
                        dve.tensor_scalar(cve[:, :], cve[:, :], EPS, None, ALU.add).then_inc(S["cv_ready"], 1)
                    if a % 2 == 0 and a and has_out:
                        ln2(c - 1, a // 2 - 1)
                    if a == 2:
                        dve.wait_ge(S["cpw_ready"], c + 1)
                        dve.tensor_tensor(crs[:, :].rearrange("p (j n) -> p j n", j=TT),
                                          ident[:, :].unsqueeze(1).broadcast_to([P, TT, P]),
                                          cpw[:, :].unsqueeze(2).broadcast_to([P, TT, P]), ALU.mult)\
                           .then_inc(S["dg_ready"], 1)
                if has_out:
                    ln2(c - 1, 3)

            dve.memset(vE[HD:P, 0, :], 0.0).then_inc(S["c_vhalo"], 1)
            dve.wait_ge(S["ld_small"], 16 * NSMALL)
            dve.tensor_scalar(ag_b[:, :], ag_b[:, :], ALPHA, None, ALU.mult).then_inc(S["c_fold"], 1)
            dve.scalar_tensor_tensor(ab_b[:, :], ab_b[:, :], ALPHA, xb[:, :], ALU.mult, ALU.add)\
               .then_inc(S["c_fold"], 1)
            dve.wait_ge(S["c_halo"], 2)
            for j in range(TT):
                ln1(0, j)
            dve.wait_ge(S["cols_in"], 1)
            chunk(0, False, True)
            with dve.Fori(1, NCH - 1) as c:
                chunk(c, True, True)
            c = NCH - 1
            chunk(c, True, False)
            for i in range(8):
                out_evac(c, i)
                if i % 2:
                    ln2(c, i // 2)

            count = [0]

            def step(m, also=None):
                count[0] += 1
                m.then_inc(S["rt_st"], 1)
                dve.wait_ge(S["rt_st"], count[0])

            def flat(t):
                return t.rearrange("p e t -> p (e t)")

            def bc(t, axis, shape):
                return t.unsqueeze(axis).broadcast_to(shape)

            G, E = r_G, r_E
            dve.wait_ge(S["lg_ready"], NT)
            dve.wait_ge(S["c_tri"], 4)
            step(dve.tensor_tensor(logits[:, :, :], logits[:, :, :], bc(br_b[:, :], 1, [P, NT, NR]), ALU.add))
            step(dve.tensor_reduce(r_gmax, G, AXX, ALU.max))
            step(dve.tensor_tensor(r_gd, G, bc(r_gmax, 2, [P, NT, NG]), ALU.subtract))
            step(dve.tensor_scalar(r_gk, r_gd, 0.0, None, ALU.is_ge))
            step(dve.tensor_tensor(r_gk, r_gk, bc(rev[:, EG - NG:EG], 1, [P, NT, NG]), ALU.mult))
            step(dve.tensor_reduce(r_gmax, r_gk, AXX, ALU.max))
            step(dve.tensor_tensor(r_hg, r_gk, bc(r_gmax, 2, [P, NT, NG]), ALU.is_equal))
            step(dve.tensor_tensor(r_sel, E, bc(r_hg, 3, [P, NT, NG, EG]), ALU.mult))
            step(dve.tensor_reduce(r_es, r_sel.rearrange("p t g e -> p t e g"), AXX, ALU.add))
            step(dve.tensor_reduce(r_m1, r_es, AXX, ALU.max))

            def first_of(vals, top, hot):
                step(dve.tensor_tensor(r_k8, vals, bc(top, 2, [P, NT, EG]), ALU.is_ge))
                step(dve.tensor_tensor(r_k8, r_k8, bc(rev[:, :], 1, [P, NT, EG]), ALU.mult))
                step(dve.tensor_reduce(r_kmax, r_k8, AXX, ALU.max))
                step(dve.tensor_tensor(hot, r_k8, bc(r_kmax, 2, [P, NT, EG]), ALU.is_equal))

            first_of(r_es, r_m1, r_h1)
            step(dve.scalar_tensor_tensor(r_e2, r_h1, NEG, r_es, ALU.mult, ALU.add))
            step(dve.tensor_reduce(r_m2, r_e2, AXX, ALU.max))
            first_of(r_e2, r_m2, r_h2)
            step(dve.tensor_tensor(r_ed, r_m2, r_m1, ALU.subtract))
            assert count[0] == RT_EXP_E, count[0]
            for hot8, hot in ((r_h1, r_hot1), (r_h2, r_hot2)):
                step(dve.tensor_tensor(hot, bc(r_hg, 3, [P, NT, NG, EG]), bc(hot8, 2, [P, NT, NG, EG]), ALU.mult))
            hot_all = mixc[:, 0, :]
            dve.tensor_tensor(hot_all, flat4(r_hot1), flat4(r_hot2), ALU.add).then_inc(S["r_hot"], 1)
            dve.wait_ge(S["rk_exp"], 2)
            step(dve.tensor_reduce(r_sum, r_eg, AXX, ALU.add))
            step(dve.tensor_scalar(r_one, r_ee, 1.0, None, ALU.add))
            step(dve.tensor_tensor(r_sum, r_sum, r_one, ALU.mult))
            step(dve.reciprocal(gate[:, 0, :], r_sum))
            step(dve.tensor_tensor(gate[:, 1, :], gate[:, 0, :], r_ee, ALU.mult))
            dve.wait_ge(S["rk_done"], 2)
            tot = PR[1][:, :].rearrange("p (t e) -> p t e", e=NE)
            step(dve.memset(r_z, 0.0))
            step(dve.tensor_copy(r_tot, tot.rearrange("p t e -> p e t")))
            step(dve.tensor_tensor_scan(flat(r_inc), flat(r_tot), flat(r_z), 0.0, ALU.add, ALU.add))
            step(dve.tensor_tensor(r_pre, r_inc, r_tot, ALU.subtract))
            step(dve.tensor_tensor(r_cnt, r_inc[:, :, NT - 1], r_pre[:, :, 0], ALU.subtract))
            step(dve.tensor_tensor(r_cmp, bc(r_cnt, 2, [P, NE, NT - 1]), bc(thr[:, :], 1, [P, NE, NT - 1]), ALU.is_gt))
            step(dve.tensor_reduce(r_nb, r_cmp, AXX, ALU.add))
            step(dve.tensor_scalar(r_nb, r_nb, 1.0, None, ALU.add))
            step(dve.memset(r_zero, 0.0))
            step(dve.tensor_tensor_scan(r_end, r_nb, r_zero, 0.0, ALU.add, ALU.add))
            step(dve.tensor_tensor(r_beg, r_end, r_nb, ALU.subtract))
            step(dve.scalar_tensor_tensor(r_shift, r_beg, float(P), r_pre[:, :, 0], ALU.mult, ALU.subtract))
            rk = PR[0][:, :].rearrange("p (t e) -> p t e", e=NE)
            step(dve.tensor_tensor(r_rank, rk, r_pre.rearrange("p e t -> p t e"), ALU.add))
            step(dve.tensor_tensor(r_blkrank, r_rank, bc(r_shift, 1, [P, NT, NE]), ALU.add))
            for k, hot in enumerate((r_hot1, r_hot2)):
                step(dve.tensor_tensor(r_tmp, hot.rearrange("p t g e -> p t (g e)"), r_blkrank, ALU.mult))
                step(dve.tensor_reduce(r_hi[:, k, :], r_tmp, AXX, ALU.add))
            step(dve.tensor_scalar(r_lo, r_hi, 1.0 / P, -(P / 2 - 0.5) / P, ALU.mult, ALU.add))
            step(dve.tensor_scalar(r_lo, r_lo, 1.5 * 2.0 ** 23, None, ALU.add))
            step(dve.tensor_scalar(r_blk, r_lo, -1.5 * 2.0 ** 23, None, ALU.add))
            step(dve.scalar_tensor_tensor(r_lo, r_blk, -float(P), r_hi, ALU.mult, ALU.add))
            dve.wait_ge(S["r_iota"], 2)

            def one_hot_places(k):
                return dve.tensor_tensor(r_ohl[:, k], bc(r_iota, 1, [P, NT, P]), bc(r_lo[:, k, :], 2, [P, NT, P]),
                                         ALU.is_equal)

            for k in (1, 0):
                dve.tensor_tensor(r_ohb[:, k], bc(r_iota[:, 0:MAXB], 1, [P, NT, MAXB]),
                                  bc(r_blk[:, k, :], 2, [P, NT, MAXB]), ALU.is_equal).then_inc(S["r_place"], 2 if k else 1)
            one_hot_places(0)
            dve.wait_ge(S["r_place"], 3)
            dve.tensor_tensor(r_ohb[:, 0], r_ohb[:, 0], bc(r_tok, 2, [P, NT, MAXB]), ALU.mult).then_inc(S["r_ohd"], 1)
            one_hot_places(1).then_inc(S["r_ohd"], 1)
            step(dve.tensor_copy(blk_i[0:1, 0:NE], r_nb[0:1, :]))
            step(dve.tensor_copy(blk_i[0:1, NE:2 * NE], r_beg[0:1, :]))
            step(dve.tensor_copy(blk_i[0:1, 3 * NE:3 * NE + 1], r_end[0:1, NE - 1:NE]))
            dve.tensor_copy(blk_i[0:1, 2 * NE:3 * NE], r_pre[0:1, :, 0]).then_inc(S["r_blk"], 1)
            dve.memset(tab[:, MAXB:MAXB + 1], 0)
            dve.wait_ge(S["r_tabd"], 1)
            dve.tensor_copy(tab[:, 0:MAXB], PR[2][:, 0:MAXB]).then_inc(S["r_tab"], 1)
            for k, hot in enumerate((r_hot1, r_hot2)):
                step(dve.tensor_tensor(r_tmp, hot.rearrange("p t g e -> p t (g e)"), r_rank, ALU.mult))
                step(dve.tensor_reduce(r_pos, r_tmp, AXX, ALU.add))
                m = dve.tensor_copy(pos_u[:, k, :], r_pos)
                if k == 0:
                    step(m)
                else:
                    m.then_inc(S["r_idx"], 1)

            dve.sem_inc(S["yb_free"], 1)

            def exb(g):
                dve.wait_ge(S["etr_done"], g * 2 + 4)
                dve.tensor_copy(xe[:, 4:8, :], TP[1][:, :].rearrange("p (k n) -> p k n", k=4))\
                   .then_inc(S["exb_ready"], 1)

            exb(0)
            nall = dve.value_load(blk_i[0:1, 3 * NE:3 * NE + 1], min_val=1, max_val=MAXB)
            with dve.Fori(0, nall) as g:
                for h in range(2):
                    dve.wait_ge(S["sl_ready"], g * 2 + h + 1)
                    dve.tensor_tensor(he[:, 2 * h:2 * h + 2, :],
                                      sl[:, h, :].rearrange("p (f n) -> p f n", f=2),
                                      PR[h][:, 2 * P:4 * P].rearrange("p (f n) -> p f n", f=2), ALU.mult)\
                       .then_inc(S["h_ready"], 1)
                exb(g + 1)
                dve.wait_ge(S["dn_done"], g + 1)
                dve.wait_ge(S["ys_out"], g * 16 + 16)
                dve.tensor_copy(ye[:, 512:1024], PR[3][:, :]).then_inc(S["yb_free"], 1)

            dve.wait_ge(S["ld_lnf"], 32)
            def gain4(t, s):
                dve.wait_ge(S["f_n"], t + 1)
                dve.tensor_tensor(x2r[:, s, :], x2r[:, s, :], lnf[:, 0, :], ALU.mult).then_inc(S["f_g"], 1)

            with dve.Fori(0, NT // NY) as i:
                for s in range(NY):
                    t = NY * i + s
                    row = x2r[:, s, :]
                    dve.wait_ge(x2r_in[s], i * 16 + 16)
                    dve.wait_ge(S["f_a"], t + 1)
                    dve.scalar_tensor_tensor(row, row, ALPHA, ya[:, s, :], ALU.mult, ALU.add)\
                       .then_inc(S["f_st"], 1)
                    dve.wait_ge(S["f_st"], t * 5 + 1)
                    dve.scalar_tensor_tensor(row, yb[:, s, :], gate[:, 1, bass.ds(t, 1)], row,
                                             ALU.mult, ALU.add).then_inc(S["f_st"], 1)
                    dve.wait_ge(S["f_st"], t * 5 + 2)
                    for h in range(2):
                        dve.bn_stats(bst[:, s % 2, h, :], row[:, h * 512:(h + 1) * 512]).then_inc(S["f_st"], 1)
                    wait_apart(dve, S["f_st"], t * 5 + 4)
                    dve.bn_aggr(mv[:, s % 2, :], bst[:, s % 2, :, :].rearrange("p h s -> p (h s)"))\
                       .then_inc(S["f_st"], 1)
                    dve.wait_ge(S["f_st"], t * 5 + 5)
                    dve.tensor_scalar(nm[:, s:s + 1], mv[:, s % 2, 0:1], -1.0, None, ALU.mult)
                    dve.tensor_scalar(ve4[:, s:s + 1], mv[:, s % 2, 1:2], EPS, None, ALU.add).then_inc(S["f_var"], 1)
                    if s:
                        gain4(t - 1, s - 1)
                gain4(NY * i + NY - 1, NY - 1)

    return nc


_INS = ['x', 'ln_in_g', 'ln_in_b', 'w_in', 'b_in', 'w_dw', 'ln_conv_g', 'ln_conv_b', 'sinks', 'w_out', 'b_out',
        'ln_mix_g', 'ln_mix_b', 'w_router_group', 'b_router_group', 'w_router_expert', 'b_router_expert',
        'w1', 'w3', 'w2', 'ln_ffn_g', 'ln_ffn_b']
_OUTS = [((1, SEQ, D), 'float32')]


def kernel(**inputs):
    import numpy as _np
    import concourse.bacc as _bacc
    from concourse import mybir as _mybir
    from concourse.bass_utils import run_bass_kernel_spmd as _run

    nc = _bacc.Bacc("TRN2", target_bir_lowering=False, num_devices=1)
    arrays, args = {}, []
    for name in _INS:
        a = _np.ascontiguousarray(inputs[name])
        arrays[f"in_{name}_dram"] = a
        args.append(nc.dram_tensor(f"in_{name}_dram", a.shape, _mybir.dt.from_np(a.dtype), kind="ExternalInput").ap())
    for i, (shape, dtype) in enumerate(_OUTS):
        dt = _mybir.dt.from_np(_np.dtype(dtype))
        args.append(nc.dram_tensor(f"out_{i}_dram", shape, dt, kind="ExternalOutput").ap())
    build(nc, *args)
    r = _run(nc, [arrays], core_ids=[0])
    return r.results[0]["out_0_dram"]
```

```python
from contextlib import ExitStack

import concourse.bass as bass
from concourse import mybir

F32 = mybir.dt.float32
F32R = mybir.dt.float32r
I32 = mybir.dt.int32
U32 = mybir.dt.uint32
ALU = mybir.AluOpType
ACT = mybir.ActivationFunctionType
AXX = mybir.AxisListType.X

P = 128
D = 1024
SEQ = 2048
KD = D // P
T = 512
NCH = SEQ // T
TT = T // P
NT = SEQ // P
CONV = 512
CT = CONV // P
CW = 31
HALO = CW - 1
HD = 64
NQ = 8
NKV = 2
GQ = NQ // NKV
AC = 64
AS = T // AC
DIN = 2 * CONV + NQ * HD + 2 * NKV * HD
Q0 = 2 * CONV
K0 = Q0 + NQ * HD
V0 = K0 + NKV * HD
NG = 4
EG = 8
NE = NG * EG
NR = NG + NE
DE = 512
KE = DE // P
EPS = 1e-5
ALPHA = 2.0 ** 0.25
SCALE = 1.0 / 8.0
NEG = -3.0e38
NS = 2 * SEQ
MAXB = NS // P + NE


def build(nc, x, ln_in_g, ln_in_b, w_in, b_in, w_dw, ln_conv_g, ln_conv_b, sinks, w_out, b_out,
          ln_mix_g, ln_mix_b, w_rg, b_rg, w_re, b_re, w1, w3, w2, ln_ffn_g, ln_ffn_b, out):
    ctx = ExitStack()
    with ctx:
        def sb(name, shape, dt=F32):
            return ctx.enter_context(nc.sbuf_tensor(name, shape, dt))

        def sem(name):
            return ctx.enter_context(nc.semaphore(name))

        x_d = x.rearrange("a (t p) d -> (a t) p d", p=P)
        out_d = out.rearrange("a (t p) d -> (a t) p d", p=P)
        res_d = nc.dram_tensor("res_d", (NT, P, D), F32).ap()
        x2_d = nc.dram_tensor("x2_d", (SEQ, D), F32).ap()
        x2_t = x2_d.rearrange("(t p) d -> t p d", p=P)
        ys_d = nc.dram_tensor("ys_d", (NS + P, D), F32).ap()

        WN = KD * DE * 2 + KE * D
        STAGE = 26488
        arena = sb("arena", [P, 2 * WN])
        arena_at = nc.sbuf_base - 8 * WN
        big = sb("big", [P, STAGE])
        big_at = nc.sbuf_base - 4 * STAGE

        def twin(name, base, first, k, n):
            return nc.alloc_sbuf_tensor_at(name, [P, k, n], F32R, offset=base + 4 * first)
        NW = DIN // P
        NRING, NRAW = 5, 4
        ring = [twin(f"ring{i}", arena_at, i * 2 * D, 2 * KD, P) for i in range(NRING)]
        xTl = twin("xTl", arena_at, NRING * 2 * D, KD, T)
        assert NRING * 2 * D + KD * T == KD * DIN
        wi_d = nc.dram_tensor("wi_d", (NW, P, 2 * KD * P), F32).ap()
        wout = arena[:, KD * DIN:KD * DIN + KD * D].rearrange("p (k n) -> p k n", k=KD)
        rt_at = KD * DIN + KD * D
        rt = arena[:, rt_at:rt_at + 2 * D].rearrange("p (s n) -> p s n", s=2)

        we, wl = [], []
        for s, o in enumerate((0, WN)):
            spans = ((o, KD, DE), (o + KD * DE, KD, DE), (o + 2 * KD * DE, KE, D))
            we.append([arena[:, a:a + k * n].rearrange("p (k n) -> p k n", k=k) for a, k, n in spans])
            wl.append([twin(f"rest{s}_{w}", arena_at, *span) for w, span in enumerate(spans)])
        staged = [0]

        def stage(name, shape):
            o, n = staged[0], 1
            for m in shape[1:]:
                n *= m
            staged[0] = o + n
            assert staged[0] <= STAGE, name
            t = big[:, o:o + n]
            return t if len(shape) == 2 else t.rearrange("p (a b) -> p a b", b=shape[2])

        xt = stage("xt", [P, 2, D])
        xb = stage("xb", [P, D])
        xT_at = staged[0]
        xT = stage("xT", [P, KD, T])
        xTh = twin("xTh", big_at, xT_at, KD, T)
        u = stage("u", [P, CT, HALO + T])
        acc = stage("acc", [P, CT, T])
        sg = stage("sg", [P, 2, T])
        mixc = stage("mixc", [P, CT, T])
        mixa = stage("mixa", [P, GQ, T])
        raw = [m[:, 2 * i:2 * i + 2, :].rearrange("p a n -> p (a n)").rearrange("p (k n) -> p k n", k=KD)
               for m in (mixc, mixa) for i in range(2)]
        qT = stage("qT", [P, AS, GQ * AC])
        kT = stage("kT", [P, NKV, AC + T])
        vO = stage("vO", [P, TT, P])
        vE = stage("vE", [P, TT + 1, P])
        pr = stage("pr", [P, GQ, P])
        pT = stage("pT", [P, GQ, P])
        crs = stage("crs", [P, T])
        x2T = sg[:, :, :].rearrange("p a (b n) -> p (a b) n", n=P)
        ag_b = stage("ag_b", [P, D])
        ab_b = stage("ab_b", [P, D])
        gm_b = stage("gm_b", [P, D])
        bm_b = stage("bm_b", [P, D])
        bv_b = sb("bv_b", [P, P])
        ident = sb("ident", [P, P])
        ones = sb("ones", [P, P])
        cmean = sb("cmean", [P, P])
        tri = sb("tri", [P, P])
        wr = sb("wr", [P, KD, NR])
        logits = sb("logits", [P, NT, NR])
        br_b = sb("br_b", [P, NR])
        mhalf = sb("mhalf", [P, 1])
        NV = 2 * KD + 2 * CT + 1 + 2 * CT + GQ
        vrow, wrow = pr[0:NV, 0, :], crs[0:CW, :]
        cols = sb("cols", [P, NV + CT * CW])
        lg_in, lb_in, b_ag, b_k, lcg, lcb, b_q = [
            cols[:, sum(w[:i]):sum(w[:i]) + w[i]] for w in ((KD, KD, 2 * CT, 1, CT, CT, GQ),) for i in range(7)]
        wdw = cols[:, NV:NV + CT * CW].rearrange("p (t w) -> p t w", t=CT)
        sink_b = sb("sink_b", [P, GQ])
        idy = sb("idy", [P, 4, 2], I32)
        nm = sb("nm", [P, 4])
        nr = sb("nr", [P, 4])
        rs4 = sb("rs4", [P, 4])
        ve4 = sb("ve4", [P, 4])
        bst = sb("bst", [P, 2, 2, 6])
        mv = sb("mv", [P, 2, 2])
        ve = sb("ve", [P, 2])
        rs = sb("rs", [P, 2])
        cve = sb("cve", [P, TT])
        cpw = sb("cpw", [P, TT])
        mx = sb("mx", [P, GQ])
        mm_ = sb("mm_", [P, GQ])
        negm = sb("negm", [P, GQ])
        sk = sb("sk", [P, GQ])
        es = sb("es", [P, GQ])
        psum_ = sb("psum_", [P, GQ])
        den = sb("den", [P, GQ])
        rden = sb("rden", [P, GQ])
        rev = sb("rev", [P, EG])
        thr = sb("thr", [P, NT - 1])
        gate = sb("gate", [P, 2, NT])
        pos_u = sb("pos_u", [P, 2, NT], I32)
        blk_i = sb("blk_i", [1, 3 * NE + 1], I32)
        idx = sb("idx", [P, 1], I32)

        xg = big[:, 0:D]
        at_he = 3 * D
        xeh, xel = twin("xeh", big_at, D, KD, P), twin("xel", big_at, 2 * D, KD, P)
        heh, hel = twin("heh", big_at, at_he, KE, P), twin("hel", big_at, at_he + DE, KE, P)
        sl = big[:, at_he + 2 * DE:at_he + 3 * DE]
        ye = big[:, at_he + 3 * DE:at_he + 3 * DE + D]
        at_h = at_he + 3 * DE + D
        wh13 = [[twin(f"high{s}_{w}", big_at, at_h + (2 * s + w) * KD * DE, KD, DE) for w in range(2)]
                for s in range(2)]
        at_h2 = at_h + 4 * KD * DE
        wh2 = twin("high_w2", big_at, at_h2, KE, D)
        at_tab = at_h2 + KE * D
        assert at_tab + MAXB + 2 <= staged[0]

        def f32(t):
            return t.bitcast(F32)

        def two(t):
            return t[:, :, :].rearrange("p a n -> p (a n)")[:, 0:2 * D].rearrange("p (s n) -> p s n", s=2)
        lnf = two(qT)
        NY = 4
        ya, yb, x2r = [arena[:, i * NY * D:(i + 1) * NY * D].rearrange("p (s n) -> p s n", s=NY) for i in range(3)]

        tab = big[:, at_tab:at_tab + MAXB + 2].bitcast(I32)

        uf = u[:, :, :].rearrange("p a n -> p (a n)")
        af = acc[:, :, :].rearrange("p a n -> p (a n)")
        mf = mixa[:, :, :].rearrange("p a n -> p (a n)")
        qf = qT[:, :, :].rearrange("p a n -> p (a n)")

        def flat4(t):
            return t.rearrange("p t g e -> p (t g e)")

        def carve(t, sizes):
            o, got = 0, []
            for shape in sizes:
                n = 1
                for m in shape:
                    n *= m
                v = t[:, o:o + n]
                if len(shape) == 2:
                    v = v.rearrange("p (a b) -> p a b", b=shape[1])
                elif len(shape) == 3:
                    v = v.rearrange("p (a b c) -> p a b c", b=shape[1], c=shape[2])
                got.append(v)
                o += n
            return got

        r_G = logits[:, :, 0:NG]
        r_E = logits[:, :, NG:NR].rearrange("p t (g e) -> p t g e", g=NG)
        (r_gmax, r_gd, r_gk, r_hg, r_eg, r_es, r_k8, r_kmax, r_h1, r_h2, r_e2, r_m1, r_m2, r_ed, r_ee,
         r_sum, r_one, r_nb, r_zero, r_end, r_beg, r_pos) = carve(uf, [
            [NT], [NT, NG], [NT, NG], [NT, NG], [NT, NG], [NT, EG], [NT, EG], [NT], [NT, EG], [NT, EG], [NT, EG],
            [NT], [NT], [NT], [NT], [NT], [NT], [NE], [NE], [NE], [NE], [NT]])
        r_lo, r_hi, r_blk, r_shift, r_cnt = carve(uf[:, 1400:], [[2, NT], [2, NT], [2, NT], [NE], [NE]])
        r_sel, r_hot1, r_hot2 = carve(af, [[NT, NG, EG]] * 3)
        r_tmp, r_rank, r_blkrank = carve(mf, [[NT, NE]] * 3)
        r_cmp, r_tot, r_z = carve(qf, [[NE, NT - 1], [NE, NT], [NE, NT]])
        r_inc = mixc[:, 1, :].rearrange("p (e t) -> p e t", e=NE)
        r_pre = mixc[:, 2, :].rearrange("p (e t) -> p e t", e=NE)
        r_ohl = xT[:, :, :].rearrange("p k n -> p (k n)").rearrange("p (k t n) -> p k t n", k=2, n=P)
        r_ohb = xt[:, :, :].rearrange("p k n -> p (k n)").rearrange("p (k t n) -> p k t n", k=2, n=MAXB)
        r_iota, r_tok = xb[:, 0:P], xb[:, P:P + NT]
        RT_EXP_G, RT_EXP_E = 3, 21

        bank = [ctx.enter_context(nc.psum_tensor(f"bank{i}", [P, 512], F32)) for i in range(8)]
        TP, PR, SB, OB = bank[0:2], bank[2:6], bank[6], bank[7]
        HT = (OB, PR[1])

        S = {n: sem(n) for n in (
            "passed", "c_ident", "c_tri", "c_ones", "c_fold", "c_halo", "c_vhalo", "cols_tr", "cols_in",
            "ld_small", "w_hi", "w_rest", "xt_gain", "xh_ready", "ld_wout", "ln1_st", "ln1_var", "ln1_rs",
            "ln1_done", "xb_st", "xb_ready", "xb_out", "xtr_done", "xT_ready", "gate_done", "a_done",
            "sg_ready", "u_ready", "conv_st", "sm0", "halo_u", "mean_done", "uc_ready", "sq_ready",
            "var_done", "cv_sum", "cv_ready", "cpw_ready", "dg_ready", "bc_done", "crs_ready", "un_ready",
            "mixc_ready", "q_done", "qk_ready", "v_done", "v_ready", "s_done", "sm_st", "sm_neg", "p_ready",
            "es_ready", "pn_ready", "ptr_done", "pT_ready", "pv_done", "o_ready", "halo_kv", "o_done",
            "o_evac", "ln2_st", "ln2_var", "ln2_rs", "ln2_done", "x2tr_done", "x2T_ready", "lg_done",
            "lg_ready", "rt_st", "rk_exp", "r_hot", "rk_done", "r_iota", "r_place", "r_ohd", "r_ohp",
            "r_tabd", "r_tab", "r_idx", "r_blk", "e_idx", "e_xg", "etr_done", "xeh_ready", "xel_ready",
            "u1_done", "up_done", "hm_ready", "htr_done", "heh_ready", "w1_hi", "w1_lo", "w3_hi", "w3_lo",
            "w2_hi", "w2_lo", "w2_lo2", "sl_ready", "h_ready", "dn_done", "ya_free", "yb_free", "ys_out",
            "y_idx", "f_st", "f_a", "f_var", "f_pow", "f_rs", "f_n", "f_g", "f_done", "ld_lnf")}
        raw_in = [sem(f"raw_in{i}") for i in range(NRAW)]
        tile_out = [sem(f"tile_out{i}") for i in range(NRING)]
        ring_in = [sem(f"ring_in{i}") for i in range(NRING)]
        x_in = [sem(f"x_in{i}") for i in range(2)]
        r_in = [sem(f"r_in{i}") for i in range(2)]
        x2_out = [sem(f"x2_out{i}") for i in range(2)]
        w1_in = [sem(f"w1_in{i}") for i in range(2)]
        w3_in = [sem(f"w3_in{i}") for i in range(2)]
        w2_in = [sem(f"w2_in{i}") for i in range(2)]
        y_in = [sem(f"y_in{i}") for i in range(NY)]
        x2r_in = [sem(f"x2r_in{i}") for i in range(NY)]
        f_out = [sem(f"f_out{i}") for i in range(NY)]

        def at(t, i):
            return t[i] if isinstance(i, int) else t[bass.ds(i, 1)].squeeze(0)

        def raw_loads(n):
            return sum(2 if 2 * CT <= m < 2 * CT + GQ else 1 for m in range(n % NRAW, n + 1, NRAW))

        def wait_used(eng, c, n):
            if n < 2 * CT:
                eng.wait_ge(S["a_done" if n % 2 else "gate_done"], 4 * c + n // 2 + 1)
            elif n < NW - 1:
                eng.wait_ge(S["q_done"], 5 * c + n - 2 * CT + 1)
            else:
                eng.wait_ge(S["v_done"], c + 1)

        def wait_apart(eng, semaphore, value):
            eng.wait_ge(semaphore, value)
            eng.sem_inc(S["passed"], 1)

        def expert(eng, e):
            return (eng.value_load(blk_i[0:1, bass.ds(e, 1)], min_val=1, max_val=NT),
                    eng.value_load(blk_i[0:1, bass.ds(e + NE, 1)], min_val=0, max_val=MAXB - 1),
                    eng.value_load(blk_i[0:1, bass.ds(e + 2 * NE, 1)], min_val=0, max_val=NS))

        def block_slot(s0, b):
            return nc.s_assert_within(s0 + b * P, 0, NS, skip_runtime_bounds_check_because=
                                      "a block starts at or before its expert's last slot, or at its empty first")

        def row(v):
            return v.rearrange("(a n) -> a n", a=1).broadcast_to([P, v.shape[0]])

        SMALL = []

        w_in0, b_in0, w_dw0 = w_in[0], b_in[0], w_dw[0]
        SMALL += [
            (ag_b[:, :], row(ln_in_g)), (ab_b[:, :], row(ln_in_b)), (xb[:, :], row(b_out[0])),
            (gm_b[:, :], row(ln_mix_g[0])), (bm_b[:, :], row(ln_mix_b[0])),
            (bv_b[:, :], row(b_in0[V0:DIN])), (br_b[:, 0:NG], row(b_rg[0])), (br_b[:, NG:NR], row(b_re[0])),
            (wr[:, :, 0:NG], w_rg[0].rearrange("(k p) n -> p k n", p=P)),
            (wr[:, :, NG:NR], w_re[0].rearrange("(k p) n -> p k n", p=P)),
        ]
        at_row = 0
        for vec in (ln_in_g, ln_in_b, b_in0[0:2 * CONV], b_in0[K0:V0], ln_conv_g[0], ln_conv_b[0]):
            n = vec.shape[0] // P
            SMALL.append((vrow[at_row:at_row + n, :], vec.rearrange("(k p) -> k p", p=P)))
            at_row += n
        SMALL.append((vrow[at_row:at_row + GQ, :].rearrange("g (a d) -> g a d", a=NKV),
                      b_in0[Q0:K0].rearrange("(a g d) -> g a d", a=NKV, g=GQ)))
        SMALL.append((wrow, w_dw0))
        for g in range(2):
            SMALL.append((sink_b[g * AC:(g + 1) * AC, :],
                          sinks[0].rearrange("(a c g) -> a g c", a=1, g=2)[:, g, :].broadcast_to([AC, GQ])))
        NSMALL = len(SMALL)

        block = ctx.enter_context(nc.Block())

        @block.sync
        def _(sp):
            def load_x(c, j):
                if not (isinstance(c, int) and c == 0 and j < 2):
                    sp.wait_ge(S["xtr_done"], (4 * c + j - 1) * 2)
                    sp.wait_ge(S["xb_ready"], 4 * c + j - 1)
                sp.dma_start(xt[:, j % 2, :], at(x_d, 4 * c + j)).then_inc(x_in[j % 2], 16)

            def store_res(c, j):
                sp.wait_ge(S["xb_ready"], 4 * c + j + 1)
                sp.dma_start(at(res_d, 4 * c + j), xb[:, :]).then_inc(S["xb_out"], 16)

            def load_res(c, j):
                sp.wait_ge(S["xb_out"], 16 * (4 * c + j + 1))
                if j >= 2:
                    wait_apart(sp, x2_out[j % 2], 16 * (2 * c + j // 2))
                    sp.wait_ge(S["x2tr_done"], 2 * (4 * c + j - 1))
                sp.dma_start(rt[:, j % 2, :], at(res_d, 4 * c + j)).then_inc(r_in[j % 2], 16)

            def store_x2(c, j):
                sp.wait_ge(S["ln2_done"], 4 * c + j + 1)
                sp.dma_start(at(x2_t, 4 * c + j), rt[:, j % 2, :]).then_inc(x2_out[j % 2], 16)

            load_x(0, 0)
            load_x(0, 1)
            for t, src in SMALL:
                sp.dma_start(t, src, allow_slow_non_contiguous=True).then_inc(S["ld_small"], 16)
            def load_raw(n):
                if n >= NRAW:
                    sp.wait_ge(S["w_rest"], n - NRAW + 1)
                done = raw_in[n % NRAW]
                if 2 * CT <= n < 2 * CT + GQ:
                    for kv in range(NKV):
                        c0 = Q0 + (kv * GQ + n - 2 * CT) * HD
                        sp.dma_start(raw[n % NRAW][:, :, kv * HD:(kv + 1) * HD],
                                     w_in0[:, c0:c0 + HD].rearrange("(k p) n -> p k n", p=P)).then_inc(done, 16)
                else:
                    c0 = (0 if n % 2 else CONV) + n // 2 * P if n < 2 * CT else K0 + (n - NW + 2) * P
                    sp.dma_start(raw[n % NRAW], w_in0[:, c0:c0 + P].rearrange("(k p) n -> p k n", p=P))\
                      .then_inc(done, 16)

            def store_tile(n):
                sp.wait_ge(S["w_rest"], n + 1)
                sp.dma_start(wi_d[n], f32(ring[n % NRING][:, :, :].rearrange("p k n -> p (k n)")))\
                  .then_inc(tile_out[n % NRING], 16)

            def load_tile(c, n):
                last = n - NRING if n >= NRING else n + (NW - 1 - n) // NRING * NRING
                wait_used(sp, c if n >= NRING else c - 1, last)
                sp.dma_start(f32(ring[n % NRING][:, :, :].rearrange("p k n -> p (k n)")), wi_d[n])\
                  .then_inc(ring_in[n % NRING], 16)

            for n in range(NRAW):
                load_raw(n)
            load_x(0, 2)
            store_res(0, 0)
            store_tile(0)
            load_raw(NRAW)
            store_res(0, 1)
            load_x(0, 3)
            for n in range(1, NW):
                store_tile(n)
                if n + NRAW < NW:
                    load_raw(n + NRAW)
                if n == 3:
                    store_res(0, 2)
                    store_res(0, 3)
            for i in range(NRING):
                sp.wait_ge(tile_out[i], 16 * ((NW - 1 - i) // NRING + 1))
            for k in range(CT):
                sp.dma_start(wout[:, k, :], w_out[0][k * P:(k + 1) * P, :]).then_inc(S["ld_wout"], 16)
            for kv in range(NKV):
                r0 = CONV + kv * GQ * HD
                sp.dma_start(wout[kv * HD:(kv + 1) * HD, CT:KD, :],
                             w_out[0][r0:r0 + GQ * HD, :].rearrange("(g d) n -> d g n", d=HD))\
                  .then_inc(S["ld_wout"], 16)

            def chunk(c, has_out, has_front):
                if has_front:
                    load_x(c + 1, 0)
                    load_x(c + 1, 1)
                if has_out:
                    load_res(c - 1, 0)
                    load_res(c - 1, 1)
                    for n in range(NRING, NW):
                        load_tile(c, n)
                if has_front:
                    for n in range(NRING):
                        load_tile(c + 1, n)
                for j in range(TT):
                    if has_front:
                        store_res(c + 1, j)
                        if j < 2:
                            load_x(c + 1, j + 2)
                    if has_out:
                        store_x2(c - 1, j)
                        if j < 2:
                            load_res(c - 1, j + 2)
                if has_out:
                    wait_apart(sp, x2_out[0], 32 * c)
                    wait_apart(sp, x2_out[1], 32 * c)
                    wait_apart(sp, S["x2tr_done"], 8 * c)

            chunk(0, False, True)
            with sp.Fori(1, NCH - 1) as c:
                chunk(c, True, True)
            chunk(NCH - 1, True, False)
            def load_w1(e, s):
                sp.dma_start(we[s][0], at(w1[0], e).rearrange("(k p) n -> p k n", p=P)).then_inc(w1_in[s], 16)

            def load_w3(e, s):
                sp.dma_start(we[s][1], at(w3[0], e).rearrange("(k p) n -> p k n", p=P)).then_inc(w3_in[s], 16)

            def load_w2(e, s):
                sp.dma_start(we[s][2], at(w2[0], e).rearrange("(k p) n -> p k n", p=P)).then_inc(w2_in[s], 16)

            sp.wait_ge(S["v_done"], NCH)
            load_w1(0, 0)
            load_w3(0, 0)
            load_w2(0, 0)
            c = NCH - 1
            load_res(c, 0)
            load_res(c, 1)
            for j in range(TT):
                store_x2(c, j)
                if j < 2:
                    load_res(c, j + 2)
            sp.wait_ge(S["o_done"], 8 * NCH)
            for s in range(2):
                sp.wait_ge(x2_out[s], 16 * NT // 2)
            sp.wait_ge(S["x2tr_done"], 2 * NT)
            load_w1(1, 1)
            load_w3(1, 1)
            load_w2(1, 1)
            sp.wait_ge(S["r_blk"], 1)
            with sp.Fori(1, NE // 2) as i:
                for s in range(2):
                    nb = sp.value_load(blk_i[0:1, bass.ds(2 * i - 2 + s, 1)], min_val=1, max_val=NT)
                    g0 = sp.value_load(blk_i[0:1, bass.ds(NE + 2 * i - 2 + s, 1)], min_val=0, max_val=MAXB)
                    sp.wait_ge(S["u1_done"], g0 + nb)
                    load_w1(2 * i + s, s)
                    sp.wait_ge(S["up_done"], (g0 + nb) * 2)
                    load_w3(2 * i + s, s)
                    sp.wait_ge(S["dn_done"], g0 + nb)
                    load_w2(2 * i + s, s)
            sp.wait_ge(S["dn_done"], sp.value_load(blk_i[0:1, 3 * NE:3 * NE + 1], min_val=1, max_val=MAXB))
            sp.dma_start(lnf[:, 0, :], row(ln_ffn_g[0])).then_inc(S["ld_lnf"], 16)
            sp.dma_start(lnf[:, 1, :], row(ln_ffn_b[0])).then_inc(S["ld_lnf"], 16)
            for s in range(NY):
                sp.dma_start(x2r[:, s, :], x2_t[s]).then_inc(x2r_in[s], 16)
            with sp.Fori(0, NT // NY - 1) as i:
                for s in range(NY):
                    sp.wait_ge(S["f_done"], NY * i + s + 1)
                    sp.dma_start(at(out_d, NY * i + s), x2r[:, s, :]).then_inc(f_out[s], 16)
                    if s:
                        sp.wait_ge(f_out[s - 1], 16 * (i + 1))
                        sp.dma_start(x2r[:, s - 1, :], at(x2_t, NY * i + NY + s - 1)).then_inc(x2r_in[s - 1], 16)
                sp.wait_ge(f_out[NY - 1], 16 * (i + 1))
                sp.dma_start(x2r[:, NY - 1, :], at(x2_t, NY * i + 2 * NY - 1)).then_inc(x2r_in[NY - 1], 16)
            for s in range(NY):
                sp.wait_ge(S["f_done"], NT - NY + s + 1)
                sp.dma_start(out_d[NT - NY + s], x2r[:, s, :]).then_inc(f_out[s], 16)
            for s in range(NY):
                sp.wait_ge(f_out[s], 16 * NT // NY)

        @block.gpsimd
        def _(pool):
            pool.memset(ident[:, :], 0.0).then_inc(S["c_ident"], 1)
            pool.memset(tri[:, :], 1.0).then_inc(S["c_tri"], 1)
            pool.memset(ones[:, :], 1.0).then_inc(S["c_ones"], 1)
            pool.memset(cmean[:, :], 1.0 / CONV).then_inc(S["c_ones"], 1)
            pool.memset(mhalf[:, :], -0.5).then_inc(S["c_ones"], 1)
            pool.memset(u[:, :, 0:HALO], 0.0).then_inc(S["c_halo"], 1)
            pool.memset(kT[:, :, :], 0.0).then_inc(S["c_halo"], 1)
            pool.wait_ge(S["c_ident"], 1)
            pool.affine_select(out=ident[:, :], in_=ident[:, :], compare_op=ALU.not_equal, fill=1.0,
                               base=0, pattern=[[-1, P]], channel_multiplier=1).then_inc(S["c_ident"], 1)
            pool.wait_ge(S["c_tri"], 1)
            pool.affine_select(out=tri[:, :], in_=tri[:, :], compare_op=ALU.is_gt, fill=0.0,
                               base=0, pattern=[[1, P]], channel_multiplier=-1).then_inc(S["c_tri"], 1)
            pool.iota(rev[:, :], pattern=[[-1, EG]], base=EG, channel_multiplier=0,
                      allow_small_or_imprecise_dtypes=True).then_inc(S["c_tri"], 1)
            pool.iota(thr[:, :], pattern=[[P, NT - 1]], base=P, channel_multiplier=0,
                      allow_small_or_imprecise_dtypes=True).then_inc(S["c_tri"], 1)
            pool.wait_ge(S["ld_small"], 16 * NSMALL)
            pool.wait_ge(S["c_fold"], 2)

            def rstd(var_sem, rs_sem, n, k):
                pool.wait_ge(S[var_sem], n + 1)
                pool.tensor_tensor(rs[:, k:k + 1], ve[:, k:k + 1], mhalf[:, 0:1], ALU.pow).then_inc(S[rs_sem], 1)

            def residual(c, j):
                n = 4 * c + j
                pool.wait_ge(S["ln1_done"], n + 1)
                if not (isinstance(n, int) and n == 0):
                    pool.wait_ge(S["xb_out"], 16 * n)
                pool.tensor_tensor(xb[:, :], xt[:, j % 2, :], ag_b[:, :], ALU.mult).then_inc(S["xb_st"], 1)
                pool.wait_ge(S["xb_st"], n + 1)
                pool.tensor_tensor(xb[:, :], xb[:, :], ab_b[:, :], ALU.add).then_inc(S["xb_ready"], 1)

            def front(c, j):
                rstd("ln1_var", "ln1_rs", 4 * c + j, 0)
                residual(c, j)

            for j in range(TT):
                front(0, j)

            def chunk(c, has_out, has_front):
                if has_front:
                    front(c + 1, 0)
                for a in range(AS):
                    if a == 2:
                        pool.wait_ge(S["cv_ready"], c + 1)
                        pool.tensor_tensor(cpw[:, :], cve[:, :], mhalf[:, :].broadcast_to([P, TT]), ALU.pow)\
                            .then_inc(S["cpw_ready"], 1)
                    if a % 2 and a < 6 and has_front:
                        front(c + 1, (a + 1) // 2)
                    if a % 2 == 0 and a and has_out:
                        rstd("ln2_var", "ln2_rs", 4 * (c - 1) + a // 2 - 1, 1)
                if has_out:
                    rstd("ln2_var", "ln2_rs", 4 * (c - 1) + 3, 1)

            chunk(0, False, True)
            with pool.Fori(1, NCH - 1) as c:
                chunk(c, True, True)
            chunk(NCH - 1, True, False)
            for j in range(TT):
                rstd("ln2_var", "ln2_rs", 4 * (NCH - 1) + j, 1)

            pool.wait_ge(S["xb_out"], 16 * NT)
            pool.iota(r_iota, pattern=[[1, P]], base=0, channel_multiplier=0,
                      allow_small_or_imprecise_dtypes=True).then_inc(S["r_iota"], 1)
            pool.iota(r_tok, pattern=[[P, NT]], base=0, channel_multiplier=1,
                      allow_small_or_imprecise_dtypes=True).then_inc(S["r_iota"], 1)
            pool.wait_ge(S["r_iota"], 2)
            pool.wait_ge(S["r_place"], 2)
            pool.tensor_tensor(r_ohb[:, 1], r_ohb[:, 1], r_tok.unsqueeze(2).broadcast_to([P, NT, MAXB]), ALU.mult)\
                .then_inc(S["r_ohp"], 1)
            pool.wait_ge(S["r_tab"], 1)
            for s in range(2):
                pool.wait_ge(x2_out[s], 16 * NT // 2)

            def gather(g):
                if not isinstance(g, int):
                    g = nc.s_assert_within(g, 2, MAXB + 1, skip_runtime_bounds_check_because=
                                           "there are at most MAXB blocks, and two gathers run ahead")
                pool.tensor_copy(idx[:, :], tab[:, bass.ds(g, 1)]).then_inc(S["e_idx"], 1)
                wait_apart(pool, S["etr_done"], g * 2 + 2)
                wait_apart(pool, S["e_idx"], g + 1)
                pool.indirect_dma_start(xg, None, x2_d, bass.IndirectOffsetOnAxis(ap=idx[:, :], axis=0))\
                    .then_inc(S["e_xg"], 16)
                wait_apart(pool, S["e_xg"], g * 16 + 16)

            gather(0)
            gather(1)
            with pool.Fori(0, NE // 2) as i:
                for s in range(2):
                    e = 2 * i + s
                    nb, g0, s0 = expert(pool, e)
                    for q in range(KE // 2):
                        pool.wait_ge(S["w2_hi"], KE * e + q + 1)
                        pool.tensor_tensor(wl[s][2][:, q, :], we[s][2][:, q, :], f32(wh2[:, q, :]), ALU.subtract)\
                            .then_inc(S["w2_lo"], 1)
                    with pool.Fori(0, nb) as b:
                        gather(g0 + b + 2)
            nall = pool.value_load(blk_i[0:1, 3 * NE:3 * NE + 1], min_val=1, max_val=MAXB)
            wait_apart(pool, S["ys_out"], nall * 16 + 16)

            def rows(t, s):
                pool.tensor_copy(idy[:, s, :], pos_u[:, :, bass.ds(t, 1)].rearrange("p k a -> p (k a)"))\
                    .then_inc(S["y_idx"], 1)
                wait_apart(pool, S["y_idx"], t + 1)
                for k, y in enumerate((ya, yb)):
                    pool.indirect_dma_start(y[:, s, :], None, ys_d[0:NS, :],
                                            bass.IndirectOffsetOnAxis(ap=idy[:, s, k:k + 1], axis=0))\
                        .then_inc(y_in[s], 16)

            def rstd4(t, s):
                pool.wait_ge(S["f_var"], t + 1)
                pool.tensor_tensor(rs4[:, s:s + 1], ve4[:, s:s + 1], mhalf[:, 0:1], ALU.pow)\
                    .then_inc(S["f_pow"], 1)
                pool.wait_ge(S["f_pow"], t + 1)
                pool.tensor_tensor(nr[:, s:s + 1], nm[:, s:s + 1], rs4[:, s:s + 1], ALU.mult)\
                    .then_inc(S["f_rs"], 1)

            def shift4(t, s):
                pool.wait_ge(S["f_g"], t + 1)
                pool.tensor_tensor(x2r[:, s, :], x2r[:, s, :], lnf[:, 1, :], ALU.add).then_inc(S["f_done"], 1)

            pool.wait_ge(S["r_idx"], 1)
            wait_apart(pool, S["ld_lnf"], 32)
            for s in range(NY):
                rows(s, s)
            with pool.Fori(0, NT // NY - 1) as i:
                for s in range(NY):
                    rstd4(NY * i + s, s)
                    rows(NY * i + NY + s, s)
                    if s:
                        shift4(NY * i + s - 1, s - 1)
                shift4(NY * i + NY - 1, NY - 1)
            for s in range(NY):
                rstd4(NT - NY + s, s)
                if s:
                    shift4(NT - NY + s - 1, s - 1)
            shift4(NT - 1, NY - 1)

        @block.tensor
        def _(pe):
            def x_transposes(c, j, tp_free):
                pe.wait_ge(S["ln1_done"], 4 * c + j + 1)
                tp_free()
                for h in range(2):
                    for k in range(4):
                        m = pe.transpose(TP[h][:, k * P:(k + 1) * P],
                                         xt[:, j % 2, (4 * h + k) * P:(4 * h + k + 1) * P], ident[:, :])
                    m.then_inc(S["xtr_done"], 1)

            def tile(c, n):
                if isinstance(c, int) and c == 0:
                    pe.wait_ge(S["w_rest"], n + 1)
                else:
                    loads = (NW - 1 - n % NRING) // NRING + 1
                    pe.wait_ge(ring_in[n % NRING], 16 * (loads * (c - 1) + n // NRING + 1))
                return ring[n % NRING]

            def project(c, dst, n):
                w = tile(c, n)
                for k in range(KD):
                    for j, (a, b_) in enumerate(((k, xTh), (k, xTl), (KD + k, xTh))):
                        m = pe.matmul(dst, w[:, a, :], b_[:, k, :], start=(k == 0 and j == 0),
                                      stop=(k == KD - 1 and j == 2))
                return m

            def projections(c):
                pe.wait_ge(S["xT_ready"], 8 * (c + 1))
                for ct in range(CT):
                    if ct >= 2:
                        pe.wait_ge(S["u_ready"], 4 * c + ct - 1)
                    project(c, PR[2 * (ct % 2) + 1][:, :], 2 * ct).then_inc(S["gate_done"], 1)
                    project(c, PR[2 * (ct % 2)][:, :], 2 * ct + 1).then_inc(S["a_done"], 1)
                for g in range(GQ):
                    pe.wait_ge(S["u_ready"], 4 * c + 3 + g // 2)
                    project(c, PR[g][:, :], 2 * CT + g).then_inc(S["q_done"], 1)
                pe.wait_ge(S["qk_ready"], 5 * c + 1)
                project(c, PR[0][:, :], NW - 2).then_inc(S["q_done"], 1)
                pe.wait_ge(S["qk_ready"], 5 * c + 2)
                w = tile(c, NW - 1)
                for j in range(TT):
                    cols_j = slice(j * P, (j + 1) * P)
                    for k in range(KD):
                        for i, (a, b_) in enumerate(((xTh, k), (xTh, KD + k), (xTl, k))):
                            m = pe.matmul(PR[1][:, cols_j], a[:, k, cols_j], w[:, b_, :],
                                          start=(k == 0 and i == 0), stop=(k == KD - 1 and i == 2))
                m.then_inc(S["v_done"], 1)

            def scores(c, a):
                if a == 0:
                    pe.wait_ge(S["qk_ready"], 5 * (c + 1))
                cur = AC + a * AC
                first = isinstance(c, int) and c == 0 and a == 0
                for kv in range(NKV):
                    for gp in range(2):
                        q = qT[:, a, gp * P:(gp + 1) * P]
                        o = (kv * 2 + gp) * P
                        if a % 2:
                            m = pe.matmul(SB[:, o:o + P], q, kT[:, kv, cur - AC:cur + AC], start=True, stop=True)
                        else:
                            m = pe.matmul(SB[:, o:o + AC], q, kT[:, kv, cur:cur + AC], start=True, stop=True)
                            if not first:
                                m = pe.matmul(SB[:, o + AC:o + P], q, kT[:, kv, cur - AC:cur], start=True, stop=True)
                m.then_inc(S["s_done"], 1)

            def p_transposes(c, a):
                pe.wait_ge(S["pn_ready"], 8 * c + a + 1)
                if not (isinstance(c, int) and c == 0 and a == 0):
                    pe.wait_ge(S["o_ready"], 8 * c + a)
                for i in range(GQ):
                    m = pe.transpose(OB[:, i * P:(i + 1) * P], pr[:, i, :], ident[:, :])
                m.then_inc(S["ptr_done"], 1)

            def attend(c, a):
                if a == 0:
                    if isinstance(c, int) and c == 0:
                        pe.wait_ge(S["c_vhalo"], 1)
                    pe.wait_ge(S["v_ready"], c + 1)
                pe.wait_ge(S["pT_ready"], 8 * c + a + 1)
                v = vO[:, a // 2, :] if a % 2 else vE[:, a // 2, :]
                for kv in range(NKV):
                    m = pe.matmul(OB[kv * HD:(kv + 1) * HD, 0:2 * P], v[:, kv * HD:(kv + 1) * HD],
                                  pT[:, 2 * kv:2 * kv + 2, :], start=True, stop=True)
                m.then_inc(S["pv_done"], 1)

            def out_half(c, i):
                j, n = i // 2, i % 2
                for k in range(KD):
                    mt = mixc if k < CT else mixa
                    m = pe.matmul(PR[i % 4][:, :], mt[:, k % CT, j * P:(j + 1) * P],
                                  wout[:, k, n * 512:(n + 1) * 512], start=(k == 0), stop=(k == KD - 1))
                m.then_inc(S["o_done"], 1)

            def x2_transposes(c, j):
                pe.wait_ge(S["ln2_done"], 4 * c + j + 1)
                for h in range(2):
                    for k in range(4):
                        m = pe.transpose(TP[h][:, k * P:(k + 1) * P],
                                         rt[:, j % 2, (4 * h + k) * P:(4 * h + k + 1) * P], ident[:, :])
                    m.then_inc(S["x2tr_done"], 1)

            def router(c, j):
                pe.wait_ge(S["x2T_ready"], 2 * (4 * c + j) + 2)
                for k in range(KD):
                    m = pe.matmul(TP[0][:, 0:NR], x2T[:, k, :], wr[:, k, :], start=(k == 0), stop=(k == KD - 1))
                m.then_inc(S["lg_done"], 1)

            def chunk(c, has_out, has_front):
                projections(c)
                if has_out:
                    pe.wait_ge(S["mixc_ready"], 4 * c)
                    pe.wait_ge(S["o_ready"], 8 * c)
                    pe.wait_ge(S["qk_ready"], 5 * (c + 1))
                    out_half(c - 1, 0)
                for a in range(AS):
                    scores(c, a)
                    if a:
                        attend(c, a - 1)
                    if a == 2:
                        if has_front:
                            pe.wait_ge(S["xT_ready"], 8 * (c + 1) + 2)
                        pe.wait_ge(S["conv_st"], CW * CT * (c + 1))
                        for ct in range(CT):
                            m = pe.matmul(TP[0][:, :], cmean[:, :], acc[:, ct, :], start=(ct == 0),
                                          stop=(ct == CT - 1))
                        m.then_inc(S["mean_done"], 1)
                    if a == 3:
                        if has_front:
                            pe.wait_ge(S["xT_ready"], 8 * (c + 1) + 4)
                        pe.wait_ge(S["dg_ready"], c + 1)
                        pe.matmul(TP[1][:, :], ones[:, :], crs[:, :], start=True, stop=True).then_inc(S["bc_done"], 1)
                    if a > 3 and a % 2 and has_out:
                        if has_front:
                            pe.wait_ge(S["xT_ready"], 8 * (c + 1) + 2 * ((a - 1) // 2) + 2)
                        else:
                            pe.wait_ge(S["lg_ready"], 4 * (c - 1) + (a - 3) // 2)
                        x2_transposes(c - 1, (a - 3) // 2)
                    if has_out and a < AS - 1:
                        if a == 0:
                            pe.wait_ge(S["v_ready"], c + 1)
                        if a >= 3:
                            pe.wait_ge(S["o_evac"], 8 * (c - 1) + a - 2)
                        out_half(c - 1, a + 1)
                    if a == 2:
                        pe.wait_ge(S["uc_ready"], 4 * (c + 1))
                        for ct in range(CT):
                            pe.wait_ge(S["sq_ready"], 4 * c + ct + 1)
                            for j in range(TT):
                                o = ct * TT + j
                                m = pe.matmul(TP[0][:, o:o + 1], sg[:, ct % 2, j * P:(j + 1) * P], cmean[:, 0:1],
                                              start=True, stop=True)
                            m.then_inc(S["var_done"], 1)
                    if a == 3 and has_out:
                        pe.wait_ge(S["crs_ready"], c + 1)
                        x2_transposes(c - 1, 0)
                    if a >= 3 and a % 2 and has_out:
                        router(c - 1, (a - 3) // 2)
                    if a % 2 == 0 and has_front:
                        def tp_free():
                            if a == 0:
                                return
                            elif a == 2:
                                pe.wait_ge(S["cv_ready"], c + 1)
                                pe.wait_ge(S["xT_ready"], 8 * (c + 1) + 2)
                            elif has_out:
                                pe.wait_ge(S["lg_ready"], 4 * (c - 1) + a // 2 - 1)
                            else:
                                if a == 4:
                                    pe.wait_ge(S["crs_ready"], c + 1)
                                pe.wait_ge(S["xT_ready"], 8 * (c + 1) + a)
                        x_transposes(c + 1, a // 2, tp_free)
                    p_transposes(c, a)
                attend(c, AS - 1)
                if has_out:
                    if has_front:
                        pe.wait_ge(S["xT_ready"], 8 * (c + 2))
                    pe.wait_ge(S["lg_ready"], 4 * (c - 1) + 3)
                    x2_transposes(c - 1, 3)
                    router(c - 1, 3)
                    pe.wait_ge(S["lg_ready"], 4 * c)

            pe.wait_ge(S["c_ident"], 2)
            pe.wait_ge(S["c_ones"], 3)
            pe.wait_ge(S["ld_small"], 16 * NSMALL)
            pe.transpose(OB[:, 0:NV], vrow, ident[0:NV, 0:NV])
            for ct in range(CT):
                m = pe.transpose(OB[:, NV + ct * CW:NV + (ct + 1) * CW], wrow[:, ct * P:(ct + 1) * P],
                                 ident[0:CW, 0:CW])
            m.then_inc(S["cols_tr"], 1)
            for j in range(TT):
                x_transposes(0, j, (lambda: pe.wait_ge(S["xT_ready"], 2 * j)) if j else (lambda: None))
            chunk(0, False, True)
            pe.wait_ge(S["ld_wout"], 16 * (CT + NKV))
            with pe.Fori(1, NCH - 1) as c:
                chunk(c, True, True)
            c = NCH - 1
            chunk(c, True, False)
            pe.wait_ge(S["mixc_ready"], 4 * NCH)
            pe.wait_ge(S["o_ready"], 8 * NCH)
            for i in range(8):
                pe.wait_ge(S["o_evac"], 8 * c + i - 3 if i >= 4 else 8 * c)
                out_half(c, i)
                if i in (3, 5, 7):
                    j = (i - 3) // 2
                    if j:
                        pe.wait_ge(S["lg_ready"], 4 * c + j)
                    x2_transposes(c, j)
                    router(c, j)
            pe.wait_ge(S["lg_ready"], 4 * c + 3)
            x2_transposes(c, 3)
            router(c, 3)

            pe.wait_ge(S["c_tri"], 2)
            pe.wait_ge(S["r_hot"], 1)
            hot = mixc[:, 0, :]
            pe.matmul(PR[0][:, :], tri[:, :], hot, start=True, stop=True).then_inc(S["rk_done"], 1)
            pe.matmul(PR[1][:, :], ones[:, :], hot, start=True, stop=True).then_inc(S["rk_done"], 1)
            for k in range(2):
                pe.wait_ge(S["r_ohd"], k + 1)
                if k:
                    pe.wait_ge(S["r_ohp"], 1)
                for t in range(NT):
                    m = pe.matmul(PR[2][:, 0:MAXB], r_ohl[:, k, t, :], r_ohb[:, k, t, :],
                                  start=(k == 0 and t == 0), stop=(k == 1 and t == NT - 1))
            m.then_inc(S["r_tabd"], 1)

            def e_transposes(g):
                pe.wait_ge(S["e_xg"], g * 16 + 16)
                for h in range(2):
                    for k in range(4):
                        m = pe.transpose(TP[h][:, k * P:(k + 1) * P], xg[:, (4 * h + k) * P:(4 * h + k + 1) * P],
                                         ident[:, :])
                    m.then_inc(S["etr_done"], 1)

            pe.wait_ge(S["r_blk"], 1)
            pe.wait_ge(S["r_tab"], 1)
            pe.sem_inc(S["etr_done"], 2)
            pe.wait_ge(S["lg_ready"], 4 * NCH)
            e_transposes(0)
            U1, U3, YB = PR[0], (PR[1], SB), PR[2:4]
            last = [None]

            def h_transposes(g, h):
                pe.wait_ge(S["hm_ready"], g * 2 + h + 1)
                for f in range(2):
                    m = pe.transpose(HT[h][:, f * P:(f + 1) * P], sl[:, (2 * h + f) * P:(2 * h + f + 1) * P],
                                     ident[:, :])
                m.then_inc(S["htr_done"], 1)

            def split(dst, n, lhs, rhs, first=True, final=True):
                for k in range(n):
                    (lh, ll), (rh, rl) = lhs(k), rhs(k)
                    for j, (a, b_) in enumerate(((lh, rh), (lh, rl), (ll, rh))):
                        last[0] = pe.matmul(dst, a, b_, start=(first and k == 0 and j == 0),
                                            stop=(final and k == n - 1 and j == 2))

            with pe.Fori(0, NE // 2) as i:
                for s in range(2):
                    nb = pe.value_load(blk_i[0:1, bass.ds(2 * i + s, 1)], min_val=1, max_val=NT)
                    g0 = pe.value_load(blk_i[0:1, bass.ds(NE + 2 * i + s, 1)], min_val=0, max_val=MAXB)
                    e = 2 * i + s
                    with pe.Fori(0, nb) as b:
                        g = g0 + b
                        pe.wait_ge(S["xeh_ready"], g * 2 + 2)
                        pe.wait_ge(S["xel_ready"], g * 2 + 2)
                        for dst, w, n0, n1, done in ((U1, 0, 0, DE, "u1_done"), (U3[0], 1, 0, DE // 2, "up_done"),
                                                     (U3[1], 1, DE // 2, DE, "up_done")):
                            if n0 == 0:
                                pe.wait_ge(S["w3_lo"] if w else S["w1_lo"], 4 * e + 4)
                            split(dst[:, 0:n1 - n0], KD, lambda k: (xeh[:, k, :], xel[:, k, :]),
                                  lambda k: (wh13[s][w][:, k, n0:n1], wl[s][w][:, k, n0:n1]))
                            last[0].then_inc(S[done], 1)
                        h_transposes(g, 0)
                        e_transposes(g + 1)
                        h_transposes(g, 1)
                        pe.wait_ge(S["w2_lo"], KE // 2 * (e + 1))
                        pe.wait_ge(S["w2_lo2"], KE // 2 * (e + 1))
                        pe.wait_ge(S["ya_free"], g + 1)
                        pe.wait_ge(S["yb_free"], g + 1)
                        for f in range(KE):
                            if f % 2 == 0:
                                pe.wait_ge(S["h_ready"], g * 2 + 1 + f // 2)
                            for n in range(2):
                                c0 = n * 512
                                split(YB[n][:, :], 1, lambda k: (heh[:, f, :], hel[:, f, :]),
                                      lambda k: (wh2[:, f, c0:c0 + 512], wl[s][2][:, f, c0:c0 + 512]),
                                      first=(f == 0), final=(f == KE - 1))
                        last[0].then_inc(S["dn_done"], 1)

        @block.scalar
        def _(act):
            def xT_evac(c, j):
                if j == 0 and not (isinstance(c, int) and c == 0):
                    act.wait_ge(S["v_done"], c)
                for h in range(2):
                    act.wait_ge(S["xtr_done"], 2 * (4 * c + j) + h + 1)
                    for k in range(4):
                        kk = 4 * h + k
                        t = TP[h][:, k * P:(k + 1) * P]
                        m = act.activation(t, t, ACT.Identity, bias=lb_in[:, kk:kk + 1], scale=lg_in[:, kk:kk + 1])
                    m.then_inc(S["xt_gain"], 1)
                    act.wait_ge(S["xt_gain"], 2 * (4 * c + j) + h + 1)
                    act.copy(xTh[:, 4 * h:4 * h + 4, j * P:(j + 1) * P],
                             TP[h][:, :].rearrange("p (k n) -> p k n", k=4)).then_inc(S["xh_ready"], 1)

            def tile_high(n):
                act.wait_ge(raw_in[n % NRAW], 16 * raw_loads(n))
                if n >= NRING:
                    wait_used(act, 0, n - NRING)
                    act.wait_ge(tile_out[n % NRING], 16 * (n // NRING))
                act.copy(ring[n % NRING][:, 0:KD, :], raw[n % NRAW]).then_inc(S["w_hi"], 1)

            def x2T_evac(c, j):
                if not (isinstance(c, int) and c == 0) or j:
                    act.wait_ge(S["lg_done"], 4 * c + j)
                for h in range(2):
                    act.wait_ge(S["x2tr_done"], 2 * (4 * c + j) + h + 1)
                    act.copy(x2T[:, 4 * h:4 * h + 4, :], TP[h][:, :].rearrange("p (k n) -> p k n", k=4))\
                       .then_inc(S["x2T_ready"], 1)

            def logits_evac(c, j):
                act.wait_ge(S["lg_done"], 4 * c + j + 1)
                act.copy(logits[:, bass.ds(4 * c + j, 1), :].rearrange("p a n -> p (a n)"), TP[0][:, 0:NR])\
                   .then_inc(S["lg_ready"], 1)

            def chunk(c, has_out, has_front):
                for ct in range(CT):
                    act.wait_ge(S["gate_done"], 4 * c + ct + 1)
                    if ct >= 2:
                        act.wait_ge(S["u_ready"], 4 * c + ct - 1)
                    act.activation(sg[:, ct % 2, :], PR[2 * (ct % 2) + 1][:, :], ACT.Sigmoid,
                                   bias=b_ag[:, CT + ct:CT + ct + 1]).then_inc(S["sg_ready"], 1)
                    if not has_out:
                        tile_high(2 * ct + NRING)
                        tile_high(2 * ct + NRING + 1)
                for g in range(GQ + 1):
                    act.wait_ge(S["q_done"], 5 * c + g + 1)
                    if g < GQ:
                        act.activation(qT[:, :, g * AC:(g + 1) * AC],
                                       PR[g][:, :].rearrange("p (a n) -> p a n", a=AS), ACT.Identity,
                                       bias=b_q[:, g:g + 1])\
                           .then_inc(S["qk_ready"], 1)
                        if g == 0 and not has_out:
                            tile_high(NW - 1)
                    else:
                        if not (isinstance(c, int) and c == 0):
                            act.wait_ge(S["halo_kv"], 2 * c)
                        for kv in range(NKV):
                            r = slice(kv * HD, (kv + 1) * HD)
                            m = act.activation(kT[r, kv, AC:AC + T], PR[0][r, :], ACT.Identity, bias=b_k[r, 0:1])
                        m.then_inc(S["qk_ready"], 1)
                for a in range(AS):
                    act.wait_ge(S["sm_neg"], 8 * c + a + 1)
                    act.wait_ge(S["s_done"], 8 * c + a + 1)
                    if not (isinstance(c, int) and c == 0 and a == 0):
                        act.wait_ge(S["ptr_done"], 8 * c + a)
                    for i in range(GQ):
                        m = act.activation(pr[:, i, :], SB[:, i * P:(i + 1) * P], ACT.Exp, bias=negm[:, i:i + 1],
                                           scale=SCALE, accum_out=psum_[:, i:i + 1])
                    m.then_inc(S["p_ready"], 1)
                    act.activation(es[:, :], sk[:, :], ACT.Exp).then_inc(S["es_ready"], 1)
                    if a:
                        o_evac(c, a - 1)
                    if a == 2:
                        for ct in range(2):
                            act.wait_ge(S["uc_ready"], 4 * c + ct + 1)
                            act.activation(sg[:, ct, :], acc[:, ct, :], ACT.Square).then_inc(S["sq_ready"], 1)
                        for ct in range(2, CT):
                            act.wait_ge(S["uc_ready"], 4 * c + ct + 1)
                            act.wait_ge(S["var_done"], 4 * c + ct - 1)
                            act.activation(sg[:, ct % 2, :], acc[:, ct, :], ACT.Square).then_inc(S["sq_ready"], 1)
                    if a == 3:
                        act.wait_ge(S["bc_done"], c + 1)
                        act.copy(crs[:, :], TP[1][:, :]).then_inc(S["crs_ready"], 1)
                    if a >= 3 and a % 2 and has_out:
                        x2T_evac(c - 1, (a - 3) // 2)
                        logits_evac(c - 1, (a - 3) // 2)
                    if a % 2 == 0 and has_front:
                        xT_evac(c + 1, a // 2)
                    act.wait_ge(S["ptr_done"], 8 * c + a + 1)
                    act.copy(pT[:, :, :], OB[:, :].rearrange("p (i n) -> p i n", i=GQ)).then_inc(S["pT_ready"], 1)
                o_evac(c, AS - 1)
                act.copy(kT[:, :, 0:AC], kT[:, :, T:T + AC]).then_inc(S["halo_kv"], 1)
                act.copy(vE[HD:P, 0, :], vE[HD:P, TT, :]).then_inc(S["halo_kv"], 1)
                if has_out:
                    x2T_evac(c - 1, 3)
                    logits_evac(c - 1, 3)
                    act.wait_ge(S["o_done"], 8 * c)
                for ct in range(CT):
                    act.wait_ge(S["un_ready"], 4 * c + ct + 1)
                    act.activation(mixc[:, ct, :], acc[:, ct, :], ACT.Silu, bias=lcb[:, ct:ct + 1],
                                   scale=lcg[:, ct:ct + 1]).then_inc(S["mixc_ready"], 1)

            def o_evac(c, a):
                act.wait_ge(S["pv_done"], 8 * c + a + 1)
                act.copy(mixa[:, :, a * AC:(a + 1) * AC], OB[:, 0:2 * P].rearrange("p (g n) -> p g n", g=GQ))\
                   .then_inc(S["o_ready"], 1)

            act.wait_ge(S["ld_small"], 16 * NSMALL)
            act.wait_ge(S["c_halo"], 2)
            act.wait_ge(S["cols_tr"], 1)
            act.copy(cols[:, :], OB[:, 0:NV + CT * CW]).then_inc(S["cols_in"], 1)
            act.wait_ge(S["cols_in"], 1)
            for j in range(TT):
                for n in ((0, 1), (2, 3), (4,), ())[j]:
                    tile_high(n)
                xT_evac(0, j)
            chunk(0, False, True)
            with act.Fori(1, NCH - 1) as c:
                chunk(c, True, True)
            c = NCH - 1
            chunk(c, True, False)
            for j in range(TT):
                x2T_evac(c, j)
                logits_evac(c, j)
            act.wait_ge(S["rt_st"], RT_EXP_G)
            act.activation(r_eg, r_gd, ACT.Exp).then_inc(S["rk_exp"], 1)
            act.wait_ge(S["rt_st"], RT_EXP_E)
            act.activation(r_ee, r_ed, ACT.Exp).then_inc(S["rk_exp"], 1)
            act.sem_inc(S["ya_free"], 1)
            act.sem_inc(S["ys_out"], 16)
            act.wait_ge(S["r_blk"], 1)

            def xe_high(g):
                for h in range(2):
                    act.wait_ge(S["etr_done"], g * 2 + 3 + h)
                    act.copy(xeh[:, 4 * h:4 * h + 4, :], TP[h][:, :].rearrange("p (k n) -> p k n", k=4))\
                       .then_inc(S["xeh_ready"], 1)

            def w13_high(i, s, w, q0=0, q1=4):
                if q0 == 0:
                    act.wait_ge((w3_in if w else w1_in)[s], 16 * (i + 1))
                for q in range(q0, q1):
                    act.copy(wh13[s][w][:, 2 * q:2 * q + 2, :], we[s][w][:, 2 * q:2 * q + 2, :])\
                       .then_inc(S["w3_hi" if w else "w1_hi"], 1)

            act.wait_ge(S["r_tab"], 1)
            w13_high(0, 0, 0)
            w13_high(0, 0, 1)
            xe_high(0)

            def expert_act(i, s, has_next):
                e = 2 * i + s
                nb, g0, s0 = expert(act, e)

                def block_act(g, b, first):
                    if first and has_next:
                        w13_high(i + s, 1 - s, 0, 0, 2)
                    act.wait_ge(S["u1_done"], g + 1)
                    act.activation(sl, PR[0][:, :], ACT.Silu).then_inc(S["sl_ready"], 1)
                    if first and has_next:
                        w13_high(i + s, 1 - s, 0, 2, 4)
                    for h in range(2):
                        act.wait_ge(S["htr_done"], g * 2 + h + 1)
                        act.copy(heh[:, 2 * h:2 * h + 2, :], HT[h][:, 0:2 * P].rearrange("p (f n) -> p f n", f=2))\
                           .then_inc(S["heh_ready"], 1)
                    xe_high(g + 1)
                    if first and has_next:
                        w13_high(i + s, 1 - s, 1)
                    act.wait_ge(S["dn_done"], g + 1)
                    act.wait_ge(S["ys_out"], g * 16 + 16)
                    act.copy(ye[:, 0:512], PR[2][:, :]).then_inc(S["ya_free"], 1)
                    act.wait_ge(S["ya_free"], g + 2)
                    act.wait_ge(S["yb_free"], g + 2)
                    act.dma_start(ys_d[bass.ds(block_slot(s0, b), P), :], ye).then_inc(S["ys_out"], 16)

                act.wait_ge(w2_in[s], 16 * (i + 1))
                for q in range(KE):
                    act.copy(wh2[:, q, :], we[s][2][:, q, :]).then_inc(S["w2_hi"], 1)
                block_act(g0, 0, True)
                with act.If(nb > 1):
                    with act.Fori(1, nb) as b:
                        block_act(g0 + b, b, False)

            with act.Fori(0, NE // 2 - 1) as i:
                for s in range(2):
                    expert_act(i, s, True)
            for s in range(2):
                expert_act(NE // 2 - 1, s, s == 0)
            def norm4(t, s):
                act.wait_ge(S["f_rs"], t + 1)
                act.activation(x2r[:, s, :], x2r[:, s, :], ACT.Identity, bias=nr[:, s:s + 1], scale=rs4[:, s:s + 1])\
                   .then_inc(S["f_n"], 1)

            with act.Fori(0, NT // NY) as i:
                for s in range(NY):
                    t = NY * i + s
                    act.wait_ge(y_in[s], i * 32 + 32)
                    act.activation(ya[:, s, :], ya[:, s, :], ACT.Copy, scale=gate[:, 0, bass.ds(t, 1)])\
                       .then_inc(S["f_a"], 1)
                    if s:
                        norm4(t - 1, s - 1)
                norm4(NY * i + NY - 1, NY - 1)

        @block.vector
        def _(dve):
            def statistics(src, st_sem, per, n, k):
                for h in range(2):
                    dve.bn_stats(bst[:, k, h, :], src[:, h * 512:(h + 1) * 512]).then_inc(S[st_sem], 1)
                wait_apart(dve, S[st_sem], per * n + 2)
                dve.bn_aggr(mv[:, k, :], bst[:, k, :, :].rearrange("p h s -> p (h s)")).then_inc(S[st_sem], 1)
                dve.wait_ge(S[st_sem], per * n + 3)

            def ln1(c, j):
                n = 4 * c + j
                t = xt[:, j % 2, :]
                dve.wait_ge(x_in[j % 2], 16 * (2 * c + j // 2 + 1))
                statistics(t, "ln1_st", 3, n, 0)
                dve.tensor_scalar(ve[:, 0:1], mv[:, 0, 1:2], EPS, None, ALU.add).then_inc(S["ln1_var"], 1)
                dve.wait_ge(S["ln1_rs"], n + 1)
                dve.tensor_scalar(t, t, mv[:, 0, 0:1], rs[:, 0:1], ALU.subtract, ALU.mult).then_inc(S["ln1_done"], 1)

            def xT_rest(c, j):
                for h in range(2):
                    dve.wait_ge(S["xh_ready"], 2 * (4 * c + j) + h + 1)
                    cols_j = slice(j * P, (j + 1) * P)
                    dve.tensor_tensor(xTl[:, 4 * h:4 * h + 4, cols_j], TP[h][:, :].rearrange("p (k n) -> p k n", k=4),
                                      f32(xTh[:, 4 * h:4 * h + 4, cols_j]), ALU.subtract).then_inc(S["xT_ready"], 1)

            def tile_rest(n):
                dve.wait_ge(S["w_hi"], n + 1)
                w = ring[n % NRING]
                dve.tensor_tensor(w[:, KD:2 * KD, :], raw[n % NRAW], f32(w[:, 0:KD, :]), ALU.subtract)\
                   .then_inc(S["w_rest"], 1)

            def ln2(c, j):
                n = 4 * c + j
                t = rt[:, j % 2, :]
                dve.wait_ge(S["o_evac"], 2 * (n + 1))
                statistics(t, "ln2_st", 4, n, 1)
                dve.tensor_scalar(ve[:, 1:2], mv[:, 1, 1:2], EPS, None, ALU.add).then_inc(S["ln2_var"], 1)
                dve.scalar_tensor_tensor(t, t, mv[:, 1, 0:1], gm_b[:, :], ALU.subtract, ALU.mult)\
                   .then_inc(S["ln2_st"], 1)
                dve.wait_ge(S["ln2_st"], 4 * n + 4)
                dve.wait_ge(S["ln2_rs"], n + 1)
                dve.scalar_tensor_tensor(t, t, rs[:, 1:2], bm_b[:, :], ALU.mult, ALU.add).then_inc(S["ln2_done"], 1)

            def glu(c, ct):
                dve.wait_ge(S["sg_ready"], 4 * c + ct + 1)
                dve.wait_ge(S["a_done"], 4 * c + ct + 1)
                if not (isinstance(c, int) and c == 0):
                    dve.wait_ge(S["halo_u"], c)
                dve.scalar_tensor_tensor(u[:, ct, HALO:HALO + T], PR[2 * (ct % 2)][:, :], b_ag[:, ct:ct + 1],
                                         sg[:, ct % 2, :], ALU.add, ALU.mult).then_inc(S["u_ready"], 1)

            LEAD = 12
            TAPS = []
            at_tap = [LEAD, 0, 0, 0]
            TAPS += [(0, k) for k in range(LEAD)]
            for ct in range(CT):
                while at_tap[ct] < CW:
                    TAPS.append((ct, at_tap[ct]))
                    at_tap[ct] += 1
                    if ct + 1 < CT:
                        TAPS.append((ct + 1, at_tap[ct + 1]))
                        at_tap[ct + 1] += 1

            def conv_taps(c, i0, i1):
                for i in range(i0, i1):
                    ct, k = TAPS[i]
                    if i == 0 and not (isinstance(c, int) and c == 0):
                        dve.wait_ge(S["mixc_ready"], 4 * c)
                    w = wdw[:, ct, k:k + 1]
                    if k == 0:
                        dve.wait_ge(S["u_ready"], 4 * c + ct + 1)
                        m = dve.tensor_scalar(acc[:, ct, :], u[:, ct, 0:T], w, None, ALU.mult)
                    else:
                        dve.wait_ge(S["conv_st"], CW * CT * c + TAPS.index((ct, k - 1)) + 1)
                        m = dve.scalar_tensor_tensor(acc[:, ct, :], u[:, ct, k:k + T], w, acc[:, ct, :],
                                                     ALU.mult, ALU.add)
                    m.then_inc(S["conv_st"], 1)

            def v_evac(c):
                dve.wait_ge(S["v_done"], c + 1)
                if not (isinstance(c, int) and c == 0):
                    dve.wait_ge(S["halo_kv"], 2 * c)
                src = PR[1][:, :].rearrange("p (j n) -> p j n", j=TT)
                bias = bv_b[:, :].unsqueeze(1).broadcast_to([P, TT, P])
                dve.tensor_tensor(vO[:, :, :], src, bias, ALU.add)
                dve.tensor_tensor(vE[0:HD, 0:TT, :], src[0:HD], bias[0:HD], ALU.add)
                dve.tensor_tensor(vE[HD:P, 1:TT + 1, :], src[HD:P], bias[HD:P], ALU.add).then_inc(S["v_ready"], 1)

            def softmax_max(c, a):
                n = 8 * c + a
                dve.wait_ge(S["s_done"], n + 1)
                s3 = SB[:, :].rearrange("p (i n) -> p i n", i=GQ)
                if isinstance(c, int) and n == 0:
                    dve.memset(s3[:, :, AC:P], NEG).then_inc(S["sm0"], 1)
                    dve.wait_ge(S["sm0"], 1)
                dve.tensor_reduce(mx[:, :], s3, AXX, ALU.max).then_inc(S["sm_st"], 1)
                dve.wait_ge(S["sm_st"], 4 * n + 1)
                dve.scalar_tensor_tensor(mm_[:, :], mx[:, :], SCALE, sink_b[:, :], ALU.mult, ALU.max)\
                   .then_inc(S["sm_st"], 1)
                dve.wait_ge(S["sm_st"], 4 * n + 2)
                dve.tensor_tensor(sk[:, :], sink_b[:, :], mm_[:, :], ALU.subtract)
                dve.tensor_scalar(negm[:, :], mm_[:, :], -1.0, None, ALU.mult).then_inc(S["sm_neg"], 1)

            def softmax_norm(c, a):
                n = 8 * c + a
                dve.wait_ge(S["p_ready"], n + 1)
                dve.wait_ge(S["es_ready"], n + 1)
                dve.tensor_tensor(den[:, :], psum_[:, :], es[:, :], ALU.add).then_inc(S["sm_st"], 1)
                dve.wait_ge(S["sm_st"], 4 * n + 3)
                dve.reciprocal(rden[:, :], den[:, :]).then_inc(S["sm_st"], 1)
                dve.wait_ge(S["sm_st"], 4 * n + 4)
                dve.tensor_tensor(pr[:, :, :], pr[:, :, :], rden[:, :].unsqueeze(2).broadcast_to([P, GQ, P]),
                                  ALU.mult).then_inc(S["pn_ready"], 1)

            def out_evac(c, i):
                j, n = i // 2, i % 2
                dve.wait_ge(S["o_done"], 8 * c + i + 1)
                dve.wait_ge(r_in[j % 2], 16 * (2 * c + j // 2 + 1))
                t = rt[:, j % 2, n * 512:(n + 1) * 512]
                dve.tensor_tensor(t, PR[i % 4][:, :], t, ALU.add).then_inc(S["o_evac"], 1)

            def chunk(c, has_out, has_front):
                def glu_and_tiles(ct):
                    glu(c, ct)
                    if not has_out:
                        tile_rest(2 * ct + NRING)
                        tile_rest(2 * ct + NRING + 1)

                glu_and_tiles(0)
                conv_taps(c, 0, LEAD)
                glu_and_tiles(1)
                conv_taps(c, LEAD, 27)
                glu_and_tiles(2)
                conv_taps(c, 27, 42)
                glu_and_tiles(3)
                if not has_out:
                    tile_rest(NW - 1)
                conv_taps(c, 42, 94)
                v_evac(c)
                if has_front:
                    ln1(c + 1, 0)
                for a in range(AS):
                    softmax_max(c, a)
                    if a == 0:
                        conv_taps(c, 94, 94)
                    if a == 1:
                        conv_taps(c, 108, 112)
                    if a == 2:
                        dve.wait_ge(S["mean_done"], c + 1)
                        for ct in range(CT):
                            dve.tensor_tensor(acc[:, ct, :], acc[:, ct, :], TP[0][:, :], ALU.subtract)\
                               .then_inc(S["uc_ready"], 1)
                    if has_out:
                        out_evac(c - 1, a)
                    softmax_norm(c, a)
                    if a == 0:
                        conv_taps(c, 94, 108)
                    if a == 1:
                        conv_taps(c, 112, CW * CT)
                        dve.wait_ge(S["conv_st"], CW * CT * (c + 1))
                        dve.tensor_copy(u[:, :, 0:HALO], u[:, :, T:T + HALO]).then_inc(S["halo_u"], 1)
                    if a == 3:
                        dve.wait_ge(S["crs_ready"], c + 1)
                        for ct in range(CT):
                            dve.tensor_tensor(acc[:, ct, :], acc[:, ct, :], crs[:, :], ALU.mult)\
                               .then_inc(S["un_ready"], 1)
                    if a % 2 and a < 6 and has_front:
                        ln1(c + 1, (a + 1) // 2)
                    if a == 2:
                        dve.wait_ge(S["var_done"], 4 * (c + 1))
                        dve.tensor_reduce(cve[:, :], TP[0][:, 0:CT * TT].rearrange("p (a j) -> p j a", a=CT), AXX,
                                          ALU.add).then_inc(S["cv_sum"], 1)
                        dve.wait_ge(S["cv_sum"], c + 1)
                        dve.tensor_scalar(cve[:, :], cve[:, :], EPS, None, ALU.add).then_inc(S["cv_ready"], 1)
                    if a % 2 == 0 and a and has_out:
                        ln2(c - 1, a // 2 - 1)
                    if a == 2:
                        dve.wait_ge(S["cpw_ready"], c + 1)
                        dve.tensor_tensor(crs[:, :].rearrange("p (j n) -> p j n", j=TT),
                                          ident[:, :].unsqueeze(1).broadcast_to([P, TT, P]),
                                          cpw[:, :].unsqueeze(2).broadcast_to([P, TT, P]), ALU.mult)\
                           .then_inc(S["dg_ready"], 1)
                    if a % 2 == 0 and has_front:
                        xT_rest(c + 1, a // 2)
                if has_out:
                    ln2(c - 1, 3)

            dve.memset(vE[HD:P, 0, :], 0.0).then_inc(S["c_vhalo"], 1)
            dve.wait_ge(S["ld_small"], 16 * NSMALL)
            dve.tensor_scalar(ag_b[:, :], ag_b[:, :], ALPHA, None, ALU.mult).then_inc(S["c_fold"], 1)
            dve.scalar_tensor_tensor(ab_b[:, :], ab_b[:, :], ALPHA, xb[:, :], ALU.mult, ALU.add)\
               .then_inc(S["c_fold"], 1)
            dve.wait_ge(S["c_halo"], 2)
            ln1(0, 0)
            ln1(0, 1)
            for j in range(TT):
                if j >= 2:
                    ln1(0, j)
                for n in ((0, 1), (2, 3), (4,), ())[j]:
                    tile_rest(n)
                xT_rest(0, j)
            dve.wait_ge(S["cols_in"], 1)
            chunk(0, False, True)
            with dve.Fori(1, NCH - 1) as c:
                chunk(c, True, True)
            c = NCH - 1
            chunk(c, True, False)
            for i in range(8):
                out_evac(c, i)
                if i % 2:
                    ln2(c, i // 2)

            count = [0]

            def step(m, also=None):
                count[0] += 1
                m.then_inc(S["rt_st"], 1)
                dve.wait_ge(S["rt_st"], count[0])

            def flat(t):
                return t.rearrange("p e t -> p (e t)")

            def bc(t, axis, shape):
                return t.unsqueeze(axis).broadcast_to(shape)

            G, E = r_G, r_E
            dve.wait_ge(S["lg_ready"], NT)
            dve.wait_ge(S["c_tri"], 4)
            step(dve.tensor_tensor(logits[:, :, :], logits[:, :, :], bc(br_b[:, :], 1, [P, NT, NR]), ALU.add))
            step(dve.tensor_reduce(r_gmax, G, AXX, ALU.max))
            step(dve.tensor_tensor(r_gd, G, bc(r_gmax, 2, [P, NT, NG]), ALU.subtract))
            step(dve.tensor_scalar(r_gk, r_gd, 0.0, None, ALU.is_ge))
            step(dve.tensor_tensor(r_gk, r_gk, bc(rev[:, EG - NG:EG], 1, [P, NT, NG]), ALU.mult))
            step(dve.tensor_reduce(r_gmax, r_gk, AXX, ALU.max))
            step(dve.tensor_tensor(r_hg, r_gk, bc(r_gmax, 2, [P, NT, NG]), ALU.is_equal))
            step(dve.tensor_tensor(r_sel, E, bc(r_hg, 3, [P, NT, NG, EG]), ALU.mult))
            step(dve.tensor_reduce(r_es, r_sel.rearrange("p t g e -> p t e g"), AXX, ALU.add))
            step(dve.tensor_reduce(r_m1, r_es, AXX, ALU.max))

            def first_of(vals, top, hot):
                step(dve.tensor_tensor(r_k8, vals, bc(top, 2, [P, NT, EG]), ALU.is_ge))
                step(dve.tensor_tensor(r_k8, r_k8, bc(rev[:, :], 1, [P, NT, EG]), ALU.mult))
                step(dve.tensor_reduce(r_kmax, r_k8, AXX, ALU.max))
                step(dve.tensor_tensor(hot, r_k8, bc(r_kmax, 2, [P, NT, EG]), ALU.is_equal))

            first_of(r_es, r_m1, r_h1)
            step(dve.scalar_tensor_tensor(r_e2, r_h1, NEG, r_es, ALU.mult, ALU.add))
            step(dve.tensor_reduce(r_m2, r_e2, AXX, ALU.max))
            first_of(r_e2, r_m2, r_h2)
            step(dve.tensor_tensor(r_ed, r_m2, r_m1, ALU.subtract))
            assert count[0] == RT_EXP_E, count[0]
            for hot8, hot in ((r_h1, r_hot1), (r_h2, r_hot2)):
                step(dve.tensor_tensor(hot, bc(r_hg, 3, [P, NT, NG, EG]), bc(hot8, 2, [P, NT, NG, EG]), ALU.mult))
            hot_all = mixc[:, 0, :]
            dve.tensor_tensor(hot_all, flat4(r_hot1), flat4(r_hot2), ALU.add).then_inc(S["r_hot"], 1)
            dve.wait_ge(S["rk_exp"], 2)
            step(dve.tensor_reduce(r_sum, r_eg, AXX, ALU.add))
            step(dve.tensor_scalar(r_one, r_ee, 1.0, None, ALU.add))
            step(dve.tensor_tensor(r_sum, r_sum, r_one, ALU.mult))
            step(dve.reciprocal(gate[:, 0, :], r_sum))
            step(dve.tensor_tensor(gate[:, 1, :], gate[:, 0, :], r_ee, ALU.mult))
            dve.wait_ge(S["rk_done"], 2)
            tot = PR[1][:, :].rearrange("p (t e) -> p t e", e=NE)
            step(dve.memset(r_z, 0.0))
            step(dve.tensor_copy(r_tot, tot.rearrange("p t e -> p e t")))
            step(dve.tensor_tensor_scan(flat(r_inc), flat(r_tot), flat(r_z), 0.0, ALU.add, ALU.add))
            step(dve.tensor_tensor(r_pre, r_inc, r_tot, ALU.subtract))
            step(dve.tensor_tensor(r_cnt, r_inc[:, :, NT - 1], r_pre[:, :, 0], ALU.subtract))
            step(dve.tensor_tensor(r_cmp, bc(r_cnt, 2, [P, NE, NT - 1]), bc(thr[:, :], 1, [P, NE, NT - 1]), ALU.is_gt))
            step(dve.tensor_reduce(r_nb, r_cmp, AXX, ALU.add))
            step(dve.tensor_scalar(r_nb, r_nb, 1.0, None, ALU.add))
            step(dve.memset(r_zero, 0.0))
            step(dve.tensor_tensor_scan(r_end, r_nb, r_zero, 0.0, ALU.add, ALU.add))
            step(dve.tensor_tensor(r_beg, r_end, r_nb, ALU.subtract))
            step(dve.scalar_tensor_tensor(r_shift, r_beg, float(P), r_pre[:, :, 0], ALU.mult, ALU.subtract))
            rk = PR[0][:, :].rearrange("p (t e) -> p t e", e=NE)
            step(dve.tensor_tensor(r_rank, rk, r_pre.rearrange("p e t -> p t e"), ALU.add))
            step(dve.tensor_tensor(r_blkrank, r_rank, bc(r_shift, 1, [P, NT, NE]), ALU.add))
            for k, hot in enumerate((r_hot1, r_hot2)):
                step(dve.tensor_tensor(r_tmp, hot.rearrange("p t g e -> p t (g e)"), r_blkrank, ALU.mult))
                step(dve.tensor_reduce(r_hi[:, k, :], r_tmp, AXX, ALU.add))
            step(dve.tensor_scalar(r_lo, r_hi, 1.0 / P, -(P / 2 - 0.5) / P, ALU.mult, ALU.add))
            step(dve.tensor_scalar(r_lo, r_lo, 1.5 * 2.0 ** 23, None, ALU.add))
            step(dve.tensor_scalar(r_blk, r_lo, -1.5 * 2.0 ** 23, None, ALU.add))
            step(dve.scalar_tensor_tensor(r_lo, r_blk, -float(P), r_hi, ALU.mult, ALU.add))
            dve.wait_ge(S["r_iota"], 2)

            def one_hot_places(k):
                return dve.tensor_tensor(r_ohl[:, k], bc(r_iota, 1, [P, NT, P]), bc(r_lo[:, k, :], 2, [P, NT, P]),
                                         ALU.is_equal)

            for k in (1, 0):
                dve.tensor_tensor(r_ohb[:, k], bc(r_iota[:, 0:MAXB], 1, [P, NT, MAXB]),
                                  bc(r_blk[:, k, :], 2, [P, NT, MAXB]), ALU.is_equal).then_inc(S["r_place"], 2 if k else 1)
            one_hot_places(0)
            dve.wait_ge(S["r_place"], 3)
            dve.tensor_tensor(r_ohb[:, 0], r_ohb[:, 0], bc(r_tok, 2, [P, NT, MAXB]), ALU.mult).then_inc(S["r_ohd"], 1)
            one_hot_places(1).then_inc(S["r_ohd"], 1)
            step(dve.tensor_copy(blk_i[0:1, 0:NE], r_nb[0:1, :]))
            step(dve.tensor_copy(blk_i[0:1, NE:2 * NE], r_beg[0:1, :]))
            step(dve.tensor_copy(blk_i[0:1, 3 * NE:3 * NE + 1], r_end[0:1, NE - 1:NE]))
            dve.tensor_copy(blk_i[0:1, 2 * NE:3 * NE], r_pre[0:1, :, 0]).then_inc(S["r_blk"], 1)
            for k, hot in enumerate((r_hot1, r_hot2)):
                step(dve.tensor_tensor(r_tmp, hot.rearrange("p t g e -> p t (g e)"), r_rank, ALU.mult))
                step(dve.tensor_reduce(r_pos, r_tmp, AXX, ALU.add))
                m = dve.tensor_copy(pos_u[:, k, :], r_pos)
                if k == 0:
                    step(m)
                else:
                    m.then_inc(S["r_idx"], 1)
            dve.memset(tab[:, MAXB:MAXB + 2], 0)
            dve.wait_ge(S["r_tabd"], 1)
            dve.tensor_copy(tab[:, 0:MAXB], PR[2][:, 0:MAXB]).then_inc(S["r_tab"], 1)

            dve.sem_inc(S["yb_free"], 1)

            def xe_rest(g):
                for h in range(2):
                    dve.wait_ge(S["xeh_ready"], g * 2 + 1 + h)
                    dve.tensor_tensor(xel[:, 4 * h:4 * h + 4, :], TP[h][:, :].rearrange("p (k n) -> p k n", k=4),
                                      f32(xeh[:, 4 * h:4 * h + 4, :]), ALU.subtract).then_inc(S["xel_ready"], 1)

            def w13_rest(e, s, w, q0=0, q1=4):
                for q in range(q0, q1):
                    dve.wait_ge(S["w3_hi" if w else "w1_hi"], 4 * e + q + 1)
                    k2 = slice(2 * q, 2 * q + 2)
                    dve.tensor_tensor(wl[s][w][:, k2, :], we[s][w][:, k2, :], f32(wh13[s][w][:, k2, :]), ALU.subtract)\
                       .then_inc(S["w3_lo" if w else "w1_lo"], 1)

            w13_rest(0, 0, 0)
            w13_rest(0, 0, 1)
            xe_rest(0)

            def expert_dve(i, s, has_next):
                e = 2 * i + s
                nb, g0, s0 = expert(dve, e)

                def block_dve(g, first):
                    for h in range(2):
                        if first and has_next:
                            w13_rest(e + 1, 1 - s, 0, 2 * h, 2 * h + 2)
                        n2 = slice(2 * h * P, 2 * (h + 1) * P)
                        if h == 0:
                            dve.wait_ge(S["sl_ready"], g + 1)
                        dve.wait_ge(S["up_done"], g * 2 + h + 1)
                        dve.tensor_tensor(sl[:, n2], sl[:, n2], (PR[1], SB)[h][:, 0:2 * P], ALU.mult)\
                           .then_inc(S["hm_ready"], 1)
                    for h in range(2):
                        dve.wait_ge(S["heh_ready"], g * 2 + h + 1)
                        dve.tensor_tensor(hel[:, 2 * h:2 * h + 2, :],
                                          HT[h][:, 0:2 * P].rearrange("p (f n) -> p f n", f=2),
                                          f32(heh[:, 2 * h:2 * h + 2, :]), ALU.subtract).then_inc(S["h_ready"], 1)
                    xe_rest(g + 1)
                    if first and has_next:
                        w13_rest(e + 1, 1 - s, 1)
                    dve.wait_ge(S["dn_done"], g + 1)
                    dve.wait_ge(S["ys_out"], g * 16 + 16)
                    dve.tensor_copy(ye[:, 512:1024], PR[3][:, :]).then_inc(S["yb_free"], 1)

                for q in range(KE // 2, KE):
                    dve.wait_ge(S["w2_hi"], KE * e + q + 1)
                    dve.tensor_tensor(wl[s][2][:, q, :], we[s][2][:, q, :], f32(wh2[:, q, :]), ALU.subtract)\
                       .then_inc(S["w2_lo2"], 1)
                block_dve(g0, True)
                with dve.If(nb > 1):
                    with dve.Fori(1, nb) as b:
                        block_dve(g0 + b, False)

            with dve.Fori(0, NE // 2 - 1) as i:
                for s in range(2):
                    expert_dve(i, s, True)
            for s in range(2):
                expert_dve(NE // 2 - 1, s, s == 0)

            dve.wait_ge(S["ld_lnf"], 32)
            def gain4(t, s):
                dve.wait_ge(S["f_n"], t + 1)
                dve.tensor_tensor(x2r[:, s, :], x2r[:, s, :], lnf[:, 0, :], ALU.mult).then_inc(S["f_g"], 1)

            with dve.Fori(0, NT // NY) as i:
                for s in range(NY):
                    t = NY * i + s
                    row = x2r[:, s, :]
                    dve.wait_ge(x2r_in[s], i * 16 + 16)
                    dve.wait_ge(S["f_a"], t + 1)
                    dve.scalar_tensor_tensor(row, row, ALPHA, ya[:, s, :], ALU.mult, ALU.add)\
                       .then_inc(S["f_st"], 1)
                    dve.wait_ge(S["f_st"], t * 5 + 1)
                    dve.scalar_tensor_tensor(row, yb[:, s, :], gate[:, 1, bass.ds(t, 1)], row,
                                             ALU.mult, ALU.add).then_inc(S["f_st"], 1)
                    dve.wait_ge(S["f_st"], t * 5 + 2)
                    for h in range(2):
                        dve.bn_stats(bst[:, s % 2, h, :], row[:, h * 512:(h + 1) * 512]).then_inc(S["f_st"], 1)
                    wait_apart(dve, S["f_st"], t * 5 + 4)
                    dve.bn_aggr(mv[:, s % 2, :], bst[:, s % 2, :, :].rearrange("p h s -> p (h s)"))\
                       .then_inc(S["f_st"], 1)
                    dve.wait_ge(S["f_st"], t * 5 + 5)
                    dve.tensor_scalar(nm[:, s:s + 1], mv[:, s % 2, 0:1], -1.0, None, ALU.mult)
                    dve.tensor_scalar(ve4[:, s:s + 1], mv[:, s % 2, 1:2], EPS, None, ALU.add).then_inc(S["f_var"], 1)
                    if s:
                        gain4(t - 1, s - 1)
                gain4(NY * i + NY - 1, NY - 1)

    return nc


_INS = ['x', 'ln_in_g', 'ln_in_b', 'w_in', 'b_in', 'w_dw', 'ln_conv_g', 'ln_conv_b', 'sinks', 'w_out', 'b_out',
        'ln_mix_g', 'ln_mix_b', 'w_router_group', 'b_router_group', 'w_router_expert', 'b_router_expert',
        'w1', 'w3', 'w2', 'ln_ffn_g', 'ln_ffn_b']
_OUTS = [((1, SEQ, D), 'float32')]


def kernel(**inputs):
    import numpy as _np
    import concourse.bacc as _bacc
    from concourse import mybir as _mybir
    from concourse.bass_utils import run_bass_kernel_spmd as _run

    nc = _bacc.Bacc("TRN2", target_bir_lowering=False, num_devices=1)
    arrays, args = {}, []
    for name in _INS:
        a = _np.ascontiguousarray(inputs[name])
        arrays[f"in_{name}_dram"] = a
        args.append(nc.dram_tensor(f"in_{name}_dram", a.shape, _mybir.dt.from_np(a.dtype), kind="ExternalInput").ap())
    for i, (shape, dtype) in enumerate(_OUTS):
        dt = _mybir.dt.from_np(_np.dtype(dtype))
        args.append(nc.dram_tensor(f"out_{i}_dram", shape, dt, kind="ExternalOutput").ap())
    build(nc, *args)
    r = _run(nc, [arrays], core_ids=[0])
    return r.results[0]["out_0_dram"]
```
